# Optimizing a Trainium2 kernel written in Bass

```python
import math
import jax, jax.numpy as jnp
from jax import lax
import numpy as np

D_MODEL = 2048
BATCH = 1
SEQ = 256
DEPTH = 1

MLA_HEADS = 8
MLA_Q_RANK = 768
MLA_KV_RANK = 512
MLA_NOPE = 128
MLA_ROPE = 64
MLA_V = 128
ROPE_THETA = 10000.0
Q_BLOCK = 128
NSA_HEADS = 8
NSA_GROUPS = 2
NSA_HPG = NSA_HEADS // NSA_GROUPS
NSA_DK = 192
NSA_DV = 128
CMP_LEN = 32
CMP_STRIDE = 16
CMP_HIDDEN = 256
SLC_LEN = 64
SLC_TOPN = 16
WINDOW = 512
N_BRANCH = 3
NSA_Q_BLOCK = 64
REL_BUCKETS = 32
REL_MAX_DIST = 128
D_FF = 5632
EPS = 1e-6

MIX_WIDTH = MLA_HEADS * MLA_V + NSA_HEADS * NSA_DV
IN_SPLITS = (
    MLA_Q_RANK,
    MLA_KV_RANK,
    MLA_ROPE,
    NSA_HEADS * NSA_DK,
    N_BRANCH * NSA_GROUPS * NSA_DK,
    N_BRANCH * NSA_GROUPS * NSA_DV,
    NSA_HEADS * N_BRANCH,
)
D_IN = sum(IN_SPLITS)

kernel_name = 'hybrid_mla_nsa_macaron_adaln'

def rms_norm(x, g):
    x32 = x.astype(jnp.float32)
    y = x32 * lax.rsqrt(jnp.mean(x32 * x32, axis=-1, keepdims=True) + EPS)
    return (y * g.astype(jnp.float32)).astype(x.dtype)

def modulate(h, shift, scale):
    return h * (1.0 + scale[:, None, :]) + shift[:, None, :]

def swiglu(h, w_gate, w_up, w_down):
    return (jax.nn.silu(h @ w_gate) * (h @ w_up)) @ w_down

def split_cols(h, sizes):
    return jnp.split(h, np.cumsum(sizes)[:-1].tolist(), axis=-1)

def rope(t, pos):
    d = t.shape[-1]
    inv = ROPE_THETA ** (-jnp.arange(0, d, 2, dtype=jnp.float32) / d)
    ang = pos.astype(jnp.float32)[:, None] * inv[None, :]
    cos = jnp.cos(ang)[None, :, None, :].astype(t.dtype)
    sin = jnp.sin(ang)[None, :, None, :].astype(t.dtype)
    t1, t2 = t[..., : d // 2], t[..., d // 2:]
    return jnp.concatenate([t1 * cos - t2 * sin, t1 * sin + t2 * cos], axis=-1)

def masked_softmax(logits, mask):
    logits = jnp.where(mask, logits.astype(jnp.float32), -jnp.inf)
    m = jnp.max(logits, axis=-1, keepdims=True)
    m = jnp.where(jnp.isfinite(m), m, 0.0)
    p = jnp.exp(logits - m)
    return p / jnp.maximum(jnp.sum(p, axis=-1, keepdims=True), 1e-30)

def t5_bucket(dist):
    n = jnp.maximum(dist, 0)
    max_exact = REL_BUCKETS // 2
    nf = jnp.maximum(n, 1).astype(jnp.float32)
    large = max_exact + (jnp.log(nf / max_exact) / math.log(REL_MAX_DIST / max_exact)
                         * (REL_BUCKETS - max_exact)).astype(jnp.int32)
    large = jnp.minimum(large, REL_BUCKETS - 1)
    return jnp.where(n < max_exact, n, large)

def mla_group(cq, ckv, kr, pos, q_norm, w_uq, kv_norm, w_ukv):
    B, S, _ = cq.shape
    dqk = MLA_NOPE + MLA_ROPE
    q = (rms_norm(cq, q_norm) @ w_uq).reshape(B, S, MLA_HEADS, dqk)
    q = jnp.concatenate([q[..., :MLA_NOPE], rope(q[..., MLA_NOPE:], pos)], axis=-1)
    kv = (rms_norm(ckv, kv_norm) @ w_ukv).reshape(B, S, MLA_HEADS, MLA_NOPE + MLA_V)
    k_nope, v = kv[..., :MLA_NOPE], kv[..., MLA_NOPE:]
    k_rope = rope(kr[:, :, None, :], pos)
    k = jnp.concatenate([k_nope, jnp.broadcast_to(k_rope, (B, S, MLA_HEADS, MLA_ROPE))], axis=-1)
    scale = dqk ** -0.5
    nb = S // Q_BLOCK
    qb = q.reshape(B, nb, Q_BLOCK, MLA_HEADS, dqk).transpose(1, 0, 2, 3, 4)

    def block(args):
        qi, i = args
        tq = i * Q_BLOCK + jnp.arange(Q_BLOCK)
        s = jnp.einsum('bqhd,bkhd->bhqk', qi, k) * scale
        p = masked_softmax(s, pos[None, :] <= tq[:, None])
        return jnp.einsum('bhqk,bkhd->bqhd', p.astype(v.dtype), v)

    o = lax.map(block, (qb, jnp.arange(nb)))
    return o.transpose(1, 0, 2, 3, 4).reshape(B, S, MLA_HEADS * MLA_V)

def compress(t, pe, w1, w2):
    B, S, G, d = t.shape
    n_cmp = (S - CMP_LEN) // CMP_STRIDE + 1
    idx = jnp.arange(n_cmp)[:, None] * CMP_STRIDE + jnp.arange(CMP_LEN)[None, :]
    blocks = t[:, idx] + pe[None, None, :, None, :]
    flat = blocks.transpose(0, 1, 3, 2, 4).reshape(B, n_cmp, G, CMP_LEN * d)
    return jax.nn.silu(flat @ w1) @ w2

def nsa_group(q, k3, v3, gates, pe_cmp_k, w_cmp_k1, w_cmp_k2, pe_cmp_v, w_cmp_v1, w_cmp_v2, rel_bias):
    B, S = q.shape[:2]
    G, HPG, NQ = NSA_GROUPS, NSA_HPG, NSA_Q_BLOCK
    kc = compress(k3[:, :, 0], pe_cmp_k, w_cmp_k1, w_cmp_k2)
    vc = compress(v3[:, :, 0], pe_cmp_v, w_cmp_v1, w_cmp_v2)
    n_cmp = kc.shape[1]
    n_slc = S // SLC_LEN
    n_top = min(SLC_TOPN, n_slc)
    c_start = jnp.arange(n_cmp) * CMP_STRIDE
    cmp_end = c_start + CMP_LEN - 1
    s_start = jnp.arange(n_slc) * SLC_LEN
    j_ids = jnp.arange(n_slc)
    overlap = ((c_start[:, None] < s_start[None, :] + SLC_LEN)
               & (c_start[:, None] + CMP_LEN > s_start[None, :])).astype(jnp.float32)
    ks_blk = k3[:, :, 1].reshape(B, n_slc, SLC_LEN, G, NSA_DK).transpose(0, 3, 1, 2, 4)
    vs_blk = v3[:, :, 1].reshape(B, n_slc, SLC_LEN, G, NSA_DV).transpose(0, 3, 1, 2, 4)
    kw_pad = jnp.pad(k3[:, :, 2], ((0, 0), (WINDOW, 0), (0, 0), (0, 0)))
    vw_pad = jnp.pad(v3[:, :, 2], ((0, 0), (WINDOW, 0), (0, 0), (0, 0)))
    rb_group = rel_bias.reshape(REL_BUCKETS, G, HPG)
    scale = NSA_DK ** -0.5
    nb = S // NQ
    qb = q.reshape(B, nb, NQ, G, HPG, NSA_DK).transpose(1, 0, 2, 3, 4, 5)
    gb = gates.reshape(B, nb, NQ, G, HPG, N_BRANCH).transpose(1, 0, 2, 3, 4, 5)
    b_idx = jnp.arange(B)[:, None, None, None]
    g_idx = jnp.arange(G)[None, None, :, None]

    def head_bias(bucket):
        nq, nk = bucket.shape
        return rel_bias[bucket].reshape(nq, nk, G, HPG).transpose(2, 3, 0, 1)

    def step(args):
        qi, gi, i = args
        tq = i * NQ + jnp.arange(NQ)
        s_c = (jnp.einsum('bqghd,bngd->bghqn', qi, kc) * scale
               + head_bias(t5_bucket(tq[:, None] - cmp_end[None, :])))
        p_c = masked_softmax(s_c, cmp_end[None, :] <= tq[:, None])
        o_c = jnp.einsum('bghqn,bngd->bqghd', p_c.astype(vc.dtype), vc)
        imp = jnp.einsum('bghqn,nj->bqgj', p_c, overlap)
        valid = (s_start[None, :] <= tq[:, None])[None, :, None, :]
        cur = (tq // SLC_LEN)[:, None]
        forced = ((j_ids[None, :] == 0)
                  | ((j_ids[None, :] <= cur) & (j_ids[None, :] >= cur - 1)))[None, :, None, :]
        score = jnp.where(valid, jnp.where(forced, jnp.inf, imp), -jnp.inf)
        top_val, top_idx = lax.top_k(score, n_top)
        k_sel = ks_blk[b_idx, g_idx, top_idx].reshape(B, NQ, G, n_top * SLC_LEN, NSA_DK)
        v_sel = vs_blk[b_idx, g_idx, top_idx].reshape(B, NQ, G, n_top * SLC_LEN, NSA_DV)
        tok = (top_idx[..., None] * SLC_LEN + jnp.arange(SLC_LEN)).reshape(B, NQ, G, n_top * SLC_LEN)
        tq_b = tq[None, :, None, None]
        m_s = jnp.repeat(top_val > -jnp.inf, SLC_LEN, axis=-1) & (tok <= tq_b)
        bias_s = rb_group[t5_bucket(tq_b - tok), g_idx].transpose(0, 2, 4, 1, 3)
        s_s = jnp.einsum('bqghd,bqgkd->bghqk', qi, k_sel) * scale + bias_s
        p_s = masked_softmax(s_s, m_s.transpose(0, 2, 1, 3)[:, :, None])
        o_s = jnp.einsum('bghqk,bqgkd->bqghd', p_s.astype(v_sel.dtype), v_sel)
        kw = lax.dynamic_slice_in_dim(kw_pad, i * NQ, WINDOW + NQ, axis=1)
        vw = lax.dynamic_slice_in_dim(vw_pad, i * NQ, WINDOW + NQ, axis=1)
        kpos = i * NQ - WINDOW + jnp.arange(WINDOW + NQ)
        dist = tq[:, None] - kpos[None, :]
        m_w = (kpos[None, :] >= 0) & (dist >= 0) & (dist < WINDOW)
        s_w = jnp.einsum('bqghd,bkgd->bghqk', qi, kw) * scale + head_bias(t5_bucket(dist))
        p_w = masked_softmax(s_w, m_w)
        o_w = jnp.einsum('bghqk,bkgd->bqghd', p_w.astype(vw.dtype), vw)
        o = gi[..., 0:1] * o_c + gi[..., 1:2] * o_s + gi[..., 2:3] * o_w
        return o.reshape(B, NQ, NSA_HEADS * NSA_DV)

    o = lax.map(step, (qb, gb, jnp.arange(nb)))
    return o.transpose(1, 0, 2, 3).reshape(B, S, NSA_HEADS * NSA_DV)

def token_mixing(h, w_in, mla_q_norm, w_uq, mla_kv_norm, w_ukv, pe_cmp_k, w_cmp_k1, w_cmp_k2,
                 pe_cmp_v, w_cmp_v1, w_cmp_v2, rel_bias, w_out):
    B, S, _ = h.shape
    cq, ckv, kr, q_n, k_n, v_n, g_n = split_cols(h @ w_in, IN_SPLITS)
    pos = jnp.arange(S)
    o_mla = mla_group(cq, ckv, kr, pos, mla_q_norm, w_uq, mla_kv_norm, w_ukv)
    o_nsa = nsa_group(q_n.reshape(B, S, NSA_HEADS, NSA_DK),
                      k_n.reshape(B, S, N_BRANCH, NSA_GROUPS, NSA_DK),
                      v_n.reshape(B, S, N_BRANCH, NSA_GROUPS, NSA_DV),
                      jax.nn.sigmoid(g_n.reshape(B, S, NSA_HEADS, N_BRANCH)),
                      pe_cmp_k, w_cmp_k1, w_cmp_k2, pe_cmp_v, w_cmp_v1, w_cmp_v2, rel_bias)
    return jnp.concatenate([o_mla, o_nsa], axis=-1) @ w_out

def setup_inputs(seed: int = 0) -> dict:
    key = jax.random.key(seed)
    keys = iter(jax.random.split(key, 40))
    L, D = DEPTH, D_MODEL

    def nrm(shape, s=1.0):
        return jax.random.normal(next(keys), shape, jnp.float32) * s

    def w(shape, fan_in, s=1.0):
        return nrm(shape, s * fan_in ** -0.5)

    def gain(shape):
        return 1.0 + nrm(shape, 0.02)

    return {
        'x': nrm((BATCH, SEQ, D)),
        'c': nrm((BATCH, D)),
        'w_ada': w((L, D, 9 * D), D, 0.5),
        'b_ada': nrm((L, 9 * D), 0.02),
        'norm_ffn1': gain((L, D)),
        'w1_gate': w((L, D, D_FF), D),
        'w1_up': w((L, D, D_FF), D),
        'w1_down': w((L, D_FF, D), D_FF),
        'norm_mix': gain((L, D)),
        'w_in': w((L, D, D_IN), D),
        'mla_q_norm': gain((L, MLA_Q_RANK)),
        'w_uq': w((L, MLA_Q_RANK, MLA_HEADS * (MLA_NOPE + MLA_ROPE)), MLA_Q_RANK),
        'mla_kv_norm': gain((L, MLA_KV_RANK)),
        'w_ukv': w((L, MLA_KV_RANK, MLA_HEADS * (MLA_NOPE + MLA_V)), MLA_KV_RANK),
        'pe_cmp_k': nrm((L, CMP_LEN, NSA_DK), 0.1),
        'w_cmp_k1': w((L, CMP_LEN * NSA_DK, CMP_HIDDEN), CMP_LEN * NSA_DK),
        'w_cmp_k2': w((L, CMP_HIDDEN, NSA_DK), CMP_HIDDEN),
        'pe_cmp_v': nrm((L, CMP_LEN, NSA_DV), 0.1),
        'w_cmp_v1': w((L, CMP_LEN * NSA_DV, CMP_HIDDEN), CMP_LEN * NSA_DV),
        'w_cmp_v2': w((L, CMP_HIDDEN, NSA_DV), CMP_HIDDEN),
        'rel_bias': nrm((REL_BUCKETS, NSA_HEADS), 0.1),
        'w_out': w((L, MIX_WIDTH, D), MIX_WIDTH),
        'norm_ffn2': gain((L, D)),
        'w2_gate': w((L, D, D_FF), D),
        'w2_up': w((L, D, D_FF), D),
        'w2_down': w((L, D_FF, D), D_FF),
        'norm_final': gain((D,)),
    }

def reference(x, c, w_ada, b_ada, norm_ffn1, w1_gate, w1_up, w1_down, norm_mix, w_in,
              mla_q_norm, w_uq, mla_kv_norm, w_ukv, pe_cmp_k, w_cmp_k1, w_cmp_k2,
              pe_cmp_v, w_cmp_v1, w_cmp_v2, rel_bias, w_out, norm_ffn2, w2_gate, w2_up,
              w2_down, norm_final):
    for l in range(DEPTH):
        mod = jax.nn.silu(c) @ w_ada[l] + b_ada[l]
        sh1, sc1, g1, sh2, sc2, g2, sh3, sc3, g3 = jnp.split(mod, 9, axis=-1)
        h = modulate(rms_norm(x, norm_ffn1[l]), sh1, sc1)
        x = x + 0.5 * g1[:, None, :] * swiglu(h, w1_gate[l], w1_up[l], w1_down[l])
        h = modulate(rms_norm(x, norm_mix[l]), sh2, sc2)
        x = x + g2[:, None, :] * token_mixing(h, w_in[l], mla_q_norm[l], w_uq[l], mla_kv_norm[l],
                                              w_ukv[l], pe_cmp_k[l], w_cmp_k1[l], w_cmp_k2[l],
                                              pe_cmp_v[l], w_cmp_v1[l], w_cmp_v2[l], rel_bias,
                                              w_out[l])
        h = modulate(rms_norm(x, norm_ffn2[l]), sh3, sc3)
        x = x + 0.5 * g3[:, None, :] * swiglu(h, w2_gate[l], w2_up[l], w2_down[l])
    return rms_norm(x, norm_final)


_drawn_inputs = setup_inputs


def setup_inputs(seed=0):
    import zlib

    import numpy as np

    out = dict(_drawn_inputs(seed))
    spreads = {}
    factors = {'b_ada': 3.779,
     'norm_ffn1': 8.0,
     'norm_mix': 8.0,
     'mla_q_norm': 8.0,
     'mla_kv_norm': 8.0,
     'pe_cmp_k': 8.0,
     'w_cmp_k1': 3.644,
     'w_cmp_k2': 3.633,
     'pe_cmp_v': 40.092,
     'rel_bias': 24.502,
     'norm_ffn2': 23.001,
     'norm_final': 8.504}
    for name, (base, spread) in spreads.items():
        noise = np.random.default_rng([zlib.crc32(name.encode()), seed]).standard_normal(out[name].shape)
        drawn = base * np.exp(spread * noise) if base else spread * noise
        out[name] = __import__('jax').numpy.asarray(drawn.astype(out[name].dtype))
    for name, factor in factors.items():
        out[name] = (out[name] * factor).astype(out[name].dtype)
    return out
```

```python
from contextlib import ExitStack

import numpy as np

import concourse.bass as bass
from concourse import mybir

P = 128
F32 = mybir.dt.float32
F32R = mybir.dt.float32r
ALU = mybir.AluOpType
ACT = mybir.ActivationFunctionType
AX = mybir.AxisListType

D, SEQ, FF = 2048, 256, 5632
TT = SEQ // P
KD = D // P
KF = FF // P
CW = 512
Q_RANK, KV_RANK, ROPE, NOPE, VD = 768, 512, 64, 128, 128
HEADS = 8
DK = NOPE + ROPE
GROUPS, HPG = 2, 4
CMP_LEN, CMP_STRIDE, CMP_HID = 32, 16, 256
N_CMP = (SEQ - CMP_LEN) // CMP_STRIDE + 1
BUCKETS, MAX_DIST = 32, 128
EPS = 1e-6
SCALE = float(DK) ** -0.5
MASKED = -1e30
CMP_IN_REACH = [min(N_CMP, ((t + 1) * P - CMP_LEN) // CMP_STRIDE + 1) for t in range(TT)]
C_Q, C_KV, C_KR = 0, Q_RANK, Q_RANK + KV_RANK
C_NQ = C_KR + ROPE
C_NK = C_NQ + HEADS * DK
C_NV = C_NK + 3 * GROUPS * DK
C_NG = C_NV + 3 * GROUPS * VD
D_IN = C_NG + HEADS * 3
LAST_W = D_IN - (D_IN // CW) * CW

RING = 4
ADA_CHUNKS = 9 * D // CW
START_CHUNKS = 8
STAGES = {"gu0": (FF // CW, KD), "dn0": (D // CW, KF // 2), "win": (D_IN // CW + 1, KD // 2),
          "uq": (HEADS * DK // CW, Q_RANK // P // 2), "ukv": (HEADS * 2 * P // CW, KV_RANK // P // 2),
          "wout": (D // CW, KD // 2), "gu1": (FF // CW, KD), "dn1": (D // CW, KF // 2)}


def count_panels():
    table, uses, last, n = {}, [0] * RING, [None] * RING, 0
    for stage, (units, panels) in STAGES.items():
        for u in range(units):
            for j in range(panels):
                s = j % RING
                uses[s] += 1
                table[stage, u, j] = (n, uses[s], last[s])
                last[s] = n
                n += 1
    return table


def count_chunks():
    of, q = {("start", u): [(u, u % 2)] for u in range(START_CHUNKS)}, START_CHUNKS
    for stage, each in (("gu0", 1), ("dn0", 2), ("win", 1)):
        for u in range(STAGES[stage][0] - (stage == "win")):
            accs = [0] if stage == "gu0" else [0, 1] if stage == "dn0" else [u % 2]
            of[stage, u] = [(q + e, accs[e]) for e in range(each)]
            q += each
    assert q == ADA_CHUNKS
    before, uses, last = {}, [0, 0], [None, None]
    for chunks in of.values():
        for q, a in chunks:
            before[q] = (uses[a], last[a])
            uses[a] += 1
            last[a] = q
    return of, before


PANELS = count_panels()
ADA_OF, ADA_BEFORE = count_chunks()


class Unit:

    def __init__(self, stage, first, i=None, step=1, times=1):
        self.stage, self.first, self.i, self.step, self.times = stage, first, i, step, times

    def at(self, f):
        v = [f(self.first + r * self.step) for r in range(self.times)]
        if self.i is None or self.times == 1:
            return v[0]
        by = v[1] - v[0]
        assert all(b - a == by for a, b in zip(v, v[1:])), (self.stage, v)
        return self.i * by + v[0]

    def done(self, j):
        return self.at(lambda u: PANELS[self.stage, u, j][0] + 1)

    def landed(self, j):
        return self.at(lambda u: 16 * PANELS[self.stage, u, j][1])

    def slot_free(self, j):
        if PANELS[self.stage, self.first, j][2] is None:
            return None
        return self.at(lambda u: PANELS[self.stage, u, j][2] + 1)


def units(eng, stage, first, last, step=1):
    times = (last - first) // step
    assert times * step == last - first
    with eng.Fori(0, times) as i:
        for e in range(step):
            yield Unit(stage, first + e, i, step, times)


def before(U):
    return Unit(U.stage, U.first - 1, U.i, U.step, U.times)


def part(U, ring, s):
    if U.stage == "win" and U.first == STAGES["win"][0] - 1:
        return ring[:, s, :].rearrange("p (k n) -> p k n", k=2)[:, :, 0:LAST_W]
    return ring[:, s, :]


def bucket_table():
    dist = SEQ - 1 - np.arange(384)
    n = np.maximum(dist, 0)
    exact = BUCKETS // 2
    nf = np.maximum(n, 1).astype(np.float32)
    large = exact + (np.log(nf / np.float32(exact)) / np.float32(np.log(MAX_DIST / exact))
                     * np.float32(BUCKETS - exact)).astype(np.int32)
    bucket = np.where(n < exact, n, np.minimum(large, BUCKETS - 1))
    table = np.zeros((BUCKETS + 1, 384), np.float32)
    table[bucket, np.arange(384)] = 1.0
    table[:, dist < 0] = 0.0
    table[BUCKETS, dist < 0] = MASKED
    return table


def rope_table():
    inv = np.float32(10000.0) ** (-np.arange(0, ROPE, 2, dtype=np.float32) / np.float32(ROPE))
    ang = np.arange(SEQ, dtype=np.float32)[:, None] * inv[None, :]
    both = np.stack([np.cos(ang), np.sin(ang)], 1).astype(np.float32)
    return np.ascontiguousarray(both.reshape(TT, P, 2, ROPE // 2).transpose(1, 0, 2, 3))


def decoder_layer(nc, x, c, w_ada, b_ada, norm_ffn1, w1_gate, w1_up, w1_down, norm_mix, w_in,
                  mla_q_norm, w_uq, mla_kv_norm, w_ukv, pe_cmp_k, w_cmp_k1, w_cmp_k2, pe_cmp_v,
                  w_cmp_v1, w_cmp_v2, rel_bias, w_out, norm_ffn2, w2_gate, w2_up, w2_down,
                  norm_final, out):
    ident_c = nc.inline_tensor(np.eye(P, dtype=np.float32), name="identity").ap()
    bucket_c = nc.inline_tensor(bucket_table(), name="bucket_one_hot").ap()
    rope_c = nc.inline_tensor(rope_table(), name="rope_cos_sin").ap()
    bias_scratch = nc.dram_tensor("bias_by_distance", (HEADS + 1, P, 384), F32, kind="Internal")

    def tiles(w):
        return w.rearrange("(k p) n -> p k n", p=P)

    gate_w = [tiles(w1_gate[0]), tiles(w2_gate[0])]
    up_w = [tiles(w1_up[0]), tiles(w2_up[0])]
    down_w = [tiles(w1_down[0]), tiles(w2_down[0])]
    w_in_t, w_uq_t, w_ukv_t, w_out_t = tiles(w_in[0]), tiles(w_uq[0]), tiles(w_ukv[0]), tiles(w_out[0])
    w_ada_t = tiles(w_ada[0])
    x_t = x[0].rearrange("(t p) n -> p t n", p=P)
    out_t = out[0].rearrange("(t p) n -> p t n", p=P)

    with ExitStack() as ctx:
        def sb(name, shape, dt=F32, within=ctx):
            return within.enter_context(nc.sbuf_tensor(name, shape, dt))

        def sem(name):
            return ctx.enter_context(nc.semaphore(name))

        ident = sb("ident", [P, P])
        ones = sb("ones", [P, P])
        x_sb = sb("x_sb", [P, TT, D])
        raw = sb("raw", [P, RING, 2 * CW])
        w_hi = sb("w_hi", [P, RING, 2 * CW], F32R)
        w_lo = sb("w_lo", [P, RING, 2 * CW], F32R)
        ada_raw = sb("ada_raw", [P, RING, 2 * CW])
        mod_cols = sb("mod_cols", [P, 9 * KD])
        VROWS = {"ffn1": 0, "mix": 16, "ffn2": 32, "q": 48, "kv": 54, "c": 58}
        NV = 58 + KD
        v_cols = sb("v_cols", [P, NV])
        silu_c = sb("silu_c", [P, KD])
        scale_cols = sb("scale_cols", [P, KD])
        stat = sb("stat", [P, 6, 4])
        norm_tmp = sb("norm_tmp", [P, 2, CW])
        with ExitStack() as s:
            acc = sb("ada_acc", [P, 2, CW], within=s)
            b_row = sb("b_row", [P, 2, CW], within=s)
        with ExitStack() as s:
            rope_tmp = sb("rope_tmp", [P, 4, HEADS * ROPE // 2], within=s)
        small_hold = sb("small_hold", [P, 4, CW])
        with ExitStack() as s:
            act_sg = sb("silu_gate", [P, TT, CW], within=s)
        with ExitStack() as s:
            probs = sb("probs", [P, 2, 3 * P], within=s)
        sg_hold = sb("sg_hold", [P, TT, CW])
        with ExitStack() as s:
            hT_hi = sb("hT_hi", [P, KD, SEQ], F32R, within=s)
            hT_lo = sb("hT_lo", [P, KD, SEQ], F32R, within=s)
        with ExitStack() as s:
            gate_b = sb("gate_b", [P, D], within=s)
            final_b = sb("final_b", [P, D], within=s)
        with ExitStack() as s:
            with ExitStack() as s2:
                cqT = [sb(f"cqT_{n}", [P, 6, SEQ], F32R, within=s2) for n in ("hi", "lo")]
                ckvT = [sb(f"ckvT_{n}", [P, 4, SEQ], F32R, within=s2) for n in ("hi", "lo")]
            with ExitStack() as s2:
                kpe128 = sb("kpe128", [P, CMP_LEN, GROUPS * N_CMP], within=s2)
                kpe64 = sb("kpe64", [ROPE, CMP_LEN, GROUPS * N_CMP], within=s2)
                vpe = sb("vpe", [P, CMP_LEN, GROUPS * N_CMP], within=s2)
                v_cmp = sb("v_cmp", [P, GROUPS, HPG * VD], within=s2)
                hid = sb("hid", [GROUPS * N_CMP, 2, CMP_HID], within=s2)
                hidT = sb("hidT", [P, 4, GROUPS * N_CMP], within=s2)
                kc128 = sb("kc128", [P, GROUPS * N_CMP], within=s2)
                kc64 = sb("kc64", [ROPE, GROUPS * N_CMP], within=s2)
                w2v = sb("w2v", [P, 2, VD], within=s2)
                peT = sb("peT", [P, 3, CMP_LEN], within=s2)
            proj_in_hold = sb("proj_in_hold", [P, 20 * SEQ], within=s)
            bias = sb("bias_toeplitz", [P, HEADS + 1, SEQ], within=s)
            probsT = sb("probsT", [P, 2, 3 * P], within=s)
        h_hold = sb("h_hold", [P, 2 * KD * SEQ])
        with ExitStack() as s:
            act_hi = sb("actT_hi", [P, KF, SEQ], F32R, within=s)
            act_lo = sb("actT_lo", [P, KF, SEQ], F32R, within=s)
        with ExitStack() as s:
            xn = sb("x_normed", [P, TT, D], within=s)
            bucket_sb = sb("bucket_sb", [BUCKETS + 1, 384], within=s)
            rel_sb = sb("rel_sb", [BUCKETS + 1, HEADS + 1], within=s)
            rev_sb = sb("rev_sb", [HEADS + 1, 384], within=s)
            v_rows = sb("v_rows", [NV, P], within=s)
        with ExitStack() as s:
            proj = sb("proj", [P, TT, D_IN], within=s)
            q_mla = sb("q_mla", [P, TT, HEADS * DK], within=s)
            kv_mla = sb("kv_mla", [P, TT, HEADS * 2 * P], within=s)
            kT128 = sb("kT128", [P, 6, SEQ], within=s)
            kT64 = sb("kT64", [ROPE, 6, SEQ], within=s)
            qkT = sb("qkT", [P, 2, 2 * SEQ], within=s)
            qrT = sb("qrT", [ROPE, 2, SEQ], within=s)
            krT = sb("krT", [ROPE, SEQ], within=s)
            rope_sb = sb("rope_sb", [P, TT, 2, ROPE // 2], within=s)
            w2k = sb("w2k", [P, 2, DK], within=s)
            row_max = sb("row_max", [P, 24, 2], within=s)
            neg_max = sb("neg_max", [P, 24, 2], within=s)
            row_sum = sb("row_sum", [P, 24, 2], within=s)
        a_hold = sb("a_hold", [P, 2 * KF * SEQ])
        gates = sb("gates", [P, TT, HEADS * 3])
        coef = sb("coef", [P, 24, 2])
        cmp_stat = sb("cmp_stat", [P, 4, HEADS * TT])
        pe_sb = sb("pe_sb", [CMP_LEN, DK + VD])
        o_mla, o_nsa = proj[:, :, 0:HEADS * VD], q_mla[:, :, 0:HEADS * VD]

        ps = ctx.enter_context(nc.psum_tensor("ps", [P, 8, CW], F32))
        T_BANK, ADA_BANK, MISC_BANK = 4, 6, 7

        raw_landed = [sem(f"raw_landed{s}") for s in range(RING)]
        hi_done, lo_done, mm_done = sem("hi_done"), sem("lo_done"), sem("mm_done")
        ada_landed = [sem(f"ada_landed{s}") for s in range(RING)]
        b_landed = [sem(f"b_landed{s}") for s in range(2)]
        acc_step = sem("acc_step")
        acc_turned, mod_done = sem("acc_turned"), sem("mod_done")
        const_landed, x_landed, rel_landed = sem("const_landed"), sem("x_landed"), sem("rel_landed")
        rel_set = sem("rel_set")
        ones_set, rows_set = sem("ones_set"), sem("rows_set")
        v_turned, v_done, silu_c_done = sem("v_turned"), sem("v_done"), sem("silu_c_done")
        rev_mm, rev_done, rev_stored = sem("rev_mm"), sem("rev_done"), sem("rev_stored")
        dve_step, pool_step = sem("dve_step"), sem("pool_step")
        gu = [{n: sem(f"{n}{f}") for n in ("silu_done", "prod_done", "prod_turned", "actT_hi_done",
                                          "actT_lo_done")} for f in range(2)]
        nrm = {n: {m: sem(f"{m}_{n}") for m in ("squares", "mean", "root", "xn_done", "turned", "tmp_done",
                                               "T_hi_done", "T_lo_done")}
               for n in ("ffn1", "mix", "ffn2", "mla", "o", "final")}
        gat = [{n: sem(f"{n}{f}") for n in ("diag_done", "gate_mm", "gate_b_done")} for f in range(3)]
        res = {n: {m: sem(f"{m}_{n}") for m in ("bank_read", "x_added")} for n in ("dn0", "wout", "dn1")}
        copied = {n: sem(f"copied_{n}") for n in ("win", "uq", "ukv")}
        A = {n: sem(n) for n in ("bias_landed", "kr_turned", "kr_copied",
                                 "q_turned", "qk_copied", "qr_copied", "scored", "maxed", "neg_done", "exped",
                                 "p_turned", "pT_copied", "pv_done", "o_done",
                                 "k_turned", "kT_copied", "v_turned_c", "pe_turned", "pe_copied",
                                 "kpe_done", "cw_used", "hid_done", "hid_turned", "hidT_copied",
                                 "kc_mm", "kc_copied", "vc_zero", "vc_copied", "gates_exp",
                                 "gates_done", "cmp_scored", "cmp_ready", "cmp_exped", "cmp_coef",
                                 "cmp_turned", "cmp_copied", "cmp_pv", "cmp_o", "cmp_w_landed",
                                 "rope_landed")}
        final_done, final_b_landed, stored = sem("final_done"), sem("final_b_landed"), sem("stored")
        NORM_OF = {"gu0": "ffn1", "win": "mix", "gu1": "ffn2", "wout": "o"}
        ada_after_lo = {"gu0": 4, "dn0": 4, "win": 0}

        block = ctx.enter_context(nc.Block())

        @block.sync
        def _(sp):
            def load(U, j, src, width=CW):
                free = U.slot_free(j)
                if free is not None:
                    sp.wait_ge(lo_done, free)
                dst = raw[:, j % RING, :].rearrange("p (k n) -> p k n", k=2)[:, :, 0:width]
                sp.dma_start(dst, src).then_inc(raw_landed[j % RING], 16)

            def columns(w, k, U, width=CW):
                return w[:, k:k + 2, bass.ds(U.at(lambda u: u * CW), width)]

            def load_ada(U, e, p):
                q = U.at(lambda u: ADA_OF[U.stage, u][e][0])
                _, a = ADA_OF[U.stage, U.first][e]
                if p == 0:
                    if ADA_BEFORE[ADA_OF[U.stage, U.first][e][0]][1] is not None:
                        sp.wait_ge(acc_step, U.at(lambda u: 16 * ADA_BEFORE[ADA_OF[U.stage, u][e][0]][1] + 1))
                    else:
                        sp.wait_ge(rows_set, 1)
                    sp.dma_start(b_row[0:1, a, :], b_ada[0:1, bass.ds(q * CW, CW)]).then_inc(b_landed[a], 16)
                if not (U.stage == "start" and U.first == 0 and p < RING):
                    sp.wait_ge(acc_step, U.at(lambda u: 16 * ADA_OF[U.stage, u][e][0] + 2 * (p - RING + 1)))
                sp.dma_start(ada_raw[:, p % RING, :].rearrange("p (k n) -> p k n", k=2),
                             w_ada_t[:, 2 * p:2 * p + 2, bass.ds(q * CW, CW)]).then_inc(ada_landed[p % RING], 16)

            def load_unit(U, panel):
                chunks = ADA_OF.get((U.stage, U.first), [])
                for j in range(STAGES[U.stage][1]):
                    p = j - ada_after_lo.get(U.stage, 0)
                    if 0 <= p < 8 * len(chunks):
                        load_ada(U, p // 8, p % 8)
                    panel(U, j)

            def gate_up(f):
                def panel(U, j):
                    load(U, j, columns((gate_w, up_w)[j % 2][f], j // 2 * 2, U))
                return panel

            def rows_of(w, width=CW):
                return lambda U, j: load(U, j, columns(w, 2 * j, U, width), width)

            first = Unit("gu0", 0)
            load_ada(Unit("start", 0), 0, 0)
            for p in range(1, RING):
                load_ada(Unit("start", 0), 0, p)
            for j in range(RING):
                gate_up(0)(first, j)
            for p in range(RING, 8):
                load_ada(Unit("start", 0), 0, p)
            for p in range(8):
                load_ada(Unit("start", 1), 0, p)
            for U in units(sp, "start", 2, START_CHUNKS, 2):
                for p in range(8):
                    load_ada(U, 0, p)

            for j in range(RING, STAGES["gu0"][1]):
                p = j - ada_after_lo["gu0"]
                if 0 <= p < 8:
                    load_ada(first, 0, p)
                gate_up(0)(first, j)
            for U in units(sp, "gu0", 1, STAGES["gu0"][0]):
                load_unit(U, gate_up(0))
            load_unit(Unit("dn0", 0), rows_of(down_w[0]))
            for U in units(sp, "dn0", 1, STAGES["dn0"][0]):
                load_unit(U, rows_of(down_w[0]))
            load_unit(Unit("win", 0), rows_of(w_in_t))
            for U in units(sp, "win", 1, STAGES["win"][0] - 1, 2):
                load_unit(U, rows_of(w_in_t))
            load_unit(Unit("win", STAGES["win"][0] - 1), rows_of(w_in_t, LAST_W))
            sp.wait_ge(copied["win"], 1)
            sp.dma_start(rope_sb[:, :, :, :], rope_c).then_inc(A["rope_landed"], 16)
            sp.dma_start(w2k[:, :, :], tiles(w_cmp_k2[0])).then_inc(A["cmp_w_landed"], 16)
            for stage, w in (("uq", w_uq_t), ("ukv", w_ukv_t)):
                for u in range(STAGES[stage][0]):
                    load_unit(Unit(stage, u), rows_of(w))
                if stage == "uq":
                    sp.wait_ge(mm_done, Unit("win", STAGES["win"][0] - 1).done(KD // 2 - 1))
                    sp.wait_ge(rev_stored, 16)
                    sp.dma_start(bias[:, :, :], bass.AP(tensor=bias_scratch, offset=P - 1,
                                                        ap=[[383, P], [P * 384, HEADS + 1], [1, SEQ]]))\
                        .then_inc(A["bias_landed"], 16)
            for j in range(RING):
                rows_of(w_out_t)(Unit("wout", 0), j)
            k1 = w_cmp_k1[0].rearrange("(l d) n -> d l n", d=DK)
            v1 = w_cmp_v1[0].rearrange("(l d) n -> d l n", d=VD)
            for m in range(24):
                l0 = m % 8 * 4
                if m < RING:
                    sp.wait_ge(acc_step, 16 * ADA_CHUNKS)
                else:
                    sp.wait_ge(A["cw_used"], m - RING + 1)
                rows, src = [(P, k1[0:P]), (ROPE, k1[P:DK]), (P, v1)][m // 8]
                sp.dma_start(ada_raw[0:rows, m % RING, :].rearrange("p (l n) -> p l n", l=4),
                             src[:, l0:l0 + 4, :]).then_inc(ada_landed[m % RING], 16)
                if m == RING - 1:
                    sp.wait_ge(mm_done, Unit("ukv", 3).done(1))
                    sp.dma_start(w2v[:, :, :], tiles(w_cmp_v2[0])).then_inc(A["cmp_w_landed"], 16)
            for j in range(RING, STAGES["wout"][1]):
                rows_of(w_out_t)(Unit("wout", 0), j)
            for U in units(sp, "wout", 1, STAGES["wout"][0]):
                load_unit(U, rows_of(w_out_t))
            load_unit(Unit("gu1", 0), gate_up(1))
            for U in units(sp, "gu1", 1, STAGES["gu1"][0]):
                load_unit(U, gate_up(1))
            load_unit(Unit("dn1", 0), rows_of(down_w[1]))
            sp.wait_ge(gat[2]["gate_b_done"], 4)
            sp.dma_start(final_b[:, :], norm_final.rearrange("(a n) -> a n", a=1).broadcast_to([P, D]))\
                .then_inc(final_b_landed, 16)
            for U in units(sp, "dn1", 1, STAGES["dn1"][0]):
                load_unit(U, rows_of(down_w[1]))
            for t in range(TT):
                for h in range(2):
                    sp.wait_ge(final_done, 2 * t + h + 1)
                    sl = slice(h * D // 2, (h + 1) * D // 2)
                    sp.dma_start(out_t[:, t, sl], x_sb[:, t, sl]).then_inc(stored, 16)
            sp.wait_ge(stored, 16 * 2 * TT)

        @block.gpsimd
        def _(pool):
            pool.memset(b_row[:, :, :], 0.0).then_inc(rows_set, 1)
            pool.memset(ones[:, :], 1.0).then_inc(ones_set, 1)

            n_step = 0

            def rotate(t1, t2, cos, sin, tmp):
                nonlocal n_step
                for o, a, b in ((0, t1, cos), (1, t2, sin), (2, t1, sin), (3, t2, cos)):
                    pool.tensor_tensor(tmp[o], a, b, ALU.mult).then_inc(pool_step, 1)
                n_step += 4
                pool.wait_ge(pool_step, n_step)
                pool.tensor_tensor(t1, tmp[0], tmp[1], ALU.subtract).then_inc(pool_step, 1)
                pool.tensor_tensor(t2, tmp[2], tmp[3], ALU.add).then_inc(pool_step, 1)
                n_step += 2
                pool.wait_ge(pool_step, n_step)

            half = ROPE // 2
            pool.wait_ge(A["rope_landed"], 16)
            pool.wait_ge(copied["win"], 2 * STAGES["win"][0])
            pool.wait_ge(mod_done, ADA_CHUNKS)
            for t in range(TT):
                kr = proj[:, t, C_KR:C_KR + ROPE]
                rotate(kr[:, 0:half], kr[:, half:ROPE], rope_sb[:, t, 0, :], rope_sb[:, t, 1, :],
                       [rope_tmp[:, o, 0:half] for o in range(4)])
            pool.wait_ge(copied["uq"], 2 * STAGES["uq"][0])
            for t in range(TT):
                qr = q_mla[:, t, :].rearrange("p (h d) -> p h d", h=HEADS)
                cos, sin = (rope_sb[:, t, o, :].unsqueeze(1).broadcast_to([P, HEADS, half]) for o in range(2))
                rotate(qr[:, :, NOPE:NOPE + half], qr[:, :, NOPE + half:DK], cos, sin,
                       [rope_tmp[:, o, :].rearrange("p (h d) -> p h d", h=HEADS) for o in range(4)])

        @block.tensor
        def _(pe):
            def three(bank, lhs_hi, lhs_lo, rhs_hi, rhs_lo, start, stop):
                pe.matmul(bank, lhs_hi, rhs_hi, start=start, stop=False)
                pe.matmul(bank, lhs_hi, rhs_lo, start=False, stop=False)
                return pe.matmul(bank, lhs_lo, rhs_hi, start=False, stop=stop)

            def panel(U, j, T, k, bank, first, last, width=CW, tile_ready=None):
                pe.wait_ge(lo_done, U.done(j))
                s = j % RING
                for t in range(TT):
                    if tile_ready is not None:
                        tile_ready(t)
                    for kk in range(2):
                        mm = three(ps[:, bank + t, 0:width], T[0][:, k + kk, t * P:(t + 1) * P],
                                   T[1][:, k + kk, t * P:(t + 1) * P],
                                   w_hi[:, s, kk * CW:kk * CW + width], w_lo[:, s, kk * CW:kk * CW + width],
                                   first and kk == 0, last and kk == 1)
                mm.then_inc(mm_done, 1)

            def turn_ada(U, e):
                q = U.at(lambda u: ADA_OF[U.stage, u][e][0])
                a = ADA_OF[U.stage, U.first][e][1]
                pe.wait_ge(acc_step, q * 16 + 16)
                if not (U.stage == "start" and U.first == 0):
                    pe.wait_ge(mod_done, q)
                for b in range(4):
                    mm = pe.transpose(ps[:, ADA_BANK, b * P:(b + 1) * P], acc[:, a, b * P:(b + 1) * P], ident[:, :])
                mm.then_inc(acc_turned, 1)

            def turn_norm(n, r, k_tiles, src):
                if r >= 2:
                    pe.wait_ge(nrm[n]["T_lo_done" if n == "o" else "tmp_done"], r - 1)
                for kk in range(2):
                    for t in range(TT):
                        mm = pe.transpose(ps[:, T_BANK + r % 2, (kk * TT + t) * P:(kk * TT + t + 1) * P],
                                          src(2 * r + kk, t), ident[:, :])
                mm.then_inc(nrm[n]["turned"], 1)

            def turn_products(f, U):
                pe.wait_ge(gu[f]["prod_done"], U.at(lambda u: 2 * u + 2))
                for b in range(2):
                    for kk in range(2):
                        for t in range(TT):
                            mm = pe.transpose(ps[:, T_BANK + b, (kk * TT + t) * P:(kk * TT + t + 1) * P],
                                              act_sg[:, t, (2 * b + kk) * P:(2 * b + kk + 1) * P], ident[:, :])
                    mm.then_inc(gu[f]["prod_turned"], 1)

            def gate_up_unit(f, U, fresh):
                prev = None if U.first == 0 else before(U)
                for j in range(KD):
                    if fresh:
                        r = j // 2
                        if j % 2 == 0 and 1 <= r < 7:
                            turn_norm(NORM_OF[U.stage], r + 1, KD, lambda k, t: xn[:, t, k * P:(k + 1) * P])
                        if j % 2 == 0:
                            pe.wait_ge(nrm[NORM_OF[U.stage]]["T_lo_done"], r + 1)
                    elif j == 0:
                        pe.wait_ge(gu[f]["silu_done"], U.at(lambda u: 2 * u))
                    elif j == 1:
                        pe.wait_ge(gu[f]["prod_done"], U.at(lambda u: 2 * u))
                    panel(U, j, (hT_hi, hT_lo), j // 2 * 2, 2 * (j % 2), j < 2, j >= KD - 2)
                    if not fresh and j == 0 and f == 0:
                        turn_ada(prev, 0)
                    if not fresh and j == 1:
                        turn_products(f, prev)

            def gate_broadcast(f, c):
                pe.wait_ge(gat[f]["diag_done"], c + 1)
                if c > 0:
                    pe.wait_ge(gat[f]["gate_b_done"], c)
                pe.matmul(ps[:, MISC_BANK, :], ones[:, :], norm_tmp[:, c % 2, :], start=True, stop=True).then_inc(gat[f]["gate_mm"], 1)

            def down_unit(f, U):
                stage, L = U.stage, STAGES[U.stage][1]
                done = res[stage]["bank_read"]
                for j in range(L):
                    if j == L - 2 and U.first == 0:
                        pe.wait_ge(gu[f]["actT_lo_done"], 2 * (FF // CW))

                    def tile_ready(t):
                        if j == 0 and U.first > 0:
                            pe.wait_ge(done, U.at(lambda u: 2 * (u - 1) + t + 1))
                        elif j == 0:
                            pe.wait_ge(gu[f]["silu_done"], 2 * (FF // CW))
                    panel(U, j, (act_hi, act_lo), 2 * j, 0, j == 0, j == L - 1, tile_ready=tile_ready)
                    if j == 0 and f == 0:
                        if U.first == 0:
                            turn_ada(Unit("gu0", FF // CW - 1), 0)
                        else:
                            turn_ada(before(U), 1)
                    if j == 1 and U.first == 0:
                        turn_products(f, Unit(f"gu{f}", FF // CW - 1))
                    if j == 14 and f == 0:
                        turn_ada(U, 0)
                    if U.first == 0 and j in (8, 10, 12, 14):
                        gate_broadcast(2 * f, (j - 8) // 2)

            pe.wait_ge(const_landed, 16 * 10)
            pe.transpose(ps[:, MISC_BANK, 0:NV], v_rows[:, :], ident[0:NV, 0:NV]).then_inc(v_turned, 1)
            pe.wait_ge(rel_landed, 16)
            pe.wait_ge(ones_set, 1)
            pe.matmul(ps[0:HEADS + 1, T_BANK + 1, 0:384], rel_sb[:, :], bucket_sb[:, :], start=True, stop=True)\
                .then_inc(rev_mm, 1)
            turn_ada(Unit("start", 0), 0)
            turn_ada(Unit("start", 1), 0)
            for U in units(pe, "start", 2, START_CHUNKS, 2):
                turn_ada(U, 0)

            def first_rounds(n):
                pe.wait_ge(nrm[n]["xn_done"], TT)
                for r in range(2):
                    turn_norm(n, r, KD, lambda k, t: xn[:, t, k * P:(k + 1) * P])

            pe.wait_ge(rev_done, 1)
            first_rounds("ffn1")
            gate_up_unit(0, Unit("gu0", 0), True)
            for U in units(pe, "gu0", 1, FF // CW):
                gate_up_unit(0, U, False)
            down_unit(0, Unit("dn0", 0))
            for U in units(pe, "dn0", 1, D // CW):
                down_unit(0, U)

            def project_in(U, width=CW):
                L = STAGES["win"][1]
                for j in range(L):
                    def tile_ready(t):
                        if j == 0 and U.first > 0:
                            pe.wait_ge(copied["win"], U.at(lambda u: 2 * (u - 1) + t + 1))
                        elif j == 0:
                            pe.wait_ge(res["dn0"]["bank_read"], 2 * (D // CW))
                    if U.first == 0:
                        if 1 <= j < 7:
                            turn_norm("mix", j + 1, KD, lambda k, t: xn[:, t, k * P:(k + 1) * P])
                        pe.wait_ge(nrm["mix"]["T_lo_done"], j + 1)
                    panel(U, j, (hT_hi, hT_lo), 2 * j, 0, j == 0, j == L - 1, width, tile_ready)
                    if j == 0:
                        if U.first == 0:
                            turn_ada(Unit("dn0", D // CW - 1), 1)
                        else:
                            turn_ada(before(U), 0)

            first_rounds("mix")
            project_in(Unit("win", 0))
            for U in units(pe, "win", 1, STAGES["win"][0] - 1, 2):
                project_in(U)
            project_in(Unit("win", STAGES["win"][0] - 1), LAST_W)

            pe.wait_ge(nrm["mla"]["xn_done"], 4)
            for r in range(5):
                c0 = C_Q if r < 3 else C_KV - 6 * P
                turn_norm("mla", r, 10, lambda k, t: proj[:, t, c0 + k * P:c0 + (k + 1) * P])
            bank = 0
            for stage, T, n0 in (("uq", cqT, 0), ("ukv", ckvT, 3)):
                for u in range(STAGES[stage][0]):
                    L = STAGES[stage][1]
                    b = 2 * ((u + (stage == "ukv")) % 2)

                    def tile_ready(t):
                        if u >= 2:
                            pe.wait_ge(copied[stage], 2 * (u - 2) + t + 1)
                        elif stage == "ukv":
                            pe.wait_ge(copied["uq"], 2 * (u + 1) + t + 1)
                        elif u == 0:
                            pe.wait_ge(copied["win"], 2 * STAGES["win"][0])
                    for j in range(L):
                        if u == 0:
                            pe.wait_ge(nrm["mla"]["T_lo_done"], n0 + j + 1)
                        panel(Unit(stage, u), j, T, 2 * j, b, j == 0, j == L - 1,
                              tile_ready=tile_ready if j == 0 else None)
            pe.wait_ge(pool_step, 6 * TT)
            for t in range(TT):
                mm = pe.transpose(ps[0:ROPE, T_BANK, t * P:(t + 1) * P], proj[:, t, C_KR:C_KR + ROPE], ident[:, :])
            mm.then_inc(A["kr_turned"], 1)
            pe.wait_ge(pool_step, 12 * TT)
            pe.wait_ge(copied["ukv"], 2 * STAGES["ukv"][0])

            def turn_q(u):
                if u < HEADS:
                    h, e = u, u
                else:
                    h, e = (u - HEADS) // 2, HEADS + (u - HEADS) // 2
                    if u % 2:
                        return
                if e == 0:
                    pe.wait_ge(A["kr_copied"], 1)
                elif e == HEADS:
                    pe.wait_ge(A["vc_copied"], 2 * HPG)
                else:
                    pe.wait_ge(A["qk_copied"], e)
                if 0 < e < HEADS:
                    pe.wait_ge(A["qr_copied"], e)
                for t in range(TT):
                    cols = slice(t * P, (t + 1) * P)
                    cols2 = slice(SEQ + t * P, SEQ + (t + 1) * P)
                    if u < HEADS:
                        pe.transpose(ps[:, T_BANK, cols], q_mla[:, t, h * DK:h * DK + NOPE], ident[:, :])
                        pe.transpose(ps[:, T_BANK, cols2], kv_mla[:, t, h * 2 * P:h * 2 * P + P], ident[:, :])
                        mm = pe.transpose(ps[0:ROPE, T_BANK + 1, cols], q_mla[:, t, h * DK + NOPE:(h + 1) * DK],
                                          ident[:, :])
                    else:
                        q0 = C_NQ + h * DK
                        pe.transpose(ps[:, T_BANK, cols], proj[:, t, q0:q0 + NOPE], ident[:, :])
                        mm = pe.transpose(ps[0:ROPE, T_BANK, cols2], proj[:, t, q0 + NOPE:q0 + DK], ident[:, :])
                mm.then_inc(A["q_turned"], 1)

            def score(u):
                mla = u < HEADS
                h = u if mla else (u - HEADS) // 2
                e = u if mla else HEADS + h
                b = e % 2
                pe.wait_ge(A["qk_copied"], e + 1)
                if mla:
                    pe.wait_ge(A["qr_copied"], e + 1)
                if u >= 2:
                    pe.wait_ge(A["maxed"], 2 * (u - 1))
                else:
                    pe.wait_ge(copied["ukv"], 2 * STAGES["ukv"][0])
                kx = (1 + u % 2) * GROUPS + h // HPG
                for t in range(TT):
                    n = (t + 1) * P
                    dst = ps[:, 2 + u % 2, t * P:t * P + n]
                    pe.matmul(dst, qkT[:, b, t * P:(t + 1) * P],
                              qkT[:, b, SEQ:SEQ + n] if mla else kT128[:, kx, 0:n], start=True, stop=False)
                    mm = pe.matmul(dst, qrT[:, b, t * P:(t + 1) * P],
                                   krT[:, 0:n] if mla else kT64[:, kx, 0:n], start=False, stop=True)
                mm.then_inc(A["scored"], 1)
                if not mla and u % 2 == 0:
                    g = h // HPG
                    for t in range(TT):
                        dst = ps[:, 5, t * SEQ + h * 32:t * SEQ + h * 32 + N_CMP]
                        pe.matmul(dst, qkT[:, b, t * P:(t + 1) * P], kc128[:, g * N_CMP:(g + 1) * N_CMP],
                                  start=True, stop=False)
                        mm = pe.matmul(dst, qrT[:, b, t * P:(t + 1) * P], kc64[:, g * N_CMP:(g + 1) * N_CMP],
                                       start=False, stop=True)
                    mm.then_inc(A["cmp_scored"], 1)

            def turn_p(u):
                pe.wait_ge(A["exped"], 2 * (u + 1))
                if u >= 2:
                    pe.wait_ge(A["pT_copied"], u - 1)
                for b in range(3):
                    mm = pe.transpose(ps[:, 6 + u % 2, b * P:(b + 1) * P], probs[:, u % 2, b * P:(b + 1) * P],
                                      ident[:, :])
                mm.then_inc(A["p_turned"], 1)

            def times_v(u):
                pe.wait_ge(A["pT_copied"], u + 1)
                if u >= 2:
                    pe.wait_ge(A["o_done"], 2 * (u - 1))
                for t in range(TT):
                    for kt in range(t + 1):
                        if u < HEADS:
                            v = kv_mla[:, kt, u * 2 * P + P:(u + 1) * 2 * P]
                        else:
                            kx = (1 + u % 2) * GROUPS + (u - HEADS) // 2 // HPG
                            v = proj[:, kt, C_NV + kx * VD:C_NV + (kx + 1) * VD]
                        mm = pe.matmul(ps[:, u % 2, t * P:(t + 1) * P], probsT[:, u % 2, (t + kt) * P:(t + kt + 1) * P],
                                       v, start=kt == 0, stop=kt == t)
                mm.then_inc(A["pv_done"], 1)

            def attend(lo, hi):
                for s in range(lo, hi + 3):
                    if s < hi:
                        turn_q(s)
                    if lo <= s - 1 < hi:
                        score(s - 1)
                    if lo <= s - 2 < hi:
                        turn_p(s - 2)
                    if lo <= s - 3 < hi:
                        times_v(s - 3)

            attend(0, HEADS)

            for r in range(3):
                pe.wait_ge(A["qk_copied"], HEADS) if r == 0 else pe.wait_ge(A["kT_copied"], 2 * r)
                if r == 0:
                    pe.wait_ge(A["qr_copied"], HEADS)
                for i in range(2):
                    for t in range(TT):
                        k0 = C_NK + (2 * r + i) * DK
                        cols = slice(i * SEQ + t * P, i * SEQ + (t + 1) * P)
                        pe.transpose(ps[:, T_BANK, cols], proj[:, t, k0:k0 + P], ident[:, :])
                        mm = pe.transpose(ps[0:ROPE, T_BANK + 1, cols], proj[:, t, k0 + P:k0 + DK], ident[:, :])
                mm.then_inc(A["k_turned"], 1)
            pe.wait_ge(A["maxed"], 2 * HEADS)
            for g in range(GROUPS):
                for t in range(TT):
                    mm = pe.transpose(ps[:, 2, g * SEQ + t * P:g * SEQ + (t + 1) * P],
                                      proj[:, t, C_NV + g * VD:C_NV + (g + 1) * VD], ident[:, :])
            mm.then_inc(A["v_turned_c"], 1)
            id32 = ident[0:CMP_LEN, 0:CMP_LEN]
            pe.transpose(ps[:, 3, 0:32], pe_sb[:, 0:P], id32)
            pe.transpose(ps[0:ROPE, 3, 32:64], pe_sb[:, P:DK], id32)
            pe.transpose(ps[:, 3, 64:96], pe_sb[:, DK:DK + VD], id32).then_inc(A["pe_turned"], 1)
            pe.wait_ge(A["o_done"], 2 * HEADS)
            for m in range(24):
                part, l0 = m // 8, m % 8 * 4
                if m % 8 == 0:
                    pe.wait_ge(A["kpe_done"], (4, 8, 12)[part])
                pe.wait_ge(ada_landed[m % RING], 16 * (2 * ADA_CHUNKS + m // RING + 1))
                blocks, rows = ((kpe128, P), (kpe64, ROPE), (vpe, P))[part]
                for l in range(4):
                    mm = pe.matmul(ps[0:GROUPS * N_CMP, part // 2, 0:CMP_HID], blocks[:, l0 + l, :],
                                   ada_raw[0:rows, m % RING, l * CMP_HID:(l + 1) * CMP_HID],
                                   start=m in (0, 16) and l == 0, stop=m in (15, 23) and l == 3)
                mm.then_inc(A["cw_used"], 1)
            n = GROUPS * N_CMP
            pe.wait_ge(A["hid_done"], 2)
            for i in range(4):
                mm = pe.transpose(ps[:, 2, i * 32:i * 32 + n], hid[:, i // 2, i % 2 * P:(i % 2 + 1) * P],
                                  ident[0:n, 0:n])
            mm.then_inc(A["hid_turned"], 1)
            pe.wait_ge(A["hidT_copied"], 1)
            pe.wait_ge(A["cmp_w_landed"], 32)
            for rows, c0 in ((P, 0), (ROPE, P)):
                for i in range(2):
                    mm = pe.matmul(ps[0:rows, 3, c0 // 4:c0 // 4 + n], w2k[:, i, c0:c0 + rows], hidT[:, i, :],
                                   start=i == 0, stop=i == 1)
            mm.then_inc(A["kc_mm"], 1)
            for g in range(GROUPS):
                if g == 0:
                    pe.wait_ge(A["kT_copied"], 6)
                for h in range(HPG):
                    for i in range(2):
                        mm = pe.matmul(ps[32 * h:32 * h + N_CMP, T_BANK + g, h * VD:(h + 1) * VD],
                                       hidT[:, 2 + i, g * N_CMP:(g + 1) * N_CMP], w2v[:, i, :],
                                       start=i == 0, stop=i == 1)
            mm.then_inc(A["kc_mm"], 1)
            pe.wait_ge(A["kc_copied"], 2)
            attend(HEADS, 3 * HEADS)

            for t in range(TT):
                pe.wait_ge(A["cmp_exped"], t + 1)
                if t == 0:
                    pe.wait_ge(A["pT_copied"], 3 * HEADS)
                for g in range(GROUPS):
                    mm = pe.transpose(ps[:, 6 + t, g * P:(g + 1) * P], probs[:, t, g * P:(g + 1) * P], ident[:, :])
                mm.then_inc(A["cmp_turned"], 1)
            pe.wait_ge(A["o_done"], 6 * HEADS)
            for t in range(TT):
                pe.wait_ge(A["cmp_copied"], t + 1)
                for g in range(GROUPS):
                    pe.matmul(ps[:, 2 * t + g, :], probsT[:, t, g * P:(g + 1) * P], v_cmp[:, g, :],
                              start=True, stop=True).then_inc(A["cmp_pv"], 1)

            def o_tile(k, t):
                return (o_mla if k < HEADS else o_nsa)[:, t, k % HEADS * VD:(k % HEADS + 1) * VD]

            def project_out(U):
                L = STAGES["wout"][1]
                for j in range(L):
                    def tile_ready(t):
                        if j == 0 and U.first > 0:
                            pe.wait_ge(res["wout"]["bank_read"], U.at(lambda u: 2 * (u - 1) + t + 1))
                        elif j == 0:
                            pe.wait_ge(A["cmp_o"], 2 * HEADS)
                    if U.first == 0:
                        if 1 <= j < 7:
                            if j == 3:
                                pe.wait_ge(A["cmp_o"], 2 * HEADS)
                            turn_norm("o", j + 1, KD, o_tile)
                        pe.wait_ge(nrm["o"]["T_lo_done"], j + 1)
                        if 2 <= j <= 5:
                            gate_broadcast(1, j - 2)
                    panel(U, j, (hT_hi, hT_lo), 2 * j, 0, j == 0, j == L - 1, CW, tile_ready)

            pe.wait_ge(A["cmp_ready"], 2)
            for r in range(2):
                turn_norm("o", r, KD, o_tile)
            project_out(Unit("wout", 0))
            for U in units(pe, "wout", 1, STAGES["wout"][0]):
                project_out(U)

            first_rounds("ffn2")
            pe.wait_ge(res["wout"]["bank_read"], 2 * (D // CW))
            gate_up_unit(1, Unit("gu1", 0), True)
            for U in units(pe, "gu1", 1, FF // CW):
                gate_up_unit(1, U, False)
            down_unit(1, Unit("dn1", 0))
            for U in units(pe, "dn1", 1, D // CW):
                down_unit(1, U)

        @block.scalar
        def _(act):
            def hi(U, j):
                s = j % RING
                act.wait_ge(raw_landed[s], U.landed(j))
                free = U.slot_free(j)
                if free is not None:
                    act.wait_ge(mm_done, free)
                act.activation(part(U, w_hi, s), part(U, raw, s), ACT.Copy).then_inc(hi_done, 1)

            def silu(f, U):
                act.wait_ge(mm_done, U.done(KD - 2))
                for t in range(TT):
                    act.activation(act_sg[:, t, :], ps[:, t, :], ACT.Silu).then_inc(gu[f]["silu_done"], 1)

            def actT(f, U):
                for b in range(2):
                    act.wait_ge(gu[f]["prod_turned"], U.at(lambda u: 2 * u + b + 1))
                    at = U.at(lambda u: (4 * u + 2 * b) * SEQ)
                    act.activation(act_hi[:, :, :].rearrange("p k n -> p (k n)")[:, bass.ds(at, CW)],
                                   ps[:, T_BANK + b, :], ACT.Copy).then_inc(gu[f]["actT_hi_done"], 1)

            def squares(n, parts):
                for i, (src, junk) in enumerate(parts):
                    act.activation(junk, src, ACT.Square, accum_out=stat[:, 0, i:i + 1])\
                       .then_inc(nrm[n]["squares"], 1)
                act.wait_ge(nrm[n]["mean"], 1)
                w = len(parts)
                act.activation(stat[:, 2, 0:w], stat[:, 1, 0:w], ACT.Sqrt).then_inc(nrm[n]["root"], 1)

            def x_squares(n, added):
                for s, v in added:
                    act.wait_ge(s, v)
                squares(n, [(x_sb[:, t, :], xn[:, t, :]) for t in range(TT)])

            def round_hi(n, r, T, k):
                if n == "o":
                    act.wait_ge(nrm[n]["turned"], r + 1)
                    src = ps[:, T_BANK + r % 2, :]
                else:
                    act.wait_ge(nrm[n]["tmp_done"], r + 1)
                    src = norm_tmp[:, r % 2, :]
                act.activation(T[:, k:k + 2, :].rearrange("p k n -> p (k n)"), src, ACT.Copy)\
                   .then_inc(nrm[n]["T_hi_done"], 1)

            def gate_copy(f, c, dst, factor):
                act.wait_ge(gat[f]["gate_mm"], c + 1)
                act.activation(dst[:, c * CW:(c + 1) * CW], ps[:, MISC_BANK, :], ACT.Copy, scale=factor)\
                   .then_inc(gat[f]["gate_b_done"], 1)

            def copy_out(stage, U, dst, bank, width=CW):
                act.wait_ge(mm_done, U.done(STAGES[stage][1] - 1))
                at = U.at(lambda u: u * CW)
                for t in range(TT):
                    act.activation(dst[:, t, bass.ds(at, width)], ps[:, bank + t, 0:width], ACT.Copy)\
                       .then_inc(copied[stage], 1)

            dma = act.dma_start
            dma(ident[:, :], ident_c).then_inc(const_landed, 16)
            for name, v in (("ffn1", norm_ffn1), ("mix", norm_mix), ("ffn2", norm_ffn2), ("q", mla_q_norm),
                            ("kv", mla_kv_norm), ("c", c)):
                n = v.shape[1] // P
                dma(v_rows[VROWS[name]:VROWS[name] + n, :], v[0].rearrange("(k p) -> k p", p=P))\
                    .then_inc(const_landed, 16)
            dma(bucket_sb[:, :], bucket_c).then_inc(const_landed, 16)
            dma(pe_sb[:, 0:DK], pe_cmp_k[0]).then_inc(const_landed, 16)
            dma(pe_sb[:, DK:DK + VD], pe_cmp_v[0]).then_inc(const_landed, 16)
            dma(x_sb[:, :, :], x_t).then_inc(x_landed, 16)
            act.wait_ge(rel_set, 2)
            dma(rel_sb[0:BUCKETS, 0:HEADS], rel_bias).then_inc(rel_landed, 16)
            act.wait_ge(v_done, 1)
            act.activation(silu_c[:, :], v_cols[:, VROWS["c"]:NV], ACT.Silu).then_inc(silu_c_done, 1)
            act.wait_ge(rev_done, 1)
            dma(bias_scratch.ap(), rev_sb[:, :].unsqueeze(1).broadcast_to([HEADS + 1, P, 384]))\
                .then_inc(rev_stored, 16)

            def fresh_unit(n, U, per, added, between):
                hi(U, 0)
                hi(U, 1)
                between(1)
                hi(U, 2)
                hi(U, 3)
                between(3)
                if added is not None:
                    x_squares(n, added)
                for r in range(RING // per):
                    round_hi(n, r, hT_hi, 2 * r)
                for j in range(RING, STAGES[U.stage][1]):
                    if j % per == 0:
                        round_hi(n, j // per, hT_hi, j // per * 2)
                    hi(U, j)
                    between(j)

            def gate_up_unit(f, U):
                for j in range(KD):
                    hi(U, j)
                    if j == 1:
                        silu(f, before(U))
                    if j == 3:
                        actT(f, before(U))

            def down_unit(f, U):
                for j in range(STAGES[U.stage][1]):
                    hi(U, j)
                    if U.first == 0:
                        if j == 1:
                            silu(f, Unit(f"gu{f}", FF // CW - 1))
                        if j == 3:
                            actT(f, Unit(f"gu{f}", FF // CW - 1))
                        if j in (10, 12, 14, 16):
                            gate_copy(2 * f, (j - 10) // 2, gate_b, 0.5)

            fresh_unit("ffn1", Unit("gu0", 0), 2, [(x_landed, 16)], lambda j: None)
            act.wait_ge(rev_stored, 16)
            for U in units(act, "gu0", 1, FF // CW):
                gate_up_unit(0, U)
            down_unit(0, Unit("dn0", 0))
            for U in units(act, "dn0", 1, D // CW):
                down_unit(0, U)

            def project_in(U):
                for j in range(STAGES["win"][1]):
                    hi(U, j)
                    if j == 1:
                        copy_out("win", before(U), proj, 0)

            fresh_unit("mix", Unit("win", 0), 1, [(res["dn0"]["x_added"], 2 * (D // CW))], lambda j: None)
            for U in units(act, "win", 1, STAGES["win"][0] - 1, 2):
                project_in(U)
            last_in = Unit("win", STAGES["win"][0] - 1)
            project_in(last_in)

            for j in range(STAGES["uq"][1]):
                hi(Unit("uq", 0), j)
            copy_out("win", last_in, proj, 0, LAST_W)
            squares("mla", [(proj[:, t, c0:c0 + w], q_mla[:, t, c0:c0 + w])
                            for c0, w in ((C_Q, Q_RANK), (C_KV, KV_RANK)) for t in range(TT)])
            for r in range(5):
                round_hi("mla", r, cqT[0] if r < 3 else ckvT[0], 2 * r if r < 3 else 2 * r - 6)
            small_units = [("uq", u) for u in range(STAGES["uq"][0])] + [("ukv", u) for u in range(STAGES["ukv"][0])]

            def copy_small(i):
                stage, u = small_units[i]
                copy_out(stage, Unit(stage, u), q_mla if stage == "uq" else kv_mla, 2 * (i % 2))

            for i, (stage, u) in enumerate(small_units):
                if i > 0:
                    for j in range(STAGES[stage][1]):
                        hi(Unit(stage, u), j)
                    copy_small(i - 1)
            copy_small(len(small_units) - 1)
            for j in range(RING):
                hi(Unit("wout", 0), j)
            act.activation(gates[:, :, :], proj[:, :, C_NG:D_IN], ACT.Exp, scale=-1.0).then_inc(A["gates_exp"], 1)
            act.wait_ge(A["kr_turned"], 1)
            act.activation(krT[:, :], ps[0:ROPE, T_BANK, 0:SEQ], ACT.Copy).then_inc(A["kr_copied"], 1)

            def copy_q(u):
                if u >= HEADS and u % 2:
                    return
                e = u if u < HEADS else HEADS + (u - HEADS) // 2
                act.wait_ge(A["q_turned"], e + 1)
                if u < HEADS:
                    if u >= 2:
                        act.wait_ge(A["scored"], u - 1)
                    act.activation(qkT[:, e % 2, :], ps[:, T_BANK, :], ACT.Copy).then_inc(A["qk_copied"], 1)
                else:
                    act.wait_ge(A["scored"], max(HEADS, u - 2))
                    act.activation(qkT[:, e % 2, 0:SEQ], ps[:, T_BANK, 0:SEQ], ACT.Copy)
                    act.activation(qrT[:, e % 2, :], ps[0:ROPE, T_BANK, SEQ:2 * SEQ], ACT.Copy)\
                       .then_inc(A["qk_copied"], 1)

            def exps(u):
                act.wait_ge(A["neg_done"], u + 1)
                for t in range(TT):
                    sl = slice(t * P, t * P + (t + 1) * P)
                    act.activation(probs[:, u % 2, sl], probs[:, u % 2, sl], ACT.Exp, bias=neg_max[:, u, t:t + 1],
                                   scale=SCALE, accum_out=row_sum[:, u, t:t + 1]).then_inc(A["exped"], 1)

            def copy_p(u):
                act.wait_ge(A["p_turned"], u + 1)
                if u >= 2:
                    act.wait_ge(A["pv_done"], u - 1)
                act.activation(probsT[:, u % 2, :], ps[:, 6 + u % 2, 0:3 * P], ACT.Copy).then_inc(A["pT_copied"], 1)

            def attend(lo, hi_):
                for s in range(lo, hi_ + 3):
                    if s < hi_:
                        copy_q(s)
                    if lo <= s - 1 < hi_:
                        exps(s - 1)
                    if lo <= s - 2 < hi_:
                        copy_p(s - 2)

            attend(0, HEADS)
            for r in range(3):
                act.wait_ge(A["k_turned"], r + 1)
                act.activation(kT128[:, 2 * r:2 * r + 2, :].rearrange("p k n -> p (k n)"), ps[:, T_BANK, :],
                               ACT.Copy).then_inc(A["kT_copied"], 1)
            for i in range(2):
                act.wait_ge(A["cw_used"], (16, 24)[i])
                act.activation(hid[:, i, :], ps[0:GROUPS * N_CMP, i, 0:CMP_HID], ACT.Silu)\
                   .then_inc(A["hid_done"], 1)
            attend(HEADS, 3 * HEADS)

            for t in range(TT):
                act.wait_ge(A["cmp_ready"], t + 1)
                pc = probs[:, t, 0:SEQ].rearrange("p (h n) -> p h n", n=32)[:, :, 0:CMP_IN_REACH[t]]
                act.activation(pc, pc, ACT.Exp, scale=SCALE).then_inc(A["cmp_exped"], 1)
            for t in range(TT):
                act.wait_ge(A["cmp_turned"], t + 1)
                if t == 0:
                    act.wait_ge(A["pv_done"], 3 * HEADS)
                act.activation(probsT[:, t, 0:SEQ], ps[:, 6 + t, 0:SEQ], ACT.Copy).then_inc(A["cmp_copied"], 1)

            for r in range(4):
                round_hi("o", r, hT_hi, 2 * r)
            U = Unit("wout", 0)
            for j in range(RING, STAGES["wout"][1]):
                round_hi("o", j, hT_hi, 2 * j)
                hi(U, j)
                gate_copy(1, j - RING, kv_mla[:, 0, :], 1.0)
            for U in units(act, "wout", 1, STAGES["wout"][0]):
                for j in range(STAGES["wout"][1]):
                    hi(U, j)

            fresh_unit("ffn2", Unit("gu1", 0), 2, [(res["wout"]["x_added"], 2 * (D // CW))], lambda j: None)
            for U in units(act, "gu1", 1, FF // CW):
                gate_up_unit(1, U)
            down_unit(1, Unit("dn1", 0))
            for U in units(act, "dn1", 1, D // CW):
                down_unit(1, U)
            x_squares("final", [(res["dn1"]["x_added"], 2 * (D // CW))])

        @block.vector
        def _(dve):
            steps = 0

            def then_wait(ins):
                nonlocal steps
                steps += 1
                ins.then_inc(dve_step, 1)
                dve.wait_ge(dve_step, steps)

            def lo(U, j):
                s = j % RING
                dve.wait_ge(hi_done, U.done(j))
                dve.tensor_tensor(part(U, w_lo, s), part(U, raw, s), part(U, w_hi, s).bitcast(F32), ALU.subtract)\
                   .then_inc(lo_done, 1)

            def add_ada(U, e, p):
                q = U.at(lambda u: ADA_OF[U.stage, u][e][0])
                q0, a = ADA_OF[U.stage, U.first][e]
                slot = p % RING
                dve.wait_ge(ada_landed[slot], q * 32 + 16 * (p // RING + 1))
                for kk in range(2):
                    k = 2 * p + kk
                    if k == 0:
                        dve.wait_ge(b_landed[a], U.at(lambda u: 16 * (ADA_BEFORE[ADA_OF[U.stage, u][e][0]][0] + 1)))
                        if ADA_BEFORE[q0][1] is not None:
                            dve.wait_ge(acc_turned, U.at(lambda u: ADA_BEFORE[ADA_OF[U.stage, u][e][0]][1] + 1))
                    else:
                        dve.wait_ge(acc_step, q * 16 + k)
                    dve.scalar_tensor_tensor(acc[:, a, :], ada_raw[:, slot, kk * CW:(kk + 1) * CW], silu_c[:, k:k + 1],
                                             b_row[:, a, :] if k == 0 else acc[:, a, :], ALU.mult, ALU.add)\
                       .then_inc(acc_step, 1)

            def sum_ada(U, e):
                q = U.at(lambda u: ADA_OF[U.stage, u][e][0])
                dve.wait_ge(acc_turned, q + 1)
                dve.tensor_reduce(mod_cols[:, bass.ds(q * 4, 4)],
                                  ps[:, ADA_BANK, :].rearrange("p (b n) -> p b n", b=4), AX.X, ALU.add)\
                   .then_inc(mod_done, 1)

            def rstd(n, parts):
                w = parts[-1][1]
                dve.wait_ge(nrm[n]["squares"], w)
                for i, (a, b, size) in enumerate(parts):
                    ins = dve.tensor_scalar(stat[:, 1, a:b], stat[:, 0, a:b], 1.0 / size, EPS, ALU.mult, ALU.add)
                ins.then_inc(nrm[n]["mean"], 1)
                dve.wait_ge(nrm[n]["root"], 1)
                v, root, r, e, out_ = (stat[:, i, 0:w] for i in (1, 2, 3, 4, 5))
                then_wait(dve.reciprocal(r, root))
                then_wait(dve.tensor_tensor(e, r, r, ALU.mult))
                then_wait(dve.tensor_tensor(e, e, v, ALU.mult))
                then_wait(dve.tensor_scalar(e, e, -0.5, 1.5, ALU.mult, ALU.add))
                then_wait(dve.tensor_tensor(out_, r, e, ALU.mult))

            def norm_x(n):
                rstd(n, [(0, TT, D)])
                for t in range(TT):
                    dve.tensor_scalar(xn[:, t, :], x_sb[:, t, :], stat[:, 5, t:t + 1], None, ALU.mult)\
                       .then_inc(nrm[n]["xn_done"], 1)

            def make_scale(n, seg, mods):
                dve.wait_ge(mod_done, mods)
                g0 = VROWS[n]
                then_wait(dve.scalar_tensor_tensor(scale_cols[:, :], mod_cols[:, seg * KD:(seg + 1) * KD], 1.0,
                                                   v_cols[:, g0:g0 + KD], ALU.add, ALU.mult))

            def round_tmp(n, r, shift):
                dve.wait_ge(nrm[n]["turned"], r + 1)
                if r >= 2:
                    dve.wait_ge(nrm[n]["T_lo_done"], r - 1)
                for kk in range(2):
                    k = 2 * r + kk
                    dst, src = (a[:, kk * SEQ:(kk + 1) * SEQ] for a in (norm_tmp[:, r % 2, :], ps[:, T_BANK + r % 2, :]))
                    if n == "mla":
                        ins = dve.tensor_scalar(dst, src, v_cols[:, VROWS["q"] + k:VROWS["q"] + k + 1], None, ALU.mult)
                    else:
                        ins = dve.tensor_scalar(dst, src, scale_cols[:, k:k + 1],
                                                mod_cols[:, shift * KD + k:shift * KD + k + 1], ALU.mult, ALU.add)
                ins.then_inc(nrm[n]["tmp_done"], 1)

            def round_lo(n, r, T, k):
                dve.wait_ge(nrm[n]["T_hi_done"], r + 1)
                src = ps[:, T_BANK + r % 2, :] if n == "o" else norm_tmp[:, r % 2, :]
                dve.tensor_tensor(T[1][:, k:k + 2, :].rearrange("p k n -> p (k n)"), src,
                                  T[0][:, k:k + 2, :].rearrange("p k n -> p (k n)").bitcast(F32), ALU.subtract)\
                   .then_inc(nrm[n]["T_lo_done"], 1)

            def rounds(n, rs, shift, T=None, k0=0):
                T = (hT_hi, hT_lo) if T is None else T
                for i, r in enumerate(rs):
                    round_tmp(n, r, shift)
                    if i:
                        round_lo(n, r - 1, T, 2 * (r - 1) - k0)
                round_lo(n, rs[-1], T, 2 * rs[-1] - k0)

            def product(f, U):
                dve.wait_ge(mm_done, U.done(KD - 1))
                for t in range(TT):
                    dve.wait_ge(gu[f]["silu_done"], U.at(lambda u: 2 * u + t + 1))
                    dve.tensor_tensor(act_sg[:, t, :], act_sg[:, t, :], ps[:, 2 + t, :], ALU.mult)\
                       .then_inc(gu[f]["prod_done"], 1)

            def actT_low(f, U):
                flat = [a[:, :, :].rearrange("p k n -> p (k n)") for a in (act_hi, act_lo)]
                for b in range(2):
                    dve.wait_ge(gu[f]["actT_hi_done"], U.at(lambda u: 2 * u + b + 1))
                    at = U.at(lambda u: (4 * u + 2 * b) * SEQ)
                    dve.tensor_tensor(flat[1][:, bass.ds(at, CW)], ps[:, T_BANK + b, :],
                                      flat[0][:, bass.ds(at, CW)].bitcast(F32), ALU.subtract)\
                       .then_inc(gu[f]["actT_lo_done"], 1)

            def residual(U, gate, L):
                s = res[U.stage]
                dve.wait_ge(mm_done, U.done(L - 1))
                at = U.at(lambda u: u * CW)
                for t in range(TT):
                    dve.tensor_tensor(act_sg[:, t, :], ps[:, t, :], gate[:, bass.ds(at, CW)], ALU.mult)\
                       .then_inc(s["bank_read"], 1)
                for t in range(TT):
                    dve.wait_ge(s["bank_read"], U.at(lambda u: 2 * u + t + 1))
                    xs = x_sb[:, t, bass.ds(at, CW)]
                    dve.tensor_tensor(xs, xs, act_sg[:, t, :], ALU.add).then_inc(s["x_added"], 1)
                dve.wait_ge(s["x_added"], U.at(lambda u: 2 * u + 2))

            def gate_diag(f, c, seg):
                if c >= 2:
                    dve.wait_ge(gat[f]["gate_mm"], c - 1)
                for b in range(4):
                    col = seg * KD + 4 * c + b
                    ins = dve.tensor_scalar(norm_tmp[:, c % 2, b * P:(b + 1) * P], ident[:, :],
                                            mod_cols[:, col:col + 1], None, ALU.mult)
                ins.then_inc(gat[f]["diag_done"], 1)

            dve.memset(rel_sb[:, :], 0.0).then_inc(rel_set, 1)
            dve.wait_ge(rel_set, 1)
            dve.memset(rel_sb[BUCKETS:BUCKETS + 1, :], 1.0).then_inc(rel_set, 1)
            dve.wait_ge(v_turned, 1)
            dve.tensor_copy(v_cols[:, :], ps[:, MISC_BANK, 0:NV]).then_inc(v_done, 1)
            dve.wait_ge(rev_mm, 1)
            dve.tensor_scalar(rev_sb[:, :], ps[0:HEADS + 1, T_BANK + 1, 0:384], 1.0 / SCALE, None, ALU.mult)\
               .then_inc(rev_done, 1)
            dve.wait_ge(silu_c_done, 1)
            for p in range(8):
                add_ada(Unit("start", 0), 0, p)
            for p in range(8):
                add_ada(Unit("start", 1), 0, p)
                if p == 1:
                    sum_ada(Unit("start", 0), 0)
            sum_ada(Unit("start", 1), 0)
            for U in units(dve, "start", 2, START_CHUNKS, 2):
                if U.first % 2:
                    for p in range(8):
                        add_ada(U, 0, p)
                        if p == 1:
                            sum_ada(before(U), 0)
                    sum_ada(U, 0)
                else:
                    for p in range(8):
                        add_ada(U, 0, p)

            def fresh_gate_up(f, n, shift, scale, mods, prev):
                U = Unit(f"gu{f}", 0)
                lo(U, 0)
                lo(U, 1)
                prev()
                lo(U, 2)
                lo(U, 3)
                make_scale(n, scale, mods)
                norm_x(n)
                rounds(n, [0, 1], shift)
                for j in range(RING, KD):
                    if j % 2 == 0:
                        rounds(n, [j // 2], shift)
                    lo(U, j)
                    if f == 0 and j < 12:
                        add_ada(U, 0, j - 4)

            def gate_up_unit(f, U):
                for j in range(KD):
                    lo(U, j)
                    if j == 1:
                        product(f, before(U))
                    if j == 3:
                        actT_low(f, before(U))
                        if f == 0:
                            sum_ada(before(U), 0)
                    if f == 0 and 4 <= j < 12:
                        add_ada(U, 0, j - 4)

            def down_unit(f, U):
                L = STAGES[U.stage][1]
                for j in range(L):
                    lo(U, j)
                    if j == 1:
                        if U.first == 0:
                            product(f, Unit(f"gu{f}", FF // CW - 1))
                        else:
                            residual(before(U), gate_b, L)
                    if j == 3:
                        if U.first == 0:
                            actT_low(f, Unit(f"gu{f}", FF // CW - 1))
                        if f == 0:
                            if U.first == 0:
                                sum_ada(Unit("gu0", FF // CW - 1), 0)
                            else:
                                sum_ada(before(U), 1)
                    if U.first == 0 and j in (6, 8, 10, 12):
                        gate_diag(2 * f, (j - 6) // 2, 2 + 6 * f)
                    if f == 0 and 4 <= j < 20:
                        add_ada(U, (j - 4) // 8, (j - 4) % 8)
                    if f == 0 and j == 17:
                        sum_ada(U, 0)

            fresh_gate_up(0, "ffn1", 0, 1, START_CHUNKS, lambda: None)
            for U in units(dve, "gu0", 1, FF // CW):
                gate_up_unit(0, U)
            down_unit(0, Unit("dn0", 0))
            for U in units(dve, "dn0", 1, D // CW):
                down_unit(0, U)

            U = Unit("win", 0)
            lo(U, 0)
            lo(U, 1)
            residual(Unit("dn0", D // CW - 1), gate_b, KF // 2)
            lo(U, 2)
            lo(U, 3)
            make_scale("mix", 4, 20)
            norm_x("mix")
            rounds("mix", [0, 1, 2, 3], 3)
            for p in range(RING):
                add_ada(U, 0, p)
            sum_ada(Unit("dn0", D // CW - 1), 1)
            for j in range(RING, 8):
                rounds("mix", [j], 3)
                lo(U, j)
                add_ada(U, 0, j)
            for U in units(dve, "win", 1, STAGES["win"][0] - 1, 2):
                for j in range(8):
                    lo(U, j)
                    add_ada(U, 0, j)
                    if j == 3:
                        sum_ada(before(U), 0)
            U = Unit("win", STAGES["win"][0] - 1)
            for j in range(8):
                lo(U, j)
                if j == 3:
                    sum_ada(before(U), 0)

            for j in range(STAGES["uq"][1]):
                lo(Unit("uq", 0), j)
            rstd("mla", [(0, TT, Q_RANK), (TT, 2 * TT, KV_RANK)])
            for i, (c0, w) in enumerate(((C_Q, Q_RANK), (C_KV, KV_RANK))):
                for t in range(TT):
                    at = proj[:, t, c0:c0 + w]
                    dve.tensor_scalar(at, at, stat[:, 5, 2 * i + t:2 * i + t + 1], None, ALU.mult)\
                       .then_inc(nrm["mla"]["xn_done"], 1)
            rounds("mla", [0, 1, 2], None, cqT)
            rounds("mla", [3, 4], None, ckvT, 6)
            for stage in ("uq", "ukv"):
                for u in range(STAGES[stage][0]):
                    if stage == "ukv" or u > 0:
                        for j in range(STAGES[stage][1]):
                            lo(Unit(stage, u), j)
            for j in range(RING):
                lo(Unit("wout", 0), j)

            dve.wait_ge(A["gates_exp"], 1)
            then_wait(dve.tensor_scalar(gates[:, :, :], gates[:, :, :], 1.0, None, ALU.add))
            dve.reciprocal(gates[:, :, :], gates[:, :, :]).then_inc(A["gates_done"], 1)

            def copy_qr(u):
                if u < HEADS:
                    dve.wait_ge(A["q_turned"], u + 1)
                    if u >= 2:
                        dve.wait_ge(A["scored"], u - 1)
                    dve.tensor_copy(qrT[:, u % 2, :], ps[0:ROPE, T_BANK + 1, 0:SEQ]).then_inc(A["qr_copied"], 1)

            def maxima(u):
                dve.wait_ge(A["scored"], u + 1)
                if u == 0:
                    dve.wait_ge(A["bias_landed"], 16)
                if u >= 2:
                    dve.wait_ge(A["p_turned"], u - 1)
                h = HEADS if u < HEADS else (u - HEADS) // 2
                for t in range(TT):
                    sl = slice(t * P, t * P + (t + 1) * P)
                    dve.tensor_tensor_reduce(probs[:, u % 2, sl], ps[:, 2 + u % 2, sl], bias[:, h, (1 - t) * P:SEQ],
                                             1.0, -3e38, ALU.add, ALU.max, row_max[:, u, t:t + 1])\
                       .then_inc(A["maxed"], 1)
                dve.wait_ge(A["maxed"], 2 * u + 2)
                dve.tensor_scalar(neg_max[:, u, :], row_max[:, u, :], -SCALE, None, ALU.mult).then_inc(A["neg_done"], 1)

            def outputs(u):
                dve.wait_ge(A["exped"], 2 * u + 2)
                then_wait(dve.reciprocal(coef[:, u, :], row_sum[:, u, :]))
                h = u if u < HEADS else (u - HEADS) // 2
                if u == HEADS:
                    dve.wait_ge(A["gates_done"], 1)
                if u >= HEADS:
                    then_wait(dve.tensor_tensor(coef[:, u, :], coef[:, u, :], gates[:, :, 3 * h + 1 + u % 2], ALU.mult))
                dve.wait_ge(A["pv_done"], u + 1)
                o = o_mla if u < HEADS else o_nsa
                for t in range(TT):
                    dst, src = o[:, t, h * VD:(h + 1) * VD], ps[:, u % 2, t * P:(t + 1) * P]
                    if u < HEADS or u % 2 == 0:
                        ins = dve.tensor_scalar(dst, src, coef[:, u, t:t + 1], None, ALU.mult)
                    else:
                        dve.wait_ge(A["o_done"], 2 * u)
                        ins = dve.scalar_tensor_tensor(dst, src, coef[:, u, t:t + 1], dst, ALU.mult, ALU.add)
                    ins.then_inc(A["o_done"], 1)

            def attend(lo_, hi_):
                for s in range(lo_, hi_ + 3):
                    if s < hi_:
                        copy_qr(s)
                    if lo_ <= s - 1 < hi_:
                        maxima(s - 1)
                    if lo_ <= s - 3 < hi_:
                        outputs(s - 3)

            attend(0, HEADS)

            for r in range(3):
                dve.wait_ge(A["k_turned"], r + 1)
                dve.tensor_copy(kT64[:, 2 * r:2 * r + 2, :].rearrange("p k n -> p (k n)"), ps[0:ROPE, T_BANK + 1, :])\
                   .then_inc(A["kT_copied"], 1)
            dve.wait_ge(A["pe_turned"], 1)
            for i, rows in enumerate((P, ROPE, P)):
                ins = dve.tensor_copy(peT[0:rows, i, :], ps[0:rows, 3, 32 * i:32 * i + 32])
            then_wait(ins)
            dve.wait_ge(A["kT_copied"], 6)
            dve.wait_ge(A["v_turned_c"], 1)
            for i, (rows, dst, src) in enumerate(((P, kpe128, lambda g: kT128[:, g, :]), (ROPE, kpe64, lambda g: kT64[:, g, :]),
                                                  (P, vpe, lambda g: ps[:, 2, g * SEQ:(g + 1) * SEQ]))):
                for g in range(GROUPS):
                    for a in range(2):
                        ls = slice(16 * a, 16 * a + 16)
                        blocks = src(g)[:, 16 * a:16 * a + 16 * N_CMP].rearrange("p (n b) -> p b n", b=16)
                        dve.tensor_tensor(dst[:, ls, g * N_CMP:(g + 1) * N_CMP], blocks,
                                          peT[0:rows, i, ls].unsqueeze(2).broadcast_to([rows, 16, N_CMP]), ALU.add)\
                           .then_inc(A["kpe_done"], 1)
            then_wait(dve.memset(v_cmp[:, :, :], 0.0))
            n = GROUPS * N_CMP
            dve.wait_ge(A["hid_turned"], 1)
            dve.tensor_copy(hidT[:, :, :], ps[:, 2, 0:P].rearrange("p (i n) -> p i n", n=32)[:, :, 0:n])\
               .then_inc(A["hidT_copied"], 1)
            dve.wait_ge(A["kc_mm"], 1)
            dve.tensor_copy(kc128[:, :], ps[:, 3, 0:n]).then_inc(A["kc_copied"], 1)
            dve.tensor_copy(kc64[:, :], ps[0:ROPE, 3, 32:32 + n]).then_inc(A["kc_copied"], 1)
            dve.wait_ge(A["kc_mm"], 2)
            for g in range(GROUPS):
                for h in range(HPG):
                    rows, cols = slice(32 * h, 32 * h + N_CMP), slice(h * VD, (h + 1) * VD)
                    dve.tensor_copy(v_cmp[rows, g, cols], ps[rows, T_BANK + g, cols]).then_inc(A["vc_copied"], 1)
            attend(HEADS, 3 * HEADS)

            dve.wait_ge(A["p_turned"], 3 * HEADS)
            then_wait(dve.memset(probs[:, :, :], 0.0))
            dve.wait_ge(A["cmp_scored"], HEADS)
            for t in range(TT):
                nv = CMP_IN_REACH[t]
                pc = probs[:, t, 0:SEQ].rearrange("p (h n) -> p h n", n=32)[:, :, 0:nv]
                first = (1 - t) * P + CMP_LEN - 1
                then_wait(dve.tensor_tensor(pc, ps[:, 5, t * SEQ:(t + 1) * SEQ].rearrange("p (h n) -> p h n", n=32)[:, :, 0:nv],
                                            bias[:, 0:HEADS, first:first + CMP_STRIDE * (nv - 1) + 1:CMP_STRIDE], ALU.add))
                m = cmp_stat[:, t, 0:HEADS]
                then_wait(dve.tensor_reduce(m, pc, AX.X, ALU.max))
                then_wait(dve.tensor_scalar(m, m, 0.1 * MASKED, None, ALU.max))
                dve.tensor_tensor(pc, pc, m.unsqueeze(2).broadcast_to([P, HEADS, nv]), ALU.subtract)\
                   .then_inc(A["cmp_ready"], 1)
            for t in range(TT):
                dve.wait_ge(A["cmp_exped"], t + 1)
                pc = probs[:, t, 0:SEQ].rearrange("p (h n) -> p h n", n=32)[:, :, 0:CMP_IN_REACH[t]]
                s = cmp_stat[:, 2 + t, 0:HEADS]
                then_wait(dve.tensor_reduce(s, pc, AX.X, ALU.add))
                then_wait(dve.tensor_scalar(s, s, 1e-30, None, ALU.max))
                then_wait(dve.reciprocal(s, s))
                then_wait(dve.tensor_tensor(s, s, gates[:, t, :].rearrange("p (h b) -> p h b", b=3)[:, :, 0], ALU.mult))
            dve.wait_ge(A["o_done"], 6 * HEADS)
            for t in range(TT):
                for h in range(HEADS):
                    if h % HPG == 0:
                        dve.wait_ge(A["cmp_pv"], 2 * t + h // HPG + 1)
                    dst = o_nsa[:, t, h * VD:(h + 1) * VD]
                    dve.scalar_tensor_tensor(dst, ps[:, 2 * t + h // HPG, h % HPG * VD:(h % HPG + 1) * VD],
                                             cmp_stat[:, 2 + t, h:h + 1], dst, ALU.mult, ALU.add)\
                       .then_inc(A["cmp_o"], 1)

            T = (hT_hi, hT_lo)
            for r in range(4):
                round_lo("o", r, T, 2 * r)
            gate_diag(1, 0, 5)
            U = Unit("wout", 0)
            for j in range(RING, 8):
                round_lo("o", j, T, 2 * j)
                lo(U, j)
                if j < 7:
                    gate_diag(1, j - 3, 5)
            gate2 = kv_mla[:, 0, :]
            for U in units(dve, "wout", 1, D // CW):
                for j in range(8):
                    lo(U, j)
                    if j == 1:
                        residual(before(U), gate2, 8)

            fresh_gate_up(1, "ffn2", 6, 7, ADA_CHUNKS, lambda: residual(Unit("wout", D // CW - 1), gate2, 8))
            for U in units(dve, "gu1", 1, FF // CW):
                gate_up_unit(1, U)
            down_unit(1, Unit("dn1", 0))
            for U in units(dve, "dn1", 1, D // CW):
                down_unit(1, U)
            residual(Unit("dn1", D // CW - 1), gate_b, KF // 2)

            rstd("final", [(0, TT, D)])
            dve.wait_ge(final_b_landed, 16)
            for t in range(TT):
                for h in range(2):
                    sl = slice(h * D // 2, (h + 1) * D // 2)
                    dve.scalar_tensor_tensor(x_sb[:, t, sl], x_sb[:, t, sl], stat[:, 5, t:t + 1], final_b[:, sl],
                                             ALU.mult, ALU.mult).then_inc(final_done, 1)


_INS = ["x", "c", "w_ada", "b_ada", "norm_ffn1", "w1_gate", "w1_up", "w1_down", "norm_mix", "w_in",
        "mla_q_norm", "w_uq", "mla_kv_norm", "w_ukv", "pe_cmp_k", "w_cmp_k1", "w_cmp_k2", "pe_cmp_v",
        "w_cmp_v1", "w_cmp_v2", "rel_bias", "w_out", "norm_ffn2", "w2_gate", "w2_up", "w2_down",
        "norm_final"]
_OUTS = [((1, SEQ, D), "float32")]


def kernel(**inputs):
    import numpy as _np
    import concourse.bacc as _bacc
    from concourse import mybir as _mybir
    from concourse.bass_utils import run_bass_kernel_spmd as _run

    nc = _bacc.Bacc("TRN2", target_bir_lowering=False, num_devices=1, dynamic_dma_scratch_size=1024)
    arrays, args = {}, []
    for name in _INS:
        a = _np.ascontiguousarray(inputs[name])
        arrays[f"in_{name}_dram"] = a
        args.append(nc.dram_tensor(f"in_{name}_dram", a.shape, _mybir.dt.from_np(a.dtype), kind="ExternalInput").ap())
    for i, (shape, dtype) in enumerate(_OUTS):
        dt = _mybir.dt.from_np(_np.dtype(dtype))
        args.append(nc.dram_tensor(f"out_{i}_dram", shape, dt, kind="ExternalOutput").ap())
    decoder_layer(nc, *args)
    r = _run(nc, [arrays], core_ids=[0])
    got = tuple(r.results[0][f"out_{i}_dram"] for i in range(len(_OUTS)))
    return got[0]
```

```python
from contextlib import ExitStack

import numpy as np

import concourse.bass as bass
from concourse import mybir

P = 128
F32 = mybir.dt.float32
F32R = mybir.dt.float32r
ALU = mybir.AluOpType
ACT = mybir.ActivationFunctionType
AX = mybir.AxisListType

D, SEQ, FF = 2048, 256, 5632
TT = SEQ // P
KD = D // P
KF = FF // P
CW = 512
Q_RANK, KV_RANK, ROPE, NOPE, VD = 768, 512, 64, 128, 128
HEADS = 8
DK = NOPE + ROPE
GROUPS, HPG = 2, 4
CMP_LEN, CMP_STRIDE, CMP_HID = 32, 16, 256
N_CMP = (SEQ - CMP_LEN) // CMP_STRIDE + 1
BUCKETS, MAX_DIST = 32, 128
EPS = 1e-6
SCALE = float(DK) ** -0.5
MASKED = -1e30
CMP_IN_REACH = [min(N_CMP, ((t + 1) * P - CMP_LEN) // CMP_STRIDE + 1) for t in range(TT)]
C_Q, C_KV, C_KR = 0, Q_RANK, Q_RANK + KV_RANK
C_NQ = C_KR + ROPE
C_NK = C_NQ + HEADS * DK
C_NV = C_NK + 3 * GROUPS * DK
C_NG = C_NV + 3 * GROUPS * VD
D_IN = C_NG + HEADS * 3
LAST_W = D_IN - (D_IN // CW) * CW

RING = 4
ADA_CHUNKS = 9 * D // CW
START_CHUNKS = 8
START_STEPS = KD // 2 + 1
CMP_PANELS = 24
STAGES = {"gu0": (FF // CW, KD), "dn0": (D // CW, KF // 2), "win": (D_IN // CW + 1, KD // 2),
          "uq": (HEADS * DK // CW, Q_RANK // P // 2), "ukv": (HEADS * 2 * P // CW, KV_RANK // P // 2),
          "wout": (D // CW, KD // 2), "gu1": (FF // CW, KD), "dn1": (D // CW, KF // 2)}


def slot_of(stage, j, last):
    if stage in ("uq", "ukv"):
        return min(range(RING), key=lambda s: last[s])
    panels = STAGES[stage][1]
    whole = panels // RING * RING
    if panels == whole:
        return j % RING
    return j % RING if j < whole - RING else (j - whole + RING) % (RING - 1)


def count_panels():
    table, uses, last, n = {}, [0] * RING, [None] * RING, 0
    for stage, (units, panels) in STAGES.items():
        for u in range(units):
            for j in range(panels):
                s = slot_of(stage, j, last)
                uses[s] += 1
                table[stage, u, j] = (n, uses[s], last[s], s)
                last[s] = n
                n += 1
    return table


def count_chunks():
    of = {("start", u): [(u, u % 2)] for u in range(START_CHUNKS)}
    where = ([("gu0", u, [0]) for u in range(STAGES["gu0"][0])] + [("dn0", u, [0, 1]) for u in range(4)]
             + [("win", u, [0]) for u in (1, 3, 5, 7)] + [("late", 0, [1])]
             + [("gu1", u, [0]) for u in range(1, 5)])
    q = START_CHUNKS
    for stage, u, accs in where:
        of[stage, u] = [(q + e, a) for e, a in enumerate(accs)]
        q += len(accs)
    assert q == ADA_CHUNKS
    before, steps, uses, last, step = {}, {}, [0, 0], [None, None], 0
    for (stage, _), chunks in of.items():
        for q, a in chunks:
            before[q] = (uses[a], q - 1 if stage in ("win", "late", "gu1") else last[a])
            uses[a] += 1
            last[a] = q
            steps[q] = step
            step += START_STEPS if stage == "start" else KD
    steps[ADA_CHUNKS] = step
    return of, before, steps


PANELS = count_panels()
ADA_OF, ADA_BEFORE, ADA_STEPS = count_chunks()
LATE = ADA_OF["late", 0][0][0]


class Unit:

    def __init__(self, stage, first, i=None, step=1, times=1):
        self.stage, self.first, self.i, self.step, self.times = stage, first, i, step, times

    def at(self, f):
        v = [f(self.first + r * self.step) for r in range(self.times)]
        if self.i is None or self.times == 1:
            return v[0]
        by = v[1] - v[0]
        assert all(b - a == by for a, b in zip(v, v[1:])), (self.stage, v)
        return self.i * by + v[0]

    def done(self, j):
        return self.at(lambda u: PANELS[self.stage, u, j][0] + 1)

    def slot(self, j):
        return PANELS[self.stage, self.first, j][3]

    def landed(self, j):
        return self.at(lambda u: 16 * PANELS[self.stage, u, j][1])

    def slot_free(self, j):
        if PANELS[self.stage, self.first, j][2] is None:
            return None
        return self.at(lambda u: PANELS[self.stage, u, j][2] + 1)


def units(eng, stage, first, last, step=1):
    times = (last - first) // step
    assert times * step == last - first
    with eng.Fori(0, times) as i:
        for e in range(step):
            yield Unit(stage, first + e, i, step, times)


def before(U):
    return Unit(U.stage, U.first - 1, U.i, U.step, U.times)


def part(U, ring, s):
    if U.stage == "win" and U.first == STAGES["win"][0] - 1:
        return ring[:, s, :].rearrange("p (k n) -> p k n", k=2)[:, :, 0:LAST_W]
    return ring[:, s, :]


def bucket_table():
    dist = SEQ - 1 - np.arange(384)
    n = np.maximum(dist, 0)
    exact = BUCKETS // 2
    nf = np.maximum(n, 1).astype(np.float32)
    large = exact + (np.log(nf / np.float32(exact)) / np.float32(np.log(MAX_DIST / exact))
                     * np.float32(BUCKETS - exact)).astype(np.int32)
    bucket = np.where(n < exact, n, np.minimum(large, BUCKETS - 1))
    table = np.zeros((BUCKETS + 1, 384), np.float32)
    table[bucket, np.arange(384)] = 1.0
    table[:, dist < 0] = 0.0
    table[BUCKETS, dist < 0] = MASKED
    return table


def rope_table():
    inv = np.float32(10000.0) ** (-np.arange(0, ROPE, 2, dtype=np.float32) / np.float32(ROPE))
    ang = np.arange(SEQ, dtype=np.float32)[:, None] * inv[None, :]
    both = np.stack([np.cos(ang), np.sin(ang)], 1).astype(np.float32)
    return np.ascontiguousarray(both.reshape(TT, P, 2, ROPE // 2).transpose(1, 0, 2, 3))


def decoder_layer(nc, x, c, w_ada, b_ada, norm_ffn1, w1_gate, w1_up, w1_down, norm_mix, w_in,
                  mla_q_norm, w_uq, mla_kv_norm, w_ukv, pe_cmp_k, w_cmp_k1, w_cmp_k2, pe_cmp_v,
                  w_cmp_v1, w_cmp_v2, rel_bias, w_out, norm_ffn2, w2_gate, w2_up, w2_down,
                  norm_final, out):
    ident_c = nc.inline_tensor(np.eye(P, dtype=np.float32), name="identity").ap()
    bucket_c = nc.inline_tensor(bucket_table(), name="bucket_one_hot").ap()
    rope_c = nc.inline_tensor(rope_table(), name="rope_cos_sin").ap()
    bias_scratch = nc.dram_tensor("bias_by_distance", (HEADS + 1, P, 384), F32, kind="Internal")

    def tiles(w):
        return w.rearrange("(k p) n -> p k n", p=P)

    gate_w = [tiles(w1_gate[0]), tiles(w2_gate[0])]
    up_w = [tiles(w1_up[0]), tiles(w2_up[0])]
    down_w = [tiles(w1_down[0]), tiles(w2_down[0])]
    w_in_t, w_uq_t, w_ukv_t, w_out_t = tiles(w_in[0]), tiles(w_uq[0]), tiles(w_ukv[0]), tiles(w_out[0])
    w_ada_t = tiles(w_ada[0])
    x_t = x[0].rearrange("(t p) n -> p t n", p=P)
    out_t = out[0].rearrange("(t p) n -> p t n", p=P)

    with ExitStack() as ctx:
        def sb(name, shape, dt=F32, within=ctx):
            return within.enter_context(nc.sbuf_tensor(name, shape, dt))

        def sem(name):
            return ctx.enter_context(nc.semaphore(name))

        ident = sb("ident", [P, P])
        ones = sb("ones", [P, P])
        x_sb = sb("x_sb", [P, TT, D])
        raw = sb("raw", [P, RING, 2 * CW])
        w_hi = sb("w_hi", [P, RING, 2 * CW], F32R)
        w_lo = sb("w_lo", [P, RING, 2 * CW], F32R)
        ada_raw = sb("ada_raw", [P, RING, 2 * CW])
        mod_cols = sb("mod_cols", [P, 9 * KD])
        VROWS = {"ffn1": 0, "mix": 16, "ffn2": 32, "q": 48, "kv": 54, "c": 58}
        NV = 58 + KD
        v_cols = sb("v_cols", [P, NV])
        silu_c = sb("silu_c", [P, KD])
        scale_cols = sb("scale_cols", [P, KD])
        stat = sb("stat", [P, 6, 4])
        norm_tmp = sb("norm_tmp", [P, 2, CW])
        with ExitStack() as s:
            acc = sb("ada_acc", [P, 2, CW], within=s)
            b_row = sb("b_row", [P, 2, CW], within=s)
        with ExitStack() as s:
            rope_tmp = sb("rope_tmp", [P, 4, HEADS // 2 * ROPE // 2], within=s)
        with ExitStack() as s:
            probsT = sb("probsT", [P, 2, 3 * P], within=s)
        small_hold = sb("small_hold", [P, 4, CW])
        with ExitStack() as s:
            act_sg = sb("silu_gate", [P, TT, CW], within=s)
        with ExitStack() as s:
            probs = sb("probs", [P, 2, 3 * P], within=s)
        sg_hold = sb("sg_hold", [P, TT, CW])
        with ExitStack() as s:
            hT_hi = sb("hT_hi", [P, KD, SEQ], F32R, within=s)
            hT_lo = sb("hT_lo", [P, KD, SEQ], F32R, within=s)
        with ExitStack() as s:
            gate_b = sb("gate_b", [P, D], within=s)
            final_b = sb("final_b", [P, D], within=s)
        with ExitStack() as s:
            cqT = [sb(f"cqT_{n}", [P, 6, SEQ], F32R, within=s) for n in ("hi", "lo")]
            ckvT = [sb(f"ckvT_{n}", [P, 4, SEQ], F32R, within=s) for n in ("hi", "lo")]
            bias = sb("bias_toeplitz", [P, HEADS + 1, SEQ], within=s)
            krT = sb("krT", [ROPE, SEQ], within=s)
            rope_sb = sb("rope_sb", [P, TT, 2, ROPE // 2], within=s)
            row_max = sb("row_max", [P, 24, 2], within=s)
            neg_max = sb("neg_max", [P, 24, 2], within=s)
            row_sum = sb("row_sum", [P, 24, 2], within=s)
        h_hold = sb("h_hold", [P, 2 * KD * SEQ])
        with ExitStack() as s:
            act_hi = sb("actT_hi", [P, KF, SEQ], F32R, within=s)
            act_lo = sb("actT_lo", [P, KF, SEQ], F32R, within=s)
        with ExitStack() as s:
            diag_r = sb("diag_rstd", [P, TT, P], within=s)
            bucket_sb = sb("bucket_sb", [BUCKETS + 1, 384], within=s)
            rel_sb = sb("rel_sb", [BUCKETS + 1, HEADS + 1], within=s)
            rev_sb = sb("rev_sb", [HEADS + 1, 384], within=s)
            v_rows = sb("v_rows", [NV, P], within=s)
        with ExitStack() as s:
            proj = sb("proj", [P, TT, D_IN], within=s)
            q_mla = sb("q_mla", [P, TT, HEADS * DK], within=s)
            kT128 = sb("kT128", [P, 6, SEQ], within=s)
            kT64 = sb("kT64", [ROPE, 6, SEQ], within=s)
            v_cmp = sb("v_cmp", [P, GROUPS, HPG * VD], within=s)
            kc128 = sb("kc128", [P, GROUPS * N_CMP], within=s)
            kc64 = sb("kc64", [ROPE, GROUPS * N_CMP], within=s)
            with ExitStack() as s2:
                kpe128 = sb("kpe128", [P, CMP_LEN, GROUPS * N_CMP], within=s2)
                kpe64 = sb("kpe64", [ROPE, CMP_LEN, GROUPS * N_CMP], within=s2)
                vpe = sb("vpe", [P, CMP_LEN, GROUPS * N_CMP], within=s2)
            kv_mla = sb("kv_mla", [P, TT, HEADS * 2 * P], within=s)
            with ExitStack() as s2:
                hid = sb("hid", [GROUPS * N_CMP, 2, CMP_HID], within=s2)
                hidT = sb("hidT", [P, 4, GROUPS * N_CMP], within=s2)
                w2v = sb("w2v", [P, 2, VD], within=s2)
                peT = sb("peT", [P, 3, CMP_LEN], within=s2)
                w2k = sb("w2k", [P, 2, DK], within=s2)
            qkT = sb("qkT", [P, 2, 2 * SEQ], within=s)
            qrT = sb("qrT", [ROPE, 2, SEQ], within=s)
        a_hold = sb("a_hold", [P, 2 * KF * SEQ])
        gates = sb("gates", [P, TT, HEADS * 3])
        coef = sb("coef", [P, 24, 2])
        cmp_stat = sb("cmp_stat", [P, 4, HEADS * TT])
        pe_sb = sb("pe_sb", [CMP_LEN, DK + VD])
        x_sq = sb("x_sq", [P, TT, D // CW])
        cmp_p = norm_tmp
        o_nsa, o_mla = proj[:, :, 0:HEADS * VD], q_mla[:, :, 0:HEADS * VD]
        cmp_pT = kT128[:, 0:2, :]
        NSA = 2 * HEADS

        ps = ctx.enter_context(nc.psum_tensor("ps", [P, 8, CW], F32))
        T_BANK, ADA_BANK, MISC_BANK = 4, 6, 7

        raw_landed = [sem(f"raw_landed{s}") for s in range(RING)]
        hi_done, lo_done, mm_done = sem("hi_done"), sem("lo_done"), sem("mm_done")
        ada_landed = [sem(f"ada_landed{s}") for s in range(RING)]
        b_landed = [sem(f"b_landed{s}") for s in range(2)]
        acc_step = sem("acc_step")
        acc_turned, mod_done = sem("acc_turned"), sem("mod_done")
        const_landed, x_landed, rel_landed = sem("const_landed"), sem("x_landed"), sem("rel_landed")
        rel_set = sem("rel_set")
        ones_set, rows_set = sem("ones_set"), sem("rows_set")
        v_turned, v_done, silu_c_done = sem("v_turned"), sem("v_done"), sem("silu_c_done")
        rev_mm, rev_done, rev_stored = sem("rev_mm"), sem("rev_done"), sem("rev_stored")
        dve_step, pool_step = sem("dve_step"), sem("pool_step")
        gu = [{n: sem(f"{n}{f}") for n in ("silu_done", "prod_done", "prod_turned", "actT_hi_done",
                                          "actT_lo_done")} for f in range(2)]
        nrm = {n: {m: sem(f"{m}_{n}") for m in ("squares", "mean", "root", "xn_done", "turned", "tmp_done",
                                               "T_hi_done", "T_lo_done")}
               for n in ("ffn1", "mix", "ffn2", "mla", "o", "final")}
        gat = [{n: sem(f"{n}{f}") for n in ("diag_done", "gate_mm", "gate_b_done")} for f in range(3)]
        res = {n: {m: sem(f"{m}_{n}") for m in ("bank_read", "x_added")} for n in ("dn0", "wout", "dn1")}
        copied = {n: sem(f"copied_{n}") for n in ("win", "uq", "ukv")}
        A = {n: sem(n) for n in ("bias_landed", "kr_turned", "kr_copied",
                                 "q_turned", "qk_copied", "qr_copied", "scored", "maxed", "neg_done", "exped",
                                 "p_turned", "pT_copied", "pv_done", "o_done",
                                 "k_turned", "kT_copied", "v_turned_c", "pe_turned", "cmp_read",
                                 "kpe_done", "cw_used", "hid_done", "hid_turned", "hidT_copied",
                                 "kc_mm", "kc_copied", "vc_copied", "gates_exp",
                                 "gates_done", "cmp_scored", "cmp_ready", "cmp_exped",
                                 "cmp_turned", "cmp_copied", "cmp_pv", "cmp_o", "cmp_w_landed",
                                 "rope_landed")}
        final_done, final_b_landed, stored = sem("final_done"), sem("final_b_landed"), sem("stored")
        NORM_OF = {"gu0": "ffn1", "win": "mix", "gu1": "ffn2", "wout": "o"}
        ada_after = {"gu0": 4, "dn0": 4, "win": 0, "gu1": 4}
        NBANKS = {"ffn1": 2, "mix": 3, "ffn2": 2, "mla": 2, "o": 3}
        ada_by_pe = sem("ada_by_pe")

        def ada_use(q, p):
            return 2 * q + p // RING + 1 + (CMP_PANELS // RING if q >= LATE else 0)

        def ada_steps(U, e, n):
            return U.at(lambda u: ADA_STEPS[ADA_OF[U.stage, u][e][0]] + n)

        block = ctx.enter_context(nc.Block())

        @block.sync
        def _(sp):
            def load(U, j, src, width=CW):
                free = U.slot_free(j)
                if free is not None:
                    sp.wait_ge(lo_done, free)
                dst = raw[:, U.slot(j), :].rearrange("p (k n) -> p k n", k=2)[:, :, 0:width]
                sp.dma_start(dst, src).then_inc(raw_landed[U.slot(j)], 16)

            def columns(w, k, U, width=CW):
                return w[:, k:k + 2, bass.ds(U.at(lambda u: u * CW), width)]

            def load_ada(U, e, p):
                q = U.at(lambda u: ADA_OF[U.stage, u][e][0])
                _, a = ADA_OF[U.stage, U.first][e]
                q0 = ADA_OF[U.stage, U.first][e][0]
                if p == 0:
                    if ADA_BEFORE[q0][1] is not None:
                        sp.wait_ge(acc_step, U.at(lambda u: ADA_STEPS[ADA_BEFORE[ADA_OF[U.stage, u][e][0]][1]] + 1))
                    else:
                        sp.wait_ge(rows_set, 1)
                    sp.dma_start(b_row[0:1, a, :], b_ada[0:1, bass.ds(q * CW, CW)]).then_inc(b_landed[a], 16)
                if U.stage == "start":
                    r = U.at(lambda u: u)
                    if p % 2:
                        if U.first > 0 or p >= RING:
                            sp.wait_ge(ada_by_pe, r * 4 + (p - RING + 1) // 2)
                    elif U.first > 0 or p >= RING:
                        sp.wait_ge(acc_step, r * START_STEPS + (p - RING + 2 if p >= RING else p - RING + 1))
                elif q0 == START_CHUNKS and p < RING:
                    if p % 2:
                        sp.wait_ge(ada_by_pe, 4 * START_CHUNKS)
                    else:
                        sp.wait_ge(acc_step, ADA_STEPS[START_CHUNKS])
                elif q0 == LATE and p < RING:
                    sp.wait_ge(A["cw_used"], CMP_PANELS - RING + p + 1)
                else:
                    sp.wait_ge(acc_step, ada_steps(U, e, 2 * (p - RING + 1)))
                sp.dma_start(ada_raw[:, p % RING, :].rearrange("p (k n) -> p k n", k=2),
                             w_ada_t[:, 2 * p:2 * p + 2, bass.ds(q * CW, CW)]).then_inc(ada_landed[p % RING], 16)

            def load_unit(U, panel):
                chunks = ADA_OF.get((U.stage, U.first), [])
                for j in range(STAGES[U.stage][1]):
                    p = j - ada_after.get(U.stage, 0)
                    if 0 <= p < 8 * len(chunks):
                        load_ada(U, p // 8, p % 8)
                    panel(U, j)

            def gate_up(f):
                def panel(U, j):
                    load(U, j, columns((gate_w, up_w)[j % 2][f], j // 2 * 2, U))
                return panel

            def rows_of(w, width=CW):
                return lambda U, j: load(U, j, columns(w, 2 * j, U, width), width)

            first = Unit("gu0", 0)
            load_ada(Unit("start", 0), 0, 0)
            for p in range(1, RING):
                load_ada(Unit("start", 0), 0, p)
            for j in range(RING):
                gate_up(0)(first, j)
            for p in range(RING, 8):
                load_ada(Unit("start", 0), 0, p)
            for p in range(8):
                load_ada(Unit("start", 1), 0, p)
            for U in units(sp, "start", 2, START_CHUNKS, 2):
                for p in range(8):
                    load_ada(U, 0, p)

            for j in range(RING, STAGES["gu0"][1]):
                p = j - ada_after["gu0"]
                if 0 <= p < 8:
                    load_ada(first, 0, p)
                gate_up(0)(first, j)
            for U in units(sp, "gu0", 1, STAGES["gu0"][0]):
                load_unit(U, gate_up(0))
            load_unit(Unit("dn0", 0), rows_of(down_w[0]))
            for U in units(sp, "dn0", 1, STAGES["dn0"][0]):
                load_unit(U, rows_of(down_w[0]))
            load_unit(Unit("win", 0), rows_of(w_in_t))
            for U in units(sp, "win", 1, STAGES["win"][0] - 1, 2):
                load_unit(U, rows_of(w_in_t))
            load_unit(Unit("win", STAGES["win"][0] - 1), rows_of(w_in_t, LAST_W))
            sp.wait_ge(copied["win"], 1)
            sp.dma_start(w2k[:, :, :], tiles(w_cmp_k2[0])).then_inc(A["cmp_w_landed"], 16)
            sp.dma_start(w2v[:, :, :], tiles(w_cmp_v2[0])).then_inc(A["cmp_w_landed"], 16)
            small = [(Unit(stage, u), j, w) for stage, w in (("uq", w_uq_t), ("ukv", w_ukv_t))
                     for u in range(STAGES[stage][0]) for j in range(STAGES[stage][1])]
            for U, j, w in small[:RING]:
                rows_of(w)(U, j)
            k1 = w_cmp_k1[0].rearrange("(l d) n -> d l n", d=DK)
            v1 = w_cmp_v1[0].rearrange("(l d) n -> d l n", d=VD)
            for m in range(CMP_PANELS):
                l0 = m % 8 * 4
                if m < RING:
                    sp.wait_ge(acc_step, ADA_STEPS[LATE])
                else:
                    sp.wait_ge(A["cw_used"], m - RING + 1)
                rows, src = [(P, k1[0:P]), (ROPE, k1[P:DK]), (P, v1)][m // 8]
                sp.dma_start(ada_raw[0:rows, m % RING, :].rearrange("p (l n) -> p l n", l=4),
                             src[:, l0:l0 + 4, :]).then_inc(ada_landed[m % RING], 16)
                if m == RING:
                    sp.wait_ge(mm_done, Unit("win", STAGES["win"][0] - 1).done(KD // 2 - 1))
                    sp.dma_start(rope_sb[:, :, :, :], rope_c).then_inc(A["rope_landed"], 16)
                    sp.wait_ge(rev_stored, 16)
                    sp.dma_start(bias[:, :, :], bass.AP(tensor=bias_scratch, offset=P - 1,
                                                        ap=[[383, P], [P * 384, HEADS + 1], [1, SEQ]]))\
                        .then_inc(A["bias_landed"], 16)
            late = Unit("late", 0)
            for i, (U, j, w) in enumerate(small[RING:]):
                rows_of(w)(U, j)
                if i < 8:
                    load_ada(late, 0, i)

            def out_rows(U, j):
                load(U, j, columns(w_out_t, (2 * j + HEADS) % KD, U))

            load_unit(Unit("wout", 0), out_rows)
            for U in units(sp, "wout", 1, STAGES["wout"][0]):
                load_unit(U, out_rows)
            load_unit(Unit("gu1", 0), gate_up(1))
            for a, b in ((1, 5), (5, STAGES["gu1"][0])):
                for U in units(sp, "gu1", a, b):
                    load_unit(U, gate_up(1))
            load_unit(Unit("dn1", 0), rows_of(down_w[1]))
            sp.wait_ge(gat[2]["gate_b_done"], 4)
            sp.dma_start(final_b[:, :], norm_final.rearrange("(a n) -> a n", a=1).broadcast_to([P, D]))\
                .then_inc(final_b_landed, 16)
            for U in units(sp, "dn1", 1, STAGES["dn1"][0]):
                load_unit(U, rows_of(down_w[1]))
            for t in range(TT):
                for h in range(2):
                    sp.wait_ge(final_done, 2 * t + h + 1)
                    sl = slice(h * D // 2, (h + 1) * D // 2)
                    sp.dma_start(out_t[:, t, sl], x_sb[:, t, sl]).then_inc(stored, 16)
            sp.wait_ge(stored, 16 * 2 * TT)

        @block.gpsimd
        def _(pool):
            pool.memset(b_row[:, :, :], 0.0).then_inc(rows_set, 1)
            pool.memset(ones[:, :], 1.0).then_inc(ones_set, 1)

            n_step = 0

            def rotate(t1, t2, cos, sin, tmp):
                nonlocal n_step
                for o, a, b in ((0, t1, cos), (1, t2, sin), (2, t1, sin), (3, t2, cos)):
                    pool.tensor_tensor(tmp[o], a, b, ALU.mult).then_inc(pool_step, 1)
                n_step += 4
                pool.wait_ge(pool_step, n_step)
                pool.tensor_tensor(t1, tmp[0], tmp[1], ALU.subtract).then_inc(pool_step, 1)
                pool.tensor_tensor(t2, tmp[2], tmp[3], ALU.add).then_inc(pool_step, 1)
                n_step += 2
                pool.wait_ge(pool_step, n_step)

            def round_lo(n, r, T, k):
                pool.wait_ge(nrm[n]["T_hi_done"], r + 1)
                pool.tensor_tensor(T[1][:, k:k + 2, :].rearrange("p k n -> p (k n)"), norm_tmp[:, r % 2, :],
                                   T[0][:, k:k + 2, :].rearrange("p k n -> p (k n)").bitcast(F32), ALU.subtract)\
                    .then_inc(nrm[n]["T_lo_done"], 1)

            for n in ("ffn1", "mix"):
                for r in range(KD // 2):
                    round_lo(n, r, (hT_hi, hT_lo), 2 * r)
            for r in range(5):
                round_lo("mla", r, cqT if r < 3 else ckvT, 2 * r if r < 3 else 2 * r - 6)

            half, hh = ROPE // 2, HEADS // 2
            pool.wait_ge(A["rope_landed"], 16)
            pool.wait_ge(mod_done, LATE)
            for t in range(TT):
                kr = proj[:, t, C_KR:C_KR + ROPE]
                rotate(kr[:, 0:half], kr[:, half:ROPE], rope_sb[:, t, 0, :], rope_sb[:, t, 1, :],
                       [rope_tmp[:, o, 0:half] for o in range(4)])
            pool.wait_ge(copied["uq"], 2 * STAGES["uq"][0])
            for t in range(TT):
                for h0 in (0, hh):
                    qr = q_mla[:, t, h0 * DK:(h0 + hh) * DK].rearrange("p (h d) -> p h d", h=hh)
                    cos, sin = (rope_sb[:, t, o, :].unsqueeze(1).broadcast_to([P, hh, half]) for o in range(2))
                    rotate(qr[:, :, NOPE:NOPE + half], qr[:, :, NOPE + half:DK], cos, sin,
                           [rope_tmp[:, o, :].rearrange("p (h d) -> p h d", h=hh) for o in range(4)])
            for r in range(KD // 2):
                round_lo("ffn2", r, (hT_hi, hT_lo), 2 * r)

        @block.tensor
        def _(pe):
            def three(bank, lhs_hi, lhs_lo, rhs_hi, rhs_lo, start, stop):
                pe.matmul(bank, lhs_hi, rhs_hi, start=start, stop=False)
                pe.matmul(bank, lhs_hi, rhs_lo, start=False, stop=False)
                return pe.matmul(bank, lhs_lo, rhs_hi, start=False, stop=stop)

            def panel(U, j, T, k, bank, first, last, width=CW, tile_ready=None):
                pe.wait_ge(lo_done, U.done(j))
                s = U.slot(j)
                for t in range(TT):
                    if tile_ready is not None:
                        tile_ready(t)
                    for kk in range(2):
                        mm = three(ps[:, bank + t, 0:width], T[0][:, k + kk, t * P:(t + 1) * P],
                                   T[1][:, k + kk, t * P:(t + 1) * P],
                                   w_hi[:, s, kk * CW:kk * CW + width], w_lo[:, s, kk * CW:kk * CW + width],
                                   first and kk == 0, last and kk == 1)
                mm.then_inc(mm_done, 1)

            def turn_ada(U, e):
                q = U.at(lambda u: ADA_OF[U.stage, u][e][0])
                a = ADA_OF[U.stage, U.first][e][1]
                pe.wait_ge(acc_step, ada_steps(U, e, START_STEPS if U.stage == "start" else KD))
                if not (U.stage == "start" and U.first == 0):
                    pe.wait_ge(mod_done, q)
                for b in range(4):
                    mm = pe.transpose(ps[:, ADA_BANK, b * P:(b + 1) * P], acc[:, a, b * P:(b + 1) * P], ident[:, :])
                mm.then_inc(acc_turned, 1)

            def start_ada(U, prev):
                q = U.at(lambda u: u)
                bank = 2 + U.first % 2
                for p in (1, 3, 5, 7):
                    pe.wait_ge(ada_landed[p % RING], q * 32 + 16 * (p // RING + 1))
                    for kk in range(2):
                        k = 2 * p + kk
                        mm = pe.matmul(ps[0:1, bank, :], silu_c[:, k:k + 1], ada_raw[:, p % RING, kk * CW:(kk + 1) * CW],
                                       start=k == 2, stop=k == KD - 1)
                    mm.then_inc(ada_by_pe, 1)
                    if p == 1 and prev is not None:
                        turn_ada(prev, 0)

            def turn_norm(n, r, src):
                nb = NBANKS[n]
                if r >= nb:
                    pe.wait_ge(nrm[n]["T_lo_done" if n == "o" else "tmp_done"], r - nb + 1)
                for kk in range(2):
                    for t in range(TT):
                        dst = ps[:, T_BANK + r % nb, (kk * TT + t) * P:(kk * TT + t + 1) * P]
                        if src is None:
                            k = 2 * r + kk
                            mm = pe.matmul(dst, x_sb[:, t, k * P:(k + 1) * P], diag_r[:, t, :], start=True, stop=True)
                        else:
                            mm = pe.transpose(dst, src(2 * r + kk, t), ident[:, :])
                mm.then_inc(nrm[n]["turned"], 1)

            def rounds_ahead(n, r, src=None):
                ahead = r + NBANKS[n] - 1
                if r >= 1 and ahead < KD // 2:
                    turn_norm(n, ahead, src)

            def turn_products(f, U):
                pe.wait_ge(gu[f]["prod_done"], U.at(lambda u: 2 * u + 2))
                for b in range(2):
                    for kk in range(2):
                        for t in range(TT):
                            mm = pe.transpose(ps[:, T_BANK + b, (kk * TT + t) * P:(kk * TT + t + 1) * P],
                                              act_sg[:, t, (2 * b + kk) * P:(2 * b + kk + 1) * P], ident[:, :])
                    mm.then_inc(gu[f]["prod_turned"], 1)

            def gate_up_unit(f, U, fresh):
                prev = None if U.first == 0 else before(U)
                for j in range(KD):
                    if fresh:
                        r = j // 2
                        if j % 2 == 0:
                            rounds_ahead(NORM_OF[U.stage], r)
                            pe.wait_ge(nrm[NORM_OF[U.stage]]["T_lo_done"], r + 1)
                    elif j == 0:
                        pe.wait_ge(gu[f]["silu_done"], U.at(lambda u: 2 * u))
                    elif j == 1:
                        pe.wait_ge(gu[f]["prod_done"], U.at(lambda u: 2 * u))
                    panel(U, j, (hT_hi, hT_lo), j // 2 * 2, 2 * (j % 2), j < 2, j >= KD - 2)
                    if j == 13 and (U.stage, U.first) in ADA_OF:
                        turn_ada(U, 0)
                    if not fresh and j == 1:
                        turn_products(f, prev)

            def gate_broadcast(f, c):
                pe.wait_ge(gat[f]["diag_done"], c + 1)
                if c > 0:
                    pe.wait_ge(gat[f]["gate_b_done"], c)
                pe.matmul(ps[:, MISC_BANK, :], ones[:, :], norm_tmp[:, c % 2, :], start=True, stop=True).then_inc(gat[f]["gate_mm"], 1)

            def down_unit(f, U):
                stage, L = U.stage, STAGES[U.stage][1]
                done = res[stage]["bank_read"]
                for j in range(L):
                    if j == L - 2 and U.first == 0:
                        pe.wait_ge(gu[f]["actT_lo_done"], 2 * (FF // CW))

                    def tile_ready(t):
                        if j == 0 and U.first > 0:
                            pe.wait_ge(done, U.at(lambda u: 2 * (u - 1) + t + 1))
                        elif j == 0:
                            pe.wait_ge(gu[f]["silu_done"], 2 * (FF // CW))
                    panel(U, j, (act_hi, act_lo), 2 * j, 0, j == 0, j == L - 1, tile_ready=tile_ready)
                    if j == 20 and f == 0:
                        turn_ada(U, 1)
                    if j == 1 and U.first == 0:
                        turn_products(f, Unit(f"gu{f}", FF // CW - 1))
                    if j == 14 and f == 0:
                        turn_ada(U, 0)
                    if U.first == 0 and j in (8, 10, 12, 14):
                        gate_broadcast(2 * f, (j - 8) // 2)

            pe.wait_ge(const_landed, 16 * 10)
            pe.transpose(ps[:, MISC_BANK, 0:NV], v_rows[:, :], ident[0:NV, 0:NV]).then_inc(v_turned, 1)
            pe.wait_ge(rel_landed, 16)
            pe.wait_ge(ones_set, 1)
            pe.matmul(ps[0:HEADS + 1, T_BANK + 1, 0:384], rel_sb[:, :], bucket_sb[:, :], start=True, stop=True)\
                .then_inc(rev_mm, 1)
            pe.wait_ge(silu_c_done, 1)
            start_ada(Unit("start", 0), None)
            start_ada(Unit("start", 1), Unit("start", 0))
            for U in units(pe, "start", 2, START_CHUNKS, 2):
                start_ada(U, before(U))
            turn_ada(Unit("start", START_CHUNKS - 1), 0)

            def first_rounds(n, src=None):
                if src is None:
                    pe.wait_ge(nrm[n]["xn_done"], 1)
                for r in range(NBANKS[n]):
                    turn_norm(n, r, src)

            pe.wait_ge(rev_done, 1)
            first_rounds("ffn1")
            gate_up_unit(0, Unit("gu0", 0), True)
            for U in units(pe, "gu0", 1, FF // CW):
                gate_up_unit(0, U, False)
            down_unit(0, Unit("dn0", 0))
            for U in units(pe, "dn0", 1, D // CW):
                down_unit(0, U)

            def project_in(U, width=CW):
                L = STAGES["win"][1]
                for j in range(L):
                    def tile_ready(t):
                        if j == 0 and U.first > 0:
                            pe.wait_ge(copied["win"], U.at(lambda u: 2 * (u - 1) + t + 1))
                        elif j == 0:
                            pe.wait_ge(res["dn0"]["bank_read"], 2 * (D // CW))
                    if U.first == 0:
                        rounds_ahead("mix", j)
                        pe.wait_ge(nrm["mix"]["T_lo_done"], j + 1)
                    panel(U, j, (hT_hi, hT_lo), 2 * j, 0, j == 0, j == L - 1, width, tile_ready)
                    if j == 0 and U.first > 0 and U.first % 2 == 0:
                        turn_ada(before(U), 0)

            first_rounds("mix")
            project_in(Unit("win", 0))
            for U in units(pe, "win", 1, STAGES["win"][0] - 1, 2):
                project_in(U)
            project_in(Unit("win", STAGES["win"][0] - 1), LAST_W)

            pe.wait_ge(copied["win"], 2 * (C_NV // CW + 1))
            pe.wait_ge(nrm["mix"]["tmp_done"], KD // 2)
            for r in range(3):
                if r > 0:
                    pe.wait_ge(A["kT_copied"], 2 * r)
                for i in range(2):
                    for t in range(TT):
                        k0 = C_NK + (2 * r + i) * DK
                        cols = slice(i * SEQ + t * P, i * SEQ + (t + 1) * P)
                        pe.transpose(ps[:, T_BANK, cols], proj[:, t, k0:k0 + P], ident[:, :])
                        mm = pe.transpose(ps[0:ROPE, T_BANK + 1, cols], proj[:, t, k0 + P:k0 + DK], ident[:, :])
                mm.then_inc(A["k_turned"], 1)
            id32 = ident[0:CMP_LEN, 0:CMP_LEN]
            pe.transpose(ps[:, 3, 0:32], pe_sb[:, 0:P], id32)
            pe.transpose(ps[0:ROPE, 3, 32:64], pe_sb[:, P:DK], id32)
            pe.transpose(ps[:, 3, 64:96], pe_sb[:, DK:DK + VD], id32).then_inc(A["pe_turned"], 1)
            pe.wait_ge(copied["win"], 2 * STAGES["win"][0])
            for g in range(GROUPS):
                for t in range(TT):
                    mm = pe.transpose(ps[:, 2, g * SEQ + t * P:g * SEQ + (t + 1) * P],
                                      proj[:, t, C_NV + g * VD:C_NV + (g + 1) * VD], ident[:, :])
            mm.then_inc(A["v_turned_c"], 1)
            pe.wait_ge(mod_done, LATE)
            for m in range(CMP_PANELS):
                which, l0 = m // 8, m % 8 * 4
                if m % 8 == 0:
                    pe.wait_ge(A["kpe_done"], (4, 8, 12)[which])
                pe.wait_ge(ada_landed[m % RING], 16 * (2 * LATE + m // RING + 1))
                blocks, rows = ((kpe128, P), (kpe64, ROPE), (vpe, P))[which]
                for l in range(4):
                    mm = pe.matmul(ps[0:GROUPS * N_CMP, 6 + which // 2, 0:CMP_HID], blocks[:, l0 + l, :],
                                   ada_raw[0:rows, m % RING, l * CMP_HID:(l + 1) * CMP_HID],
                                   start=m in (0, 16) and l == 0, stop=m in (15, 23) and l == 3)
                mm.then_inc(A["cw_used"], 1)
                if m % 3 == 2 and m >= 8 and m < 23:
                    r = (m - 8) // 3
                    if r == 0:
                        pe.wait_ge(A["kT_copied"], 6)
                        pe.wait_ge(nrm["mla"]["xn_done"], 4)
                    c0 = C_Q if r < 3 else C_KV - 6 * P
                    turn_norm("mla", r, lambda k, t: proj[:, t, c0 + k * P:c0 + (k + 1) * P])

            n = GROUPS * N_CMP

            def turn_hidden():
                pe.wait_ge(nrm["mla"]["tmp_done"], 5)
                pe.wait_ge(A["hid_done"], 2)
                for i in range(4):
                    mm = pe.transpose(ps[:, 4, i * 32:i * 32 + n], hid[:, i // 2, i % 2 * P:(i % 2 + 1) * P],
                                      ident[0:n, 0:n])
                mm.then_inc(A["hid_turned"], 1)

            def compressed_keys():
                pe.wait_ge(A["hidT_copied"], 1)
                pe.wait_ge(A["cmp_w_landed"], 32)
                for rows, c0 in ((P, 0), (ROPE, P)):
                    for i in range(2):
                        mm = pe.matmul(ps[0:rows, 5, c0 // 4:c0 // 4 + n], w2k[:, i, c0:c0 + rows], hidT[:, i, :],
                                       start=i == 0, stop=i == 1)
                mm.then_inc(A["kc_mm"], 1)

            def compressed_values():
                for g in range(GROUPS):
                    for h in range(HPG):
                        for i in range(2):
                            mm = pe.matmul(ps[32 * h:32 * h + N_CMP, 6 + g, h * VD:(h + 1) * VD],
                                           hidT[:, 2 + i, g * N_CMP:(g + 1) * N_CMP], w2v[:, i, :],
                                           start=i == 0, stop=i == 1)
                mm.then_inc(A["kc_mm"], 1)

            between_units = {("uq", 0): turn_hidden, ("uq", 1): compressed_keys, ("uq", 2): compressed_values}
            for stage, T, n0 in (("uq", cqT, 0), ("ukv", ckvT, 3)):
                for u in range(STAGES[stage][0]):
                    L = STAGES[stage][1]
                    b = 2 * ((u + (stage == "ukv")) % 2)

                    def tile_ready(t):
                        if u >= 2:
                            pe.wait_ge(copied[stage], 2 * (u - 2) + t + 1)
                        elif stage == "ukv":
                            pe.wait_ge(copied["uq"], 2 * (u + 1) + t + 1)
                        elif u == 1:
                            pe.wait_ge(A["kpe_done"], 12)
                    for j in range(L):
                        if u == 0:
                            pe.wait_ge(nrm["mla"]["T_lo_done"], n0 + j + 1)
                        panel(Unit(stage, u), j, T, 2 * j, b, j == 0, j == L - 1,
                              tile_ready=tile_ready if j == 0 else None)
                    if (stage, u) in between_units:
                        between_units[stage, u]()
            turn_ada(Unit("late", 0), 0)
            pe.wait_ge(pool_step, 6 * TT)
            pe.wait_ge(A["hidT_copied"], 1)
            for t in range(TT):
                mm = pe.transpose(ps[0:ROPE, T_BANK, t * P:(t + 1) * P], proj[:, t, C_KR:C_KR + ROPE], ident[:, :])
            mm.then_inc(A["kr_turned"], 1)
            pe.wait_ge(A["kc_copied"], 2)
            pe.wait_ge(A["vc_copied"], 2 * HPG)

            def turn_q(u):
                nsa = u < NSA
                if nsa and u % 2:
                    return
                h = u // 2 if nsa else u - NSA
                e = h if nsa else HEADS + h
                if e == 0:
                    pe.wait_ge(A["kr_copied"], 1)
                else:
                    pe.wait_ge(A["qk_copied"], e)
                if e == HEADS:
                    pe.wait_ge(A["cmp_read"], TT)
                    pe.wait_ge(pool_step, 18 * TT)
                elif e > HEADS:
                    pe.wait_ge(A["qr_copied"], h)
                for t in range(TT):
                    cols = slice(t * P, (t + 1) * P)
                    cols2 = slice(SEQ + t * P, SEQ + (t + 1) * P)
                    if nsa:
                        q0 = C_NQ + h * DK
                        pe.transpose(ps[:, T_BANK, cols], proj[:, t, q0:q0 + NOPE], ident[:, :])
                        mm = pe.transpose(ps[0:ROPE, T_BANK, cols2], proj[:, t, q0 + NOPE:q0 + DK], ident[:, :])
                    else:
                        pe.transpose(ps[:, T_BANK, cols], q_mla[:, t, h * DK:h * DK + NOPE], ident[:, :])
                        pe.transpose(ps[:, T_BANK, cols2], kv_mla[:, t, h * 2 * P:h * 2 * P + P], ident[:, :])
                        mm = pe.transpose(ps[0:ROPE, T_BANK + 1, cols], q_mla[:, t, h * DK + NOPE:(h + 1) * DK],
                                          ident[:, :])
                mm.then_inc(A["q_turned"], 1)

            def score(u):
                nsa = u < NSA
                h = u // 2 if nsa else u - NSA
                e = h if nsa else HEADS + h
                b = e % 2
                pe.wait_ge(A["qk_copied"], e + 1)
                if not nsa:
                    pe.wait_ge(A["qr_copied"], h + 1)
                if u >= 2:
                    pe.wait_ge(A["maxed"], 2 * (u - 1))
                else:
                    pe.wait_ge(copied["ukv"], 2 * STAGES["ukv"][0])
                kx = (1 + u % 2) * GROUPS + h // HPG
                for t in range(TT):
                    w = (t + 1) * P
                    dst = ps[:, 2 + u % 2, t * P:t * P + w]
                    pe.matmul(dst, qkT[:, b, t * P:(t + 1) * P],
                              kT128[:, kx, 0:w] if nsa else qkT[:, b, SEQ:SEQ + w], start=True, stop=False)
                    mm = pe.matmul(dst, qrT[:, b, t * P:(t + 1) * P],
                                   kT64[:, kx, 0:w] if nsa else krT[:, 0:w], start=False, stop=True)
                mm.then_inc(A["scored"], 1)
                if nsa and u % 2 == 0:
                    g = h // HPG
                    for t in range(TT):
                        dst = ps[:, 5, t * SEQ + h * 32:t * SEQ + h * 32 + N_CMP]
                        pe.matmul(dst, qkT[:, b, t * P:(t + 1) * P], kc128[:, g * N_CMP:(g + 1) * N_CMP],
                                  start=True, stop=False)
                        mm = pe.matmul(dst, qrT[:, b, t * P:(t + 1) * P], kc64[:, g * N_CMP:(g + 1) * N_CMP],
                                       start=False, stop=True)
                    mm.then_inc(A["cmp_scored"], 1)

            def turn_p(u):
                pe.wait_ge(A["exped"], 2 * (u + 1))
                if u >= 2:
                    pe.wait_ge(A["pT_copied"], u - 1)
                elif u == 0:
                    pe.wait_ge(mod_done, LATE + 1)
                for b in range(3):
                    mm = pe.transpose(ps[:, 6 + u % 2, b * P:(b + 1) * P], probs[:, u % 2, b * P:(b + 1) * P],
                                      ident[:, :])
                mm.then_inc(A["p_turned"], 1)

            def times_v(u):
                pe.wait_ge(A["pT_copied"], u + 1)
                if u >= 2:
                    pe.wait_ge(A["o_done"], 2 * (u - 1))
                for t in range(TT):
                    for kt in range(t + 1):
                        if u >= NSA:
                            v = kv_mla[:, kt, (u - NSA) * 2 * P + P:(u - NSA + 1) * 2 * P]
                        else:
                            kx = (1 + u % 2) * GROUPS + u // 2 // HPG
                            v = proj[:, kt, C_NV + kx * VD:C_NV + (kx + 1) * VD]
                        mm = pe.matmul(ps[:, u % 2, t * P:(t + 1) * P], probsT[:, u % 2, (t + kt) * P:(t + kt + 1) * P],
                                       v, start=kt == 0, stop=kt == t)
                mm.then_inc(A["pv_done"], 1)

            def turn_cmp():
                pe.wait_ge(A["qk_copied"], 2 * HEADS)
                pe.wait_ge(A["qr_copied"], HEADS)
                for t in range(TT):
                    pe.wait_ge(A["cmp_exped"], t + 1)
                    for g in range(GROUPS):
                        mm = pe.transpose(ps[:, T_BANK + t, g * P:(g + 1) * P], cmp_p[:, t, g * P:(g + 1) * P],
                                          ident[:, :])
                    mm.then_inc(A["cmp_turned"], 1)

            def cmp_times_v(t):
                if t == 0:
                    pe.wait_ge(A["maxed"], 2 * (NSA + HEADS))
                    pe.wait_ge(A["cmp_copied"], TT)
                for g in range(GROUPS):
                    pe.matmul(ps[:, 2 + 2 * t + g, :], cmp_pT[:, t, g * P:(g + 1) * P], v_cmp[:, g, :],
                              start=True, stop=True).then_inc(A["cmp_pv"], 1)

            last = NSA + HEADS
            for s in range(last + 3):
                if s < last:
                    turn_q(s)
                if s == last:
                    turn_cmp()
                if 0 <= s - 1 < last:
                    score(s - 1)
                if 0 <= s - 2 < last:
                    turn_p(s - 2)
                if s > last:
                    cmp_times_v(s - last - 1)
                if 0 <= s - 3 < last:
                    times_v(s - 3)

            def o_tile(k, t):
                return (o_nsa if k < HEADS else o_mla)[:, t, k % HEADS * VD:(k % HEADS + 1) * VD]

            def project_out(U):
                L = STAGES["wout"][1]
                for j in range(L):
                    def tile_ready(t):
                        if j == 0 and U.first > 0:
                            pe.wait_ge(res["wout"]["bank_read"], U.at(lambda u: 2 * (u - 1) + t + 1))
                        elif j == 0:
                            pe.wait_ge(A["o_done"], 2 * last)
                    if U.first == 0:
                        rounds_ahead("o", j, o_tile)
                        pe.wait_ge(nrm["o"]["T_lo_done"], j + 1)
                        if 2 <= j <= 5:
                            gate_broadcast(1, j - 2)
                    panel(U, j, (hT_hi, hT_lo), 2 * j, 0, j == 0, j == L - 1, CW, tile_ready)

            pe.wait_ge(A["pT_copied"], last)
            pe.wait_ge(A["o_done"], 2 * last)
            pe.wait_ge(A["cmp_o"], 2 * HEADS)
            first_rounds("o", o_tile)
            project_out(Unit("wout", 0))
            for U in units(pe, "wout", 1, STAGES["wout"][0]):
                project_out(U)

            first_rounds("ffn2")
            pe.wait_ge(res["wout"]["bank_read"], 2 * (D // CW))
            gate_up_unit(1, Unit("gu1", 0), True)
            for a, b in ((1, 5), (5, FF // CW)):
                for U in units(pe, "gu1", a, b):
                    gate_up_unit(1, U, False)
            down_unit(1, Unit("dn1", 0))
            for U in units(pe, "dn1", 1, D // CW):
                down_unit(1, U)

        @block.scalar
        def _(act):
            def hi(U, j):
                s = U.slot(j)
                act.wait_ge(raw_landed[s], U.landed(j))
                free = U.slot_free(j)
                if free is not None:
                    act.wait_ge(mm_done, free)
                act.activation(part(U, w_hi, s), part(U, raw, s), ACT.Copy).then_inc(hi_done, 1)

            def silu(f, U):
                act.wait_ge(mm_done, U.done(KD - 2))
                for t in range(TT):
                    act.activation(act_sg[:, t, :], ps[:, t, :], ACT.Silu).then_inc(gu[f]["silu_done"], 1)

            def actT(f, U):
                for b in range(2):
                    act.wait_ge(gu[f]["prod_turned"], U.at(lambda u: 2 * u + b + 1))
                    at = U.at(lambda u: (4 * u + 2 * b) * SEQ)
                    act.activation(act_hi[:, :, :].rearrange("p k n -> p (k n)")[:, bass.ds(at, CW)],
                                   ps[:, T_BANK + b, :], ACT.Copy).then_inc(gu[f]["actT_hi_done"], 1)

            def load_root_table():
                act.activation(stat[:, 5, 3:4], ones[:, 0:1], ACT.Sqrt)

            def root(n, w):
                act.wait_ge(nrm[n]["mean"], 1)
                act.activation(stat[:, 2, 0:w], stat[:, 1, 0:w], ACT.Sqrt).then_inc(nrm[n]["root"], 1)

            def x_squares(n, added, U):
                if added is not None:
                    act.wait_ge(added, U.at(lambda u: 2 * u + 2))
                c0 = U.at(lambda u: u * CW)
                for t in range(TT):
                    act.activation(norm_tmp[:, t, :], x_sb[:, t, bass.ds(c0, CW)], ACT.Square,
                                   accum_out=x_sq[:, t, bass.ds(U.at(lambda u: u), 1)]).then_inc(nrm[n]["squares"], 1)
                act.wait_ge(nrm[n]["squares"], U.at(lambda u: 2 * u + 2))

            def round_hi(n, r, T, k):
                if n == "o":
                    act.wait_ge(nrm[n]["turned"], r + 1)
                    src = ps[:, T_BANK + r % NBANKS[n], :]
                else:
                    act.wait_ge(nrm[n]["tmp_done"], r + 1)
                    src = norm_tmp[:, r % 2, :]
                act.activation(T[:, k:k + 2, :].rearrange("p k n -> p (k n)"), src, ACT.Copy)\
                   .then_inc(nrm[n]["T_hi_done"], 1)

            def gate_copy(f, c, dst, factor):
                act.wait_ge(gat[f]["gate_mm"], c + 1)
                act.activation(dst[:, c * CW:(c + 1) * CW], ps[:, MISC_BANK, :], ACT.Copy, scale=factor)\
                   .then_inc(gat[f]["gate_b_done"], 1)

            def copy_out(stage, U, dst, bank, width=CW):
                act.wait_ge(mm_done, U.done(STAGES[stage][1] - 1))
                at = U.at(lambda u: u * CW)
                for t in range(TT):
                    act.activation(dst[:, t, bass.ds(at, width)], ps[:, bank + t, 0:width], ACT.Copy)\
                       .then_inc(copied[stage], 1)

            dma = act.dma_start
            dma(ident[:, :], ident_c).then_inc(const_landed, 16)
            for name, v in (("ffn1", norm_ffn1), ("mix", norm_mix), ("ffn2", norm_ffn2), ("q", mla_q_norm),
                            ("kv", mla_kv_norm), ("c", c)):
                n = v.shape[1] // P
                dma(v_rows[VROWS[name]:VROWS[name] + n, :], v[0].rearrange("(k p) -> k p", p=P))\
                    .then_inc(const_landed, 16)
            dma(bucket_sb[:, :], bucket_c).then_inc(const_landed, 16)
            dma(pe_sb[:, 0:DK], pe_cmp_k[0]).then_inc(const_landed, 16)
            dma(pe_sb[:, DK:DK + VD], pe_cmp_v[0]).then_inc(const_landed, 16)
            dma(x_sb[:, :, :], x_t).then_inc(x_landed, 16)
            act.wait_ge(rel_set, 2)
            dma(rel_sb[0:BUCKETS, 0:HEADS], rel_bias).then_inc(rel_landed, 16)
            act.wait_ge(v_done, 1)
            act.activation(silu_c[:, :], v_cols[:, VROWS["c"]:NV], ACT.Silu).then_inc(silu_c_done, 1)
            act.wait_ge(rev_done, 1)
            dma(bias_scratch.ap(), rev_sb[:, :].unsqueeze(1).broadcast_to([HEADS + 1, P, 384]))\
                .then_inc(rev_stored, 16)

            def fresh_unit(n, U, per, added, last_chunk):
                hi(U, 0)
                hi(U, 1)
                load_root_table()
                x_squares(n, added, last_chunk)
                root(n, TT)
                round_hi(n, 0, hT_hi, 0)
                round_hi(n, 1, hT_hi, 2)
                for j in range(2, STAGES[U.stage][1]):
                    if j % per == 0 and j // per >= 2:
                        round_hi(n, j // per, hT_hi, j // per * 2)
                    hi(U, j)

            def gate_up_unit(f, U):
                for j in range(KD):
                    hi(U, j)
                    if j == 1:
                        silu(f, before(U))
                    if j == 3:
                        actT(f, before(U))

            def down_unit(f, U):
                for j in range(STAGES[U.stage][1]):
                    hi(U, j)
                    if U.first == 0:
                        if j == 1:
                            silu(f, Unit(f"gu{f}", FF // CW - 1))
                        if j == 3:
                            actT(f, Unit(f"gu{f}", FF // CW - 1))
                        if j in (10, 12, 14, 16):
                            gate_copy(2 * f, (j - 10) // 2, gate_b, 0.5)
                    elif j == 3:
                        x_squares(("mix", "final")[f], res[U.stage]["x_added"], before(U))

            act.wait_ge(x_landed, 16)
            for u in range(D // CW - 1):
                x_squares("ffn1", None, Unit("dn0", u))
            fresh_unit("ffn1", Unit("gu0", 0), 2, None, Unit("dn0", D // CW - 1))
            act.wait_ge(rev_stored, 16)
            for U in units(act, "gu0", 1, FF // CW):
                gate_up_unit(0, U)
            down_unit(0, Unit("dn0", 0))
            for U in units(act, "dn0", 1, D // CW):
                down_unit(0, U)

            def project_in(U):
                for j in range(STAGES["win"][1]):
                    hi(U, j)
                    if j == 1:
                        copy_out("win", before(U), proj, 0)

            fresh_unit("mix", Unit("win", 0), 1, res["dn0"]["x_added"], Unit("dn0", D // CW - 1))
            for U in units(act, "win", 1, STAGES["win"][0] - 1, 2):
                project_in(U)
            last_in = Unit("win", STAGES["win"][0] - 1)
            project_in(last_in)

            for j in range(STAGES["uq"][1]):
                hi(Unit("uq", 0), j)
            copy_out("win", last_in, proj, 0, LAST_W)
            for r in range(3):
                act.wait_ge(A["k_turned"], r + 1)
                act.activation(kT128[:, 2 * r:2 * r + 2, :].rearrange("p k n -> p (k n)"), ps[:, T_BANK, :],
                               ACT.Copy).then_inc(A["kT_copied"], 1)
            act.activation(gates[:, :, :], proj[:, :, C_NG:D_IN], ACT.Exp, scale=-1.0).then_inc(A["gates_exp"], 1)
            load_root_table()
            for i, (c0, w) in enumerate(((C_Q, Q_RANK), (C_KV, KV_RANK))):
                for t in range(TT):
                    act.activation(q_mla[:, t, c0:c0 + w], proj[:, t, c0:c0 + w], ACT.Square,
                                   accum_out=stat[:, 0, 2 * i + t:2 * i + t + 1]).then_inc(nrm["mla"]["squares"], 1)
            root("mla", 4)
            for r in range(5):
                round_hi("mla", r, cqT[0] if r < 3 else ckvT[0], 2 * r if r < 3 else 2 * r - 6)
            for i in range(2):
                act.wait_ge(A["cw_used"], (16, 24)[i])
                act.activation(hid[:, i, :], ps[0:GROUPS * N_CMP, 6 + i, 0:CMP_HID], ACT.Silu)\
                   .then_inc(A["hid_done"], 1)
            small_units = [("uq", u) for u in range(STAGES["uq"][0])] + [("ukv", u) for u in range(STAGES["ukv"][0])]

            def copy_small(i):
                stage, u = small_units[i]
                copy_out(stage, Unit(stage, u), q_mla if stage == "uq" else kv_mla, 2 * (i % 2))

            for i, (stage, u) in enumerate(small_units):
                if i > 0:
                    for j in range(STAGES[stage][1]):
                        hi(Unit(stage, u), j)
                    copy_small(i - 1)
            copy_small(len(small_units) - 1)
            for j in range(RING):
                hi(Unit("wout", 0), j)
            act.wait_ge(A["kr_turned"], 1)
            act.activation(krT[:, :], ps[0:ROPE, T_BANK, 0:SEQ], ACT.Copy).then_inc(A["kr_copied"], 1)

            def copy_q(u):
                nsa = u < NSA
                if nsa and u % 2:
                    return
                e = u // 2 if nsa else u - HEADS
                act.wait_ge(A["q_turned"], e + 1)
                if e >= 2:
                    act.wait_ge(A["scored"], 2 * e - 2 if e < HEADS + 2 else e + HEADS - 1)
                if nsa:
                    act.activation(qkT[:, e % 2, 0:SEQ], ps[:, T_BANK, 0:SEQ], ACT.Copy)
                    act.activation(qrT[:, e % 2, :], ps[0:ROPE, T_BANK, SEQ:2 * SEQ], ACT.Copy)\
                       .then_inc(A["qk_copied"], 1)
                else:
                    act.activation(qkT[:, e % 2, :], ps[:, T_BANK, :], ACT.Copy).then_inc(A["qk_copied"], 1)

            def exps(u):
                act.wait_ge(A["neg_done"], u + 1)
                for t in range(TT):
                    sl = slice(t * P, t * P + (t + 1) * P)
                    act.activation(probs[:, u % 2, sl], probs[:, u % 2, sl], ACT.Exp, bias=neg_max[:, u, t:t + 1],
                                   scale=SCALE, accum_out=row_sum[:, u, t:t + 1]).then_inc(A["exped"], 1)

            def copy_p(u):
                act.wait_ge(A["p_turned"], u + 1)
                if u >= 2:
                    act.wait_ge(A["pv_done"], u - 1)
                elif u == 0:
                    act.wait_ge(pool_step, 18 * TT)
                act.activation(probsT[:, u % 2, :], ps[:, 6 + u % 2, 0:3 * P], ACT.Copy).then_inc(A["pT_copied"], 1)

            last = NSA + HEADS
            for s in range(last + 3):
                if s < last:
                    copy_q(s)
                if 0 <= s - 1 < last:
                    exps(s - 1)
                if s == NSA + 3:
                    for t in range(TT):
                        act.wait_ge(A["cmp_ready"], t + 1)
                        pc = cmp_p[:, t, 0:SEQ].rearrange("p (h n) -> p h n", n=32)[:, :, 0:CMP_IN_REACH[t]]
                        act.activation(pc, pc, ACT.Exp, scale=SCALE).then_inc(A["cmp_exped"], 1)
                if s == last:
                    for t in range(TT):
                        act.wait_ge(A["cmp_turned"], t + 1)
                        act.activation(cmp_pT[:, t, :], ps[:, T_BANK + t, 0:SEQ], ACT.Copy).then_inc(A["cmp_copied"], 1)
                if 0 <= s - 2 < last:
                    copy_p(s - 2)

            for r in range(4):
                round_hi("o", r, hT_hi, 2 * r)
            U = Unit("wout", 0)
            for j in range(RING, STAGES["wout"][1]):
                round_hi("o", j, hT_hi, 2 * j)
                hi(U, j)
                gate_copy(1, j - RING, kv_mla[:, 0, :], 1.0)
            for U in units(act, "wout", 1, STAGES["wout"][0]):
                for j in range(STAGES["wout"][1]):
                    hi(U, j)
                    if j == 3:
                        x_squares("ffn2", res["wout"]["x_added"], before(U))

            fresh_unit("ffn2", Unit("gu1", 0), 2, res["wout"]["x_added"], Unit("wout", D // CW - 1))
            for U in units(act, "gu1", 1, FF // CW):
                gate_up_unit(1, U)
            down_unit(1, Unit("dn1", 0))
            for U in units(act, "dn1", 1, D // CW):
                down_unit(1, U)
            load_root_table()
            x_squares("final", res["dn1"]["x_added"], Unit("dn1", D // CW - 1))
            root("final", TT)

        @block.vector
        def _(dve):
            steps = 0

            def then_wait(ins):
                nonlocal steps
                steps += 1
                ins.then_inc(dve_step, 1)
                dve.wait_ge(dve_step, steps)

            def lo(U, j):
                s = U.slot(j)
                dve.wait_ge(hi_done, U.done(j))
                dve.tensor_tensor(part(U, w_lo, s), part(U, raw, s), part(U, w_hi, s).bitcast(F32), ALU.subtract)\
                   .then_inc(lo_done, 1)

            def add_ada(U, e, p):
                q = U.at(lambda u: ADA_OF[U.stage, u][e][0])
                q0, a = ADA_OF[U.stage, U.first][e]
                slot = p % RING
                dve.wait_ge(ada_landed[slot], U.at(lambda u: 16 * ada_use(ADA_OF[U.stage, u][e][0], p)))
                for kk in range(2):
                    k = 2 * p + kk
                    step = p + kk if U.stage == "start" else k
                    if k == 0:
                        dve.wait_ge(b_landed[a], U.at(lambda u: 16 * (ADA_BEFORE[ADA_OF[U.stage, u][e][0]][0] + 1)))
                        if ADA_BEFORE[q0][1] is not None:
                            dve.wait_ge(acc_turned, U.at(lambda u: ADA_BEFORE[ADA_OF[U.stage, u][e][0]][1] + 1))
                    else:
                        dve.wait_ge(acc_step, ada_steps(U, e, step))
                    dve.scalar_tensor_tensor(acc[:, a, :], ada_raw[:, slot, kk * CW:(kk + 1) * CW], silu_c[:, k:k + 1],
                                             b_row[:, a, :] if k == 0 else acc[:, a, :], ALU.mult, ALU.add)\
                       .then_inc(acc_step, 1)

            def start_chunk(U, prev):
                for p in (0, 2, 4, 6):
                    add_ada(U, 0, p)
                    if p == 2 and prev is not None:
                        sum_ada(prev, 0)
                a, q = U.first % 2, U.at(lambda u: u)
                dve.wait_ge(ada_by_pe, q * 4 + 4)
                dve.wait_ge(acc_step, ada_steps(U, 0, START_STEPS - 1))
                dve.tensor_tensor(acc[0:1, a, :], acc[0:1, a, :], ps[0:1, 2 + a, :], ALU.add).then_inc(acc_step, 1)

            def sum_ada(U, e):
                q = U.at(lambda u: ADA_OF[U.stage, u][e][0])
                dve.wait_ge(acc_turned, q + 1)
                dve.tensor_reduce(mod_cols[:, bass.ds(q * 4, 4)],
                                  ps[:, ADA_BANK, :].rearrange("p (b n) -> p b n", b=4), AX.X, ALU.add)\
                   .then_inc(mod_done, 1)

            def rstd(n, parts):
                w = parts[-1][1]
                for i, (a, b, size) in enumerate(parts):
                    ins = dve.tensor_scalar(stat[:, 1, a:b], stat[:, 0, a:b], 1.0 / size, EPS, ALU.mult, ALU.add)
                ins.then_inc(nrm[n]["mean"], 1)
                dve.wait_ge(nrm[n]["root"], 1)
                v, root, r, e, out_ = (stat[:, i, 0:w] for i in (1, 2, 3, 4, 5))
                then_wait(dve.reciprocal(r, root))
                then_wait(dve.tensor_tensor(e, r, r, ALU.mult))
                then_wait(dve.tensor_tensor(e, e, v, ALU.mult))
                then_wait(dve.tensor_scalar(e, e, -0.5, 1.5, ALU.mult, ALU.add))
                then_wait(dve.tensor_tensor(out_, r, e, ALU.mult))

            def x_rstd(n):
                dve.wait_ge(nrm[n]["squares"], 2 * (D // CW))
                then_wait(dve.tensor_reduce(stat[:, 0, 0:TT], x_sq[:, :, :], AX.X, ALU.add))
                rstd(n, [(0, TT, D)])

            def norm_x(n):
                x_rstd(n)
                for t in range(TT):
                    ins = dve.tensor_scalar(diag_r[:, t, :], ident[:, :], stat[:, 5, t:t + 1], None, ALU.mult)
                ins.then_inc(nrm[n]["xn_done"], 1)

            def make_scale(n, seg, mods):
                dve.wait_ge(mod_done, mods)
                g0 = VROWS[n]
                then_wait(dve.scalar_tensor_tensor(scale_cols[:, :], mod_cols[:, seg * KD:(seg + 1) * KD], 1.0,
                                                   v_cols[:, g0:g0 + KD], ALU.add, ALU.mult))

            def round_tmp(n, r, shift):
                dve.wait_ge(nrm[n]["turned"], r + 1)
                if r >= 2:
                    dve.wait_ge(nrm[n]["T_lo_done"], r - 1)
                for kk in range(2):
                    k = 2 * r + kk
                    dst, src = (a[:, kk * SEQ:(kk + 1) * SEQ]
                                for a in (norm_tmp[:, r % 2, :], ps[:, T_BANK + r % NBANKS[n], :]))
                    if n == "mla":
                        ins = dve.tensor_scalar(dst, src, v_cols[:, VROWS["q"] + k:VROWS["q"] + k + 1], None, ALU.mult)
                    else:
                        ins = dve.tensor_scalar(dst, src, scale_cols[:, k:k + 1],
                                                mod_cols[:, shift * KD + k:shift * KD + k + 1], ALU.mult, ALU.add)
                ins.then_inc(nrm[n]["tmp_done"], 1)

            def o_lo(r):
                dve.wait_ge(nrm["o"]["T_hi_done"], r + 1)
                dve.tensor_tensor(hT_lo[:, 2 * r:2 * r + 2, :].rearrange("p k n -> p (k n)"),
                                  ps[:, T_BANK + r % NBANKS["o"], :],
                                  hT_hi[:, 2 * r:2 * r + 2, :].rearrange("p k n -> p (k n)").bitcast(F32), ALU.subtract)\
                   .then_inc(nrm["o"]["T_lo_done"], 1)

            def product(f, U):
                dve.wait_ge(mm_done, U.done(KD - 1))
                for t in range(TT):
                    dve.wait_ge(gu[f]["silu_done"], U.at(lambda u: 2 * u + t + 1))
                    dve.tensor_tensor(act_sg[:, t, :], act_sg[:, t, :], ps[:, 2 + t, :], ALU.mult)\
                       .then_inc(gu[f]["prod_done"], 1)

            def actT_low(f, U):
                flat = [a[:, :, :].rearrange("p k n -> p (k n)") for a in (act_hi, act_lo)]
                for b in range(2):
                    dve.wait_ge(gu[f]["actT_hi_done"], U.at(lambda u: 2 * u + b + 1))
                    at = U.at(lambda u: (4 * u + 2 * b) * SEQ)
                    dve.tensor_tensor(flat[1][:, bass.ds(at, CW)], ps[:, T_BANK + b, :],
                                      flat[0][:, bass.ds(at, CW)].bitcast(F32), ALU.subtract)\
                       .then_inc(gu[f]["actT_lo_done"], 1)

            def residual(U, gate, L):
                s = res[U.stage]
                dve.wait_ge(mm_done, U.done(L - 1))
                at = U.at(lambda u: u * CW)
                for t in range(TT):
                    dve.tensor_tensor(act_sg[:, t, :], ps[:, t, :], gate[:, bass.ds(at, CW)], ALU.mult)\
                       .then_inc(s["bank_read"], 1)
                for t in range(TT):
                    dve.wait_ge(s["bank_read"], U.at(lambda u: 2 * u + t + 1))
                    xs = x_sb[:, t, bass.ds(at, CW)]
                    dve.tensor_tensor(xs, xs, act_sg[:, t, :], ALU.add).then_inc(s["x_added"], 1)
                dve.wait_ge(s["x_added"], U.at(lambda u: 2 * u + 2))

            def gate_diag(f, c, seg):
                if c >= 2:
                    dve.wait_ge(gat[f]["gate_mm"], c - 1)
                for b in range(4):
                    col = seg * KD + 4 * c + b
                    ins = dve.tensor_scalar(norm_tmp[:, c % 2, b * P:(b + 1) * P], ident[:, :],
                                            mod_cols[:, col:col + 1], None, ALU.mult)
                ins.then_inc(gat[f]["diag_done"], 1)

            dve.memset(rel_sb[:, :], 0.0).then_inc(rel_set, 1)
            dve.wait_ge(rel_set, 1)
            dve.memset(rel_sb[BUCKETS:BUCKETS + 1, :], 1.0).then_inc(rel_set, 1)
            dve.wait_ge(v_turned, 1)
            dve.tensor_copy(v_cols[:, :], ps[:, MISC_BANK, 0:NV]).then_inc(v_done, 1)
            dve.wait_ge(rev_mm, 1)
            dve.tensor_scalar(rev_sb[:, :], ps[0:HEADS + 1, T_BANK + 1, 0:384], 1.0 / SCALE, None, ALU.mult)\
               .then_inc(rev_done, 1)
            dve.wait_ge(silu_c_done, 1)
            start_chunk(Unit("start", 0), None)
            start_chunk(Unit("start", 1), Unit("start", 0))
            for U in units(dve, "start", 2, START_CHUNKS, 2):
                start_chunk(U, before(U))
            sum_ada(Unit("start", START_CHUNKS - 1), 0)

            def fresh_unit(U, n, shift, scale, mods, per, prev):
                lo(U, 0)
                lo(U, 1)
                make_scale(n, scale, mods)
                prev()
                norm_x(n)
                round_tmp(n, 0, shift)
                round_tmp(n, 1, shift)
                for j in range(2, STAGES[U.stage][1]):
                    if j % per == 0 and j // per >= 2:
                        round_tmp(n, j // per, shift)
                    lo(U, j)
                    if U.stage == "gu0":
                        ada_between(U, j)

            def ada_between(U, j):
                if (U.stage, U.first) not in ADA_OF:
                    return
                p = j - ada_after[U.stage]
                if 0 <= p < 8 * len(ADA_OF[U.stage, U.first]):
                    add_ada(U, p // 8, p % 8)
                if U.stage in ("gu0", "gu1") and j == KD - 1:
                    sum_ada(U, 0)
                if U.stage == "dn0" and j in (17, 21):
                    sum_ada(U, int(j == 21))

            def gate_up_unit(f, U):
                for j in range(KD):
                    lo(U, j)
                    if j == 1:
                        product(f, before(U))
                    if j == 3:
                        actT_low(f, before(U))
                    ada_between(U, j)

            def down_unit(f, U):
                L = STAGES[U.stage][1]
                for j in range(L):
                    lo(U, j)
                    if j == 1:
                        if U.first == 0:
                            product(f, Unit(f"gu{f}", FF // CW - 1))
                        else:
                            residual(before(U), gate_b, L)
                    if j == 3:
                        if U.first == 0:
                            actT_low(f, Unit(f"gu{f}", FF // CW - 1))
                    if U.first == 0 and j in (6, 8, 10, 12):
                        gate_diag(2 * f, (j - 6) // 2, 2 + 6 * f)
                    ada_between(U, j)

            fresh_unit(Unit("gu0", 0), "ffn1", 0, 1, START_CHUNKS, 2, lambda: None)
            for U in units(dve, "gu0", 1, FF // CW):
                gate_up_unit(0, U)
            down_unit(0, Unit("dn0", 0))
            for U in units(dve, "dn0", 1, D // CW):
                down_unit(0, U)

            fresh_unit(Unit("win", 0), "mix", 3, 4, 20, 1,
                       lambda: residual(Unit("dn0", D // CW - 1), gate_b, KF // 2))
            for U in units(dve, "win", 1, STAGES["win"][0] - 1, 2):
                for j in range(8):
                    lo(U, j)
                    ada_between(U, j)
                    if j == 3 and U.first % 2 == 0:
                        sum_ada(before(U), 0)
            U = Unit("win", STAGES["win"][0] - 1)
            for j in range(8):
                lo(U, j)

            for r in range(3):
                dve.wait_ge(A["k_turned"], r + 1)
                dve.tensor_copy(kT64[:, 2 * r:2 * r + 2, :].rearrange("p k n -> p (k n)"), ps[0:ROPE, T_BANK + 1, :])\
                   .then_inc(A["kT_copied"], 1)
            dve.wait_ge(A["pe_turned"], 1)
            for i, rows in enumerate((P, ROPE, P)):
                ins = dve.tensor_copy(peT[0:rows, i, :], ps[0:rows, 3, 32 * i:32 * i + 32])
            then_wait(ins)
            dve.wait_ge(A["kT_copied"], 6)
            for i, (rows, dst, src) in enumerate(((P, kpe128, lambda g: kT128[:, g, :]), (ROPE, kpe64, lambda g: kT64[:, g, :]),
                                                  (P, vpe, lambda g: ps[:, 2, g * SEQ:(g + 1) * SEQ]))):
                if i == 2:
                    dve.wait_ge(A["v_turned_c"], 1)
                for g in range(GROUPS):
                    for a in range(2):
                        ls = slice(16 * a, 16 * a + 16)
                        blocks = src(g)[:, 16 * a:16 * a + 16 * N_CMP].rearrange("p (n b) -> p b n", b=16)
                        dve.tensor_tensor(dst[:, ls, g * N_CMP:(g + 1) * N_CMP], blocks,
                                          peT[0:rows, i, ls].unsqueeze(2).broadcast_to([rows, 16, N_CMP]), ALU.add)\
                           .then_inc(A["kpe_done"], 1)

            dve.wait_ge(nrm["mla"]["squares"], 4)
            rstd("mla", [(0, TT, Q_RANK), (TT, 2 * TT, KV_RANK)])
            for i, (c0, w) in enumerate(((C_Q, Q_RANK), (C_KV, KV_RANK))):
                for t in range(TT):
                    at = proj[:, t, c0:c0 + w]
                    dve.tensor_scalar(at, at, stat[:, 5, 2 * i + t:2 * i + t + 1], None, ALU.mult)\
                       .then_inc(nrm["mla"]["xn_done"], 1)
            for j in range(STAGES["uq"][1]):
                lo(Unit("uq", 0), j)
            then_wait(dve.memset(v_cmp[:, :, :], 0.0))
            dve.wait_ge(A["gates_exp"], 1)
            then_wait(dve.tensor_scalar(gates[:, :, :], gates[:, :, :], 1.0, None, ALU.add))
            then_wait(dve.reciprocal(gates[:, :, :], gates[:, :, :]))
            for r in range(5):
                round_tmp("mla", r, None)

            n = GROUPS * N_CMP

            def copy_hidden():
                dve.wait_ge(A["hid_turned"], 1)
                dve.tensor_copy(hidT[:, :, :], ps[:, 4, 0:P].rearrange("p (i n) -> p i n", n=32)[:, :, 0:n])\
                   .then_inc(A["hidT_copied"], 1)

            def copy_keys():
                dve.wait_ge(A["kc_mm"], 1)
                dve.tensor_copy(kc128[:, :], ps[:, 5, 0:n]).then_inc(A["kc_copied"], 1)
                dve.tensor_copy(kc64[:, :], ps[0:ROPE, 5, 32:32 + n]).then_inc(A["kc_copied"], 1)

            def copy_values():
                dve.wait_ge(A["kc_mm"], 2)
                for g in range(GROUPS):
                    for h in range(HPG):
                        rows, cols = slice(32 * h, 32 * h + N_CMP), slice(h * VD, (h + 1) * VD)
                        dve.tensor_copy(v_cmp[rows, g, cols], ps[rows, 6 + g, cols]).then_inc(A["vc_copied"], 1)

            after_unit = {("uq", 1): copy_hidden, ("uq", 2): copy_keys, ("ukv", 0): copy_values}
            small = [(stage, u, j) for stage in ("uq", "ukv") for u in range(STAGES[stage][0])
                     for j in range(STAGES[stage][1])]
            for i, (stage, u, j) in enumerate(small[STAGES["uq"][1]:]):
                lo(Unit(stage, u), j)
                if j == STAGES[stage][1] - 1 and (stage, u) in after_unit:
                    after_unit[stage, u]()
                if 0 <= i - 2 < 8:
                    add_ada(Unit("late", 0), 0, i - 2)
            for j in range(RING):
                lo(Unit("wout", 0), j)
            sum_ada(Unit("late", 0), 0)

            def copy_qr(u):
                if u >= NSA:
                    e = u - HEADS
                    dve.wait_ge(A["q_turned"], e + 1)
                    dve.wait_ge(A["scored"], 2 * e - 2 if e < HEADS + 2 else e + HEADS - 1)
                    dve.tensor_copy(qrT[:, e % 2, :], ps[0:ROPE, T_BANK + 1, 0:SEQ]).then_inc(A["qr_copied"], 1)

            def maxima(u):
                dve.wait_ge(A["scored"], u + 1)
                if u == 0:
                    dve.wait_ge(A["bias_landed"], 16)
                if u >= 2:
                    dve.wait_ge(A["p_turned"], u - 1)
                h = u // 2 if u < NSA else HEADS
                for t in range(TT):
                    sl = slice(t * P, t * P + (t + 1) * P)
                    dve.tensor_tensor_reduce(probs[:, u % 2, sl], ps[:, 2 + u % 2, sl], bias[:, h, (1 - t) * P:SEQ],
                                             1.0, -3e38, ALU.add, ALU.max, row_max[:, u, t:t + 1])\
                       .then_inc(A["maxed"], 1)
                dve.wait_ge(A["maxed"], 2 * u + 2)
                dve.tensor_scalar(neg_max[:, u, :], row_max[:, u, :], -SCALE, None, ALU.mult).then_inc(A["neg_done"], 1)

            def outputs(u):
                nsa = u < NSA
                h = u // 2 if nsa else u - NSA
                dve.wait_ge(A["exped"], 2 * u + 2)
                then_wait(dve.reciprocal(coef[:, u, :], row_sum[:, u, :]))
                if nsa:
                    then_wait(dve.tensor_tensor(coef[:, u, :], coef[:, u, :], gates[:, :, 3 * h + 1 + u % 2], ALU.mult))
                dve.wait_ge(A["pv_done"], u + 1)
                o = o_nsa if nsa else o_mla
                for t in range(TT):
                    dst, src = o[:, t, h * VD:(h + 1) * VD], ps[:, u % 2, t * P:(t + 1) * P]
                    if nsa and u % 2:
                        dve.wait_ge(A["o_done"], 2 * u)
                        ins = dve.scalar_tensor_tensor(dst, src, coef[:, u, t:t + 1], dst, ALU.mult, ALU.add)
                    else:
                        ins = dve.tensor_scalar(dst, src, coef[:, u, t:t + 1], None, ALU.mult)
                    ins.then_inc(A["o_done"], 1)

            def cmp_view(t, a):
                return a.rearrange("p (h n) -> p h n", n=32)[:, :, 0:CMP_IN_REACH[t]]

            def cmp_logits():
                then_wait(dve.memset(cmp_p[:, :, 0:SEQ], 0.0))
                dve.wait_ge(A["cmp_scored"], HEADS)
                for t in range(TT):
                    first = (1 - t) * P + CMP_LEN - 1
                    reach = CMP_STRIDE * (CMP_IN_REACH[t] - 1) + 1
                    dve.tensor_tensor(cmp_view(t, cmp_p[:, t, 0:SEQ]), cmp_view(t, ps[:, 5, t * SEQ:(t + 1) * SEQ]),
                                      bias[:, 0:HEADS, first:first + reach:CMP_STRIDE], ALU.add)\
                       .then_inc(A["cmp_read"], 1)

            def cmp_shift(t):
                pc, m = cmp_view(t, cmp_p[:, t, 0:SEQ]), cmp_stat[:, t, 0:HEADS]
                dve.wait_ge(A["cmp_read"], t + 1)
                then_wait(dve.tensor_reduce(m, pc, AX.X, ALU.max))
                then_wait(dve.tensor_scalar(m, m, 0.1 * MASKED, None, ALU.max))
                dve.tensor_tensor(pc, pc, m.unsqueeze(2).broadcast_to([P, HEADS, CMP_IN_REACH[t]]), ALU.subtract)\
                   .then_inc(A["cmp_ready"], 1)

            def cmp_coef(t):
                s = cmp_stat[:, 2 + t, 0:HEADS]
                dve.wait_ge(A["cmp_exped"], t + 1)
                then_wait(dve.tensor_reduce(s, cmp_view(t, cmp_p[:, t, 0:SEQ]), AX.X, ALU.add))
                then_wait(dve.tensor_scalar(s, s, 1e-30, None, ALU.max))
                then_wait(dve.reciprocal(s, s))
                then_wait(dve.tensor_tensor(s, s, gates[:, t, :].rearrange("p (h b) -> p h b", b=3)[:, :, 0], ALU.mult))

            def cmp_outputs(t):
                for h in range(HEADS):
                    if h % HPG == 0:
                        dve.wait_ge(A["cmp_pv"], 2 * t + h // HPG + 1)
                    dst = o_nsa[:, t, h * VD:(h + 1) * VD]
                    dve.scalar_tensor_tensor(dst, ps[:, 2 + 2 * t + h // HPG, h % HPG * VD:(h % HPG + 1) * VD],
                                             cmp_stat[:, 2 + t, h:h + 1], dst, ALU.mult, ALU.add)\
                       .then_inc(A["cmp_o"], 1)

            last = NSA + HEADS
            for s in range(last + 3):
                if s == NSA:
                    cmp_logits()
                if s in (NSA + 1, NSA + 2):
                    cmp_shift(s - NSA - 1)
                if s in (NSA + 4, NSA + 5):
                    cmp_coef(s - NSA - 4)
                if s < last:
                    copy_qr(s)
                if 0 <= s - 1 < last:
                    maxima(s - 1)
                if s == last + 2:
                    cmp_outputs(0)
                if 0 <= s - 3 < last:
                    outputs(s - 3)
            cmp_outputs(1)

            for r in range(4):
                o_lo(r)
            gate_diag(1, 0, 5)
            U = Unit("wout", 0)
            for j in range(RING, 8):
                o_lo(j)
                lo(U, j)
                if j < 7:
                    gate_diag(1, j - 3, 5)
            gate2 = kv_mla[:, 0, :]
            for U in units(dve, "wout", 1, D // CW):
                for j in range(8):
                    lo(U, j)
                    if j == 1:
                        residual(before(U), gate2, 8)

            fresh_unit(Unit("gu1", 0), "ffn2", 6, 7, LATE + 1, 2,
                       lambda: residual(Unit("wout", D // CW - 1), gate2, 8))
            for a, b in ((1, 5), (5, FF // CW)):
                for U in units(dve, "gu1", a, b):
                    gate_up_unit(1, U)
            down_unit(1, Unit("dn1", 0))
            for U in units(dve, "dn1", 1, D // CW):
                down_unit(1, U)
            residual(Unit("dn1", D // CW - 1), gate_b, KF // 2)

            x_rstd("final")
            dve.wait_ge(final_b_landed, 16)
            for t in range(TT):
                for h in range(2):
                    sl = slice(h * D // 2, (h + 1) * D // 2)
                    dve.scalar_tensor_tensor(x_sb[:, t, sl], x_sb[:, t, sl], stat[:, 5, t:t + 1], final_b[:, sl],
                                             ALU.mult, ALU.mult).then_inc(final_done, 1)


_INS = ["x", "c", "w_ada", "b_ada", "norm_ffn1", "w1_gate", "w1_up", "w1_down", "norm_mix", "w_in",
        "mla_q_norm", "w_uq", "mla_kv_norm", "w_ukv", "pe_cmp_k", "w_cmp_k1", "w_cmp_k2", "pe_cmp_v",
        "w_cmp_v1", "w_cmp_v2", "rel_bias", "w_out", "norm_ffn2", "w2_gate", "w2_up", "w2_down",
        "norm_final"]
_OUTS = [((1, SEQ, D), "float32")]


def kernel(**inputs):
    import numpy as _np
    import concourse.bacc as _bacc
    from concourse import mybir as _mybir
    from concourse.bass_utils import run_bass_kernel_spmd as _run

    nc = _bacc.Bacc("TRN2", target_bir_lowering=False, num_devices=1, dynamic_dma_scratch_size=1024)
    arrays, args = {}, []
    for name in _INS:
        a = _np.ascontiguousarray(inputs[name])
        arrays[f"in_{name}_dram"] = a
        args.append(nc.dram_tensor(f"in_{name}_dram", a.shape, _mybir.dt.from_np(a.dtype), kind="ExternalInput").ap())
    for i, (shape, dtype) in enumerate(_OUTS):
        dt = _mybir.dt.from_np(_np.dtype(dtype))
        args.append(nc.dram_tensor(f"out_{i}_dram", shape, dt, kind="ExternalOutput").ap())
    decoder_layer(nc, *args)
    r = _run(nc, [arrays], core_ids=[0])
    got = tuple(r.results[0][f"out_{i}_dram"] for i in range(len(_OUTS)))
    return got[0]
```

```python
from contextlib import ExitStack

import numpy as np

import concourse.bass as bass
from concourse import mybir

P = 128
F32 = mybir.dt.float32
F32R = mybir.dt.float32r
ALU = mybir.AluOpType
ACT = mybir.ActivationFunctionType
AX = mybir.AxisListType

D, SEQ, FF = 2048, 256, 5632
TT = SEQ // P
KD = D // P
KF = FF // P
CW = 512
Q_RANK, KV_RANK, ROPE, NOPE, VD = 768, 512, 64, 128, 128
HEADS = 8
DK = NOPE + ROPE
GROUPS, HPG = 2, 4
CMP_LEN, CMP_STRIDE, CMP_HID = 32, 16, 256
N_CMP = (SEQ - CMP_LEN) // CMP_STRIDE + 1
BUCKETS, MAX_DIST = 32, 128
EPS = 1e-6
SCALE = float(DK) ** -0.5
MASKED = -1e30
CMP_IN_REACH = [min(N_CMP, ((t + 1) * P - CMP_LEN) // CMP_STRIDE + 1) for t in range(TT)]
C_Q, C_KV, C_KR = 0, Q_RANK, Q_RANK + KV_RANK
C_NQ = C_KR + ROPE
C_NK = C_NQ + HEADS * DK
C_NV = C_NK + 3 * GROUPS * DK
C_NG = C_NV + 3 * GROUPS * VD
D_IN = C_NG + HEADS * 3
LAST_W = D_IN - (D_IN // CW) * CW

RING = 4
ADA_CHUNKS = 9 * D // CW
START_CHUNKS = 8
START_STEPS = KD // 2 + 1
CMP_PANELS = 24
STAGES = {"gu0": (FF // CW, KD), "dn0": (D // CW, KF // 2), "win": (D_IN // CW + 1, KD // 2),
          "uq": (HEADS * DK // CW, Q_RANK // P // 2), "ukv": (HEADS * 2 * P // CW, KV_RANK // P // 2),
          "wout": (D // CW, KD // 2), "gu1": (FF // CW, KD), "dn1": (D // CW, KF // 2)}


def slot_of(stage, j, last):
    if stage in ("uq", "ukv"):
        return min(range(RING), key=lambda s: last[s])
    panels = STAGES[stage][1]
    whole = panels // RING * RING
    if panels == whole:
        return j % RING
    return j % RING if j < whole - RING else (j - whole + RING) % (RING - 1)


def count_panels():
    table, uses, last, n = {}, [0] * RING, [None] * RING, 0
    for stage, (units, panels) in STAGES.items():
        for u in range(units):
            for j in range(panels):
                s = slot_of(stage, j, last)
                uses[s] += 1
                table[stage, u, j] = (n, uses[s], last[s], s)
                last[s] = n
                n += 1
    return table


def ada_column(q):
    return q % 2 * (START_CHUNKS // 2) + q // 2 if q < START_CHUNKS else q


def count_chunks():
    of = {("start", u): [(u, u % 2)] for u in range(START_CHUNKS)}
    where = ([("gu0", u, [0]) for u in range(1, STAGES["gu0"][0])] + [("dn0", u, [0, 1]) for u in range(4)]
             + [("win", u, [0]) for u in (1, 3, 5, 7)] + [("late", 0, [1]), ("late", 1, [0])]
             + [("gu1", u, [0]) for u in range(1, 5)])
    q = START_CHUNKS
    for stage, u, accs in where:
        of[stage, u] = [(q + e, a) for e, a in enumerate(accs)]
        q += len(accs)
    assert q == ADA_CHUNKS
    before, steps, uses, last, step = {}, {}, [0, 0], [None, None], 0
    for (stage, _), chunks in of.items():
        for q, a in chunks:
            if stage in ("start", "dn0"):
                before[q] = (uses[a], last[a], None if last[a] is None else steps[last[a]] + 1)
            else:
                before[q] = (uses[a], q - 1, step - KD + 1)
            uses[a] += 1
            last[a] = q
            steps[q] = step
            step += START_STEPS if stage == "start" else KD
    steps[ADA_CHUNKS] = step
    return of, before, steps


PANELS = count_panels()
ADA_OF, ADA_BEFORE, ADA_STEPS = count_chunks()
LATE = ADA_OF["late", 0][0][0]


class Unit:

    def __init__(self, stage, first, i=None, step=1, times=1):
        self.stage, self.first, self.i, self.step, self.times = stage, first, i, step, times

    def at(self, f):
        v = [f(self.first + r * self.step) for r in range(self.times)]
        if self.i is None or self.times == 1:
            return v[0]
        by = v[1] - v[0]
        assert all(b - a == by for a, b in zip(v, v[1:])), (self.stage, v)
        return self.i * by + v[0]

    def done(self, j):
        return self.at(lambda u: PANELS[self.stage, u, j][0] + 1)

    def slot(self, j):
        return PANELS[self.stage, self.first, j][3]

    def landed(self, j):
        return self.at(lambda u: 16 * PANELS[self.stage, u, j][1])

    def slot_free(self, j):
        if PANELS[self.stage, self.first, j][2] is None:
            return None
        return self.at(lambda u: PANELS[self.stage, u, j][2] + 1)


def units(eng, stage, first, last, step=1):
    times = (last - first) // step
    assert times * step == last - first
    with eng.Fori(0, times) as i:
        for e in range(step):
            yield Unit(stage, first + e, i, step, times)


def before(U):
    return Unit(U.stage, U.first - 1, U.i, U.step, U.times)


def part(U, ring, s):
    if U.stage == "win" and U.first == STAGES["win"][0] - 1:
        return ring[:, s, :].rearrange("p (k n) -> p k n", k=2)[:, :, 0:LAST_W]
    return ring[:, s, :]


def bucket_table():
    dist = SEQ - 1 - np.arange(384)
    n = np.maximum(dist, 0)
    exact = BUCKETS // 2
    nf = np.maximum(n, 1).astype(np.float32)
    large = exact + (np.log(nf / np.float32(exact)) / np.float32(np.log(MAX_DIST / exact))
                     * np.float32(BUCKETS - exact)).astype(np.int32)
    bucket = np.where(n < exact, n, np.minimum(large, BUCKETS - 1))
    table = np.zeros((BUCKETS + 1, 384), np.float32)
    table[bucket, np.arange(384)] = 1.0
    table[:, dist < 0] = 0.0
    table[BUCKETS, dist < 0] = MASKED
    return table


def rope_table():
    inv = np.float32(10000.0) ** (-np.arange(0, ROPE, 2, dtype=np.float32) / np.float32(ROPE))
    ang = np.arange(SEQ, dtype=np.float32)[:, None] * inv[None, :]
    both = np.stack([np.cos(ang), np.sin(ang)], 1).astype(np.float32)
    return np.ascontiguousarray(both.reshape(TT, P, 2, ROPE // 2).transpose(1, 0, 2, 3))


def decoder_layer(nc, x, c, w_ada, b_ada, norm_ffn1, w1_gate, w1_up, w1_down, norm_mix, w_in,
                  mla_q_norm, w_uq, mla_kv_norm, w_ukv, pe_cmp_k, w_cmp_k1, w_cmp_k2, pe_cmp_v,
                  w_cmp_v1, w_cmp_v2, rel_bias, w_out, norm_ffn2, w2_gate, w2_up, w2_down,
                  norm_final, out):
    ident_c = nc.inline_tensor(np.eye(P, dtype=np.float32), name="identity").ap()
    bucket_c = nc.inline_tensor(bucket_table(), name="bucket_one_hot").ap()
    rope_c = nc.inline_tensor(rope_table(), name="rope_cos_sin").ap()
    bias_scratch = nc.dram_tensor("bias_by_distance", (HEADS + 1, P, 384), F32, kind="Internal")

    def tiles(w):
        return w.rearrange("(k p) n -> p k n", p=P)

    gate_w = [tiles(w1_gate[0]), tiles(w2_gate[0])]
    up_w = [tiles(w1_up[0]), tiles(w2_up[0])]
    down_w = [tiles(w1_down[0]), tiles(w2_down[0])]
    w_in_t, w_uq_t, w_ukv_t, w_out_t = tiles(w_in[0]), tiles(w_uq[0]), tiles(w_ukv[0]), tiles(w_out[0])
    w_ada_t = tiles(w_ada[0])
    x_t = x[0].rearrange("(t p) n -> p t n", p=P)
    out_t = out[0].rearrange("(t p) n -> p t n", p=P)

    with ExitStack() as ctx:
        def sb(name, shape, dt=F32, within=ctx):
            return within.enter_context(nc.sbuf_tensor(name, shape, dt))

        def sem(name):
            return ctx.enter_context(nc.semaphore(name))

        ident = sb("ident", [P, P])
        ones = sb("ones", [P, P])
        x_sb = sb("x_sb", [P, TT, D])
        raw = sb("raw", [P, RING, 2 * CW])
        w_hi = sb("w_hi", [P, RING, 2 * CW], F32R)
        w_lo = sb("w_lo", [P, RING, 2 * CW], F32R)
        ada_raw = sb("ada_raw", [P, RING, 2 * CW])
        mod_cols = sb("mod_cols", [P, 9 * KD])
        VROWS = {"ffn1": 0, "mix": 16, "ffn2": 32, "q": 48, "kv": 54, "c": 58}
        NV = 58 + KD
        v_cols = sb("v_cols", [P, NV])
        silu_c = sb("silu_c", [P, KD])
        scale_cols = sb("scale_cols", [P, KD])
        stat = sb("stat", [P, 6, 4])
        norm_tmp = sb("norm_tmp", [P, 2, CW])
        with ExitStack() as s:
            acc = sb("ada_acc", [P, 2, CW], within=s)
            b_row = sb("b_row", [P, 2, CW], within=s)
        with ExitStack() as s:
            rope_tmp = sb("rope_tmp", [P, 4, HEADS // 2 * ROPE // 2], within=s)
        small_hold = sb("small_hold", [P, 4, CW])
        with ExitStack() as s:
            act_sg = sb("silu_gate", [P, TT, CW], within=s)
        with ExitStack() as s:
            probs = sb("probs", [P, 2, 3 * P], within=s)
        sg_hold = sb("sg_hold", [P, TT, CW])
        with ExitStack() as s:
            hT_hi = sb("hT_hi", [P, KD, SEQ], F32R, within=s)
            hT_lo = sb("hT_lo", [P, KD, SEQ], F32R, within=s)
        with ExitStack() as s:
            gate_b = sb("gate_b", [P, D], within=s)
            final_b = sb("final_b", [P, D], within=s)
        with ExitStack() as s:
            cqT = [sb(f"cqT_{n}", [P, 6, SEQ], F32R, within=s) for n in ("hi", "lo")]
            with ExitStack() as s2:
                ckvT = [sb(f"ckvT_{n}", [P, 4, SEQ], F32R, within=s2) for n in ("hi", "lo")]
            with ExitStack() as s2:
                probsT = sb("probsT", [P, 2, 3 * P], within=s2)
            ckv_hold = sb("ckv_hold", [P, 2, 4 * SEQ], within=s)
            bias = sb("bias_toeplitz", [P, HEADS + 1, SEQ], within=s)
            krT = sb("krT", [ROPE, SEQ], within=s)
            rope_sb = sb("rope_sb", [P, TT, 2, ROPE // 2], within=s)
            row_max = sb("row_max", [P, 24, 2], within=s)
            neg_max = sb("neg_max", [P, 24, 2], within=s)
            row_sum = sb("row_sum", [P, 24, 2], within=s)
        h_hold = sb("h_hold", [P, 2 * KD * SEQ])
        with ExitStack() as s:
            act_hi = sb("actT_hi", [P, KF, SEQ], F32R, within=s)
            act_lo = sb("actT_lo", [P, KF, SEQ], F32R, within=s)
        with ExitStack() as s:
            diag_r = sb("diag_rstd", [P, TT, P], within=s)
            bucket_sb = sb("bucket_sb", [BUCKETS + 1, 384], within=s)
            rel_sb = sb("rel_sb", [BUCKETS + 1, HEADS + 1], within=s)
            rev_sb = sb("rev_sb", [HEADS + 1, 384], within=s)
            v_rows = sb("v_rows", [NV, P], within=s)
        with ExitStack() as s:
            proj = sb("proj", [P, TT, D_IN], within=s)
            q_mla = sb("q_mla", [P, TT, HEADS * DK], within=s)
            kT128 = sb("kT128", [P, 6, SEQ], within=s)
            kT64 = sb("kT64", [ROPE, 6, SEQ], within=s)
            v_cmp = sb("v_cmp", [P, GROUPS, HPG * VD], within=s)
            kc128 = sb("kc128", [P, GROUPS * N_CMP], within=s)
            kc64 = sb("kc64", [ROPE, GROUPS * N_CMP], within=s)
            with ExitStack() as s2:
                kpe128 = sb("kpe128", [P, CMP_LEN, GROUPS * N_CMP], within=s2)
                kpe64 = sb("kpe64", [ROPE, CMP_LEN, GROUPS * N_CMP], within=s2)
                vpe = sb("vpe", [P, CMP_LEN, GROUPS * N_CMP], within=s2)
            kv_mla = sb("kv_mla", [P, TT, HEADS * 2 * P], within=s)
            with ExitStack() as s2:
                hid = sb("hid", [GROUPS * N_CMP, 2, CMP_HID], within=s2)
                hidT = sb("hidT", [P, 4, GROUPS * N_CMP], within=s2)
                w2v = sb("w2v", [P, 2, VD], within=s2)
                peT = sb("peT", [P, 3, CMP_LEN], within=s2)
                w2k = sb("w2k", [P, 2, DK], within=s2)
            qkT = sb("qkT", [P, 2, 2 * SEQ], within=s)
            qrT = sb("qrT", [ROPE, 2, SEQ], within=s)
        a_hold = sb("a_hold", [P, 2 * KF * SEQ])
        gates = sb("gates", [P, TT, HEADS * 3])
        coef = sb("coef", [P, 24, 2])
        cmp_stat = sb("cmp_stat", [P, 4, HEADS * TT])
        pe_sb = sb("pe_sb", [CMP_LEN, DK + VD])
        rstd_b = sb("rstd_b", [P, SEQ])
        x_sq = sb("x_sq", [P, TT, D // CW])
        cmp_p = norm_tmp
        o_nsa, o_mla = proj[:, :, 0:HEADS * VD], q_mla[:, :, 0:HEADS * VD]
        cmp_pT = kT128[:, 0:2, :]
        NSA = 2 * HEADS

        ps = ctx.enter_context(nc.psum_tensor("ps", [P, 8, CW], F32))
        T_BANK, ADA_BANK, MISC_BANK = 4, 6, 7

        raw_landed = [sem(f"raw_landed{s}") for s in range(RING)]
        hi_done, lo_done, mm_done = sem("hi_done"), sem("lo_done"), sem("mm_done")
        ada_landed = [sem(f"ada_landed{s}") for s in range(RING)]
        b_landed = [sem(f"b_landed{s}") for s in range(2)]
        acc_step = sem("acc_step")
        acc_turned, mod_done = sem("acc_turned"), sem("mod_done")
        const_landed, x_landed, rel_landed = sem("const_landed"), sem("x_landed"), sem("rel_landed")
        rel_set = sem("rel_set")
        ones_set, rows_set = sem("ones_set"), sem("rows_set")
        v_turned, v_done, silu_c_done = sem("v_turned"), sem("v_done"), sem("silu_c_done")
        rev_mm, rev_done, rev_stored = sem("rev_mm"), sem("rev_done"), sem("rev_stored")
        dve_step, pool_step = sem("dve_step"), sem("pool_step")
        gu = [{n: sem(f"{n}{f}") for n in ("silu_done", "prod_done", "prod_turned", "actT_hi_done",
                                          "actT_lo_done")} for f in range(2)]
        nrm = {n: {m: sem(f"{m}_{n}") for m in ("squares", "mean", "root", "xn_done", "turned", "tmp_done",
                                               "T_hi_done", "T_lo_done")}
               for n in ("ffn1", "mix", "ffn2", "mla", "o", "final")}
        gat = [{n: sem(f"{n}{f}") for n in ("diag_done", "gate_mm", "gate_b_done")} for f in range(3)]
        res = {n: {m: sem(f"{m}_{n}") for m in ("bank_read", "x_added")} for n in ("dn0", "wout", "dn1")}
        copied = {n: sem(f"copied_{n}") for n in ("win", "uq", "ukv")}
        A = {n: sem(n) for n in ("bias_landed", "kr_turned", "kr_copied",
                                 "q_turned", "qk_copied", "qr_copied", "scored", "maxed", "neg_done", "exped",
                                 "p_turned", "pT_copied", "pv_done", "o_done",
                                 "k_turned", "kT_copied", "kT64_copied", "v_turned_c", "pe_turned", "cmp_read",
                                 "kpe_done", "cw_used", "hid_done", "hid_turned", "hidT_copied",
                                 "kc_mm", "kc_copied", "vc_copied", "gates_exp",
                                 "gates_done", "cmp_scored", "cmp_ready", "cmp_exped",
                                 "cmp_turned", "cmp_copied", "cmp_pv", "cmp_o", "cmp_w_landed",
                                 "rope_landed")}
        final_done, final_b_landed, stored = sem("final_done"), sem("final_b_landed"), sem("stored")
        NORM_OF = {"gu0": "ffn1", "win": "mix", "gu1": "ffn2", "wout": "o"}
        ada_after = {"gu0": 4, "dn0": 4, "win": 0, "gu1": 4}
        NBANKS = {"ffn1": 1, "mix": 3, "ffn2": 2, "mla": 2, "o": 3}
        ROW_BANK = (MISC_BANK, T_BANK + 1)
        FINAL_PIECES = [(t, c) for t in range(TT) for c in range(D // CW)]
        KEY_BANK = (T_BANK, 2, T_BANK)
        SHIFT_OF = {"ffn1": 0, "mix": 3, "ffn2": 6}
        RSTD_USE = {"ffn1": 1, "mix": 2, "ffn2": 3}
        rstd_mm, rstd_b_done, shifted = sem("rstd_mm"), sem("rstd_b_done"), sem("shifted")

        def shift_col(n, k):
            c = SHIFT_OF[n] * KD + k
            return mod_cols[:, c:c + 1]

        ada_by_pe = sem("ada_by_pe")

        def ada_use(q, p):
            return 2 * q + p // RING + 1 + (CMP_PANELS // RING if q >= LATE else 0)

        tile_done = sem("tile_done")
        TILE_BASE, n_units = {}, 0
        for stage in ("dn0", "win", "wout", "dn1"):
            TILE_BASE[stage] = n_units
            n_units += STAGES[stage][0]

        def wait_products(eng, U, t):
            if t == 0 and U.stage in TILE_BASE:
                eng.wait_ge(tile_done, U.at(lambda u: TILE_BASE[U.stage] + u + 1))
            else:
                eng.wait_ge(mm_done, U.done(STAGES[U.stage][1] - 1))

        def ada_steps(U, e, n):
            return U.at(lambda u: ADA_STEPS[ADA_OF[U.stage, u][e][0]] + n)

        block = ctx.enter_context(nc.Block())

        @block.sync
        def _(sp):
            def load(U, j, src, width=CW):
                free = U.slot_free(j)
                if free is not None:
                    sp.wait_ge(lo_done, free)
                dst = raw[:, U.slot(j), :].rearrange("p (k n) -> p k n", k=2)[:, :, 0:width]
                sp.dma_start(dst, src).then_inc(raw_landed[U.slot(j)], 16)

            def columns(w, k, U, width=CW):
                return w[:, k:k + 2, bass.ds(U.at(lambda u: u * CW), width)]

            def load_ada(U, e, p):
                col = U.at(lambda u: ada_column(ADA_OF[U.stage, u][e][0]))
                q0, a = ADA_OF[U.stage, U.first][e]
                if p == 0:
                    if ADA_BEFORE[q0][1] is not None:
                        sp.wait_ge(acc_step, U.at(lambda u: ADA_BEFORE[ADA_OF[U.stage, u][e][0]][2]))
                    else:
                        sp.wait_ge(rows_set, 1)
                    sp.dma_start(b_row[0:1, a, :], b_ada[0:1, bass.ds(col * CW, CW)]).then_inc(b_landed[a], 16)
                if U.stage == "start":
                    r = U.first
                    if p % 2:
                        if U.first > 0 or p >= RING:
                            sp.wait_ge(ada_by_pe, r * 4 + (p - RING + 1) // 2)
                    elif U.first > 0 or p >= RING:
                        sp.wait_ge(acc_step, r * START_STEPS + (p - RING + 2 if p >= RING else p - RING + 1))
                elif q0 == LATE and p < RING:
                    sp.wait_ge(A["cw_used"], CMP_PANELS - RING + p + 1)
                elif U.stage == "gu0":
                    sp.wait_ge(acc_step, ada_steps(U, e, max(0, 2 * (p - RING + 1))))
                else:
                    sp.wait_ge(acc_step, ada_steps(U, e, 2 * (p - RING + 1)))
                sp.dma_start(ada_raw[:, p % RING, :].rearrange("p (k n) -> p k n", k=2),
                             w_ada_t[:, 2 * p:2 * p + 2, bass.ds(col * CW, CW)]).then_inc(ada_landed[p % RING], 16)

            def load_unit(U, panel):
                chunks = ADA_OF.get((U.stage, U.first), [])
                for j in range(STAGES[U.stage][1]):
                    p = j - ada_after.get(U.stage, 0)
                    if 0 <= p < 8 * len(chunks):
                        load_ada(U, p // 8, p % 8)
                    panel(U, j)

            def gate_up(f):
                def panel(U, j):
                    load(U, j, columns((gate_w, up_w)[j % 2][f], j // 2 * 2, U))
                return panel

            def rows_of(w, width=CW):
                return lambda U, j: load(U, j, columns(w, 2 * j, U, width), width)

            first = Unit("gu0", 0)
            panels = iter(range(KD))
            for q in range(START_CHUNKS):
                for p in range(8):
                    load_ada(Unit("start", q), 0, p)
                    if q < 2 and p in (3, 7):
                        gate_up(0)(first, next(panels))
                    if q >= 3 and p in (1, 5):
                        gate_up(0)(first, next(panels))
            for j in panels:
                gate_up(0)(first, j)
            for U in units(sp, "gu0", 1, STAGES["gu0"][0]):
                load_unit(U, gate_up(0))
            load_unit(Unit("dn0", 0), rows_of(down_w[0]))
            for U in units(sp, "dn0", 1, STAGES["dn0"][0]):
                load_unit(U, rows_of(down_w[0]))
            load_unit(Unit("win", 0), rows_of(w_in_t))
            for U in units(sp, "win", 1, STAGES["win"][0] - 1, 2):
                load_unit(U, rows_of(w_in_t))
            load_unit(Unit("win", STAGES["win"][0] - 1), rows_of(w_in_t, LAST_W))
            sp.wait_ge(copied["win"], 1)
            sp.dma_start(w2k[:, :, :], tiles(w_cmp_k2[0])).then_inc(A["cmp_w_landed"], 16)
            sp.dma_start(w2v[:, :, :], tiles(w_cmp_v2[0])).then_inc(A["cmp_w_landed"], 16)
            small = [(Unit(stage, u), j, w) for stage, w in (("uq", w_uq_t), ("ukv", w_ukv_t))
                     for u in range(STAGES[stage][0]) for j in range(STAGES[stage][1])]
            for U, j, w in small[:RING]:
                rows_of(w)(U, j)
            k1 = w_cmp_k1[0].rearrange("(l d) n -> d l n", d=DK)
            v1 = w_cmp_v1[0].rearrange("(l d) n -> d l n", d=VD)
            for m in range(CMP_PANELS):
                l0 = m % 8 * 4
                if m < RING:
                    sp.wait_ge(acc_step, ADA_STEPS[LATE])
                else:
                    sp.wait_ge(A["cw_used"], m - RING + 1)
                rows, src = [(P, k1[0:P]), (ROPE, k1[P:DK]), (P, v1)][m // 8]
                sp.dma_start(ada_raw[0:rows, m % RING, :].rearrange("p (l n) -> p l n", l=4),
                             src[:, l0:l0 + 4, :]).then_inc(ada_landed[m % RING], 16)
                if m == RING:
                    sp.wait_ge(mm_done, Unit("win", STAGES["win"][0] - 1).done(KD // 2 - 1))
                    sp.dma_start(rope_sb[:, :, :, :], rope_c).then_inc(A["rope_landed"], 16)
                    sp.wait_ge(rev_stored, 16)
                    sp.dma_start(bias[:, :, :], bass.AP(tensor=bias_scratch, offset=P - 1,
                                                        ap=[[383, P], [P * 384, HEADS + 1], [1, SEQ]]))\
                        .then_inc(A["bias_landed"], 16)
            for i, (U, j, w) in enumerate(small[RING:]):
                rows_of(w)(U, j)
                if i < 8:
                    load_ada(Unit("late", 0), 0, i)

            def out_rows(U, j):
                load(U, j, columns(w_out_t, 2 * j, U))

            for j in range(RING):
                out_rows(Unit("wout", 0), j)
            for p in range(8):
                load_ada(Unit("late", 1), 0, p)
            for j in range(RING, STAGES["wout"][1]):
                out_rows(Unit("wout", 0), j)
            for U in units(sp, "wout", 1, STAGES["wout"][0]):
                load_unit(U, out_rows)
            load_unit(Unit("gu1", 0), gate_up(1))
            for a, b in ((1, 5), (5, STAGES["gu1"][0])):
                for U in units(sp, "gu1", a, b):
                    load_unit(U, gate_up(1))
            load_unit(Unit("dn1", 0), rows_of(down_w[1]))
            sp.wait_ge(gat[2]["gate_b_done"], 4)
            sp.dma_start(final_b[:, :], norm_final.rearrange("(a n) -> a n", a=1).broadcast_to([P, D]))\
                .then_inc(final_b_landed, 16)
            for U in units(sp, "dn1", 1, STAGES["dn1"][0]):
                load_unit(U, rows_of(down_w[1]))
            for i, (t, c) in enumerate(FINAL_PIECES):
                sp.wait_ge(final_done, i + 1)
                sl = slice(c * CW, (c + 1) * CW)
                sp.dma_start(out_t[:, t, sl], x_sb[:, t, sl]).then_inc(stored, 16)
            sp.wait_ge(stored, 16 * TT * (D // CW))

        @block.gpsimd
        def _(pool):
            pool.memset(b_row[:, :, :], 0.0).then_inc(rows_set, 1)
            pool.memset(ones[:, :], 1.0).then_inc(ones_set, 1)

            n_step = 0

            def rotate(t1, t2, cos, sin, tmp):
                nonlocal n_step
                for o, a, b in ((0, t1, cos), (1, t2, sin), (2, t1, sin), (3, t2, cos)):
                    pool.tensor_tensor(tmp[o], a, b, ALU.mult).then_inc(pool_step, 1)
                n_step += 4
                pool.wait_ge(pool_step, n_step)
                pool.tensor_tensor(t1, tmp[0], tmp[1], ALU.subtract).then_inc(pool_step, 1)
                pool.tensor_tensor(t2, tmp[2], tmp[3], ALU.add).then_inc(pool_step, 1)
                n_step += 2
                pool.wait_ge(pool_step, n_step)

            def round_lo(n, r, T, k):
                pool.wait_ge(nrm[n]["T_hi_done"], r + 1)
                pool.tensor_tensor(T[1][:, k:k + 2, :].rearrange("p k n -> p (k n)"), norm_tmp[:, r % 2, :],
                                   T[0][:, k:k + 2, :].rearrange("p k n -> p (k n)").bitcast(F32), ALU.subtract)\
                    .then_inc(nrm[n]["T_lo_done"], 1)

            for r in range(KD // 2):
                round_lo("ffn1", r, (hT_hi, hT_lo), 2 * r)
            for r in range(5):
                round_lo("mla", r, cqT if r < 3 else ckvT, 2 * r if r < 3 else 2 * r - 6)

            half, hh = ROPE // 2, HEADS // 2
            pool.wait_ge(A["rope_landed"], 16)
            pool.wait_ge(mod_done, LATE)
            for t in range(TT):
                kr = proj[:, t, C_KR:C_KR + ROPE]
                rotate(kr[:, 0:half], kr[:, half:ROPE], rope_sb[:, t, 0, :], rope_sb[:, t, 1, :],
                       [rope_tmp[:, o, 0:half] for o in range(4)])
            pool.wait_ge(copied["uq"], 2 * STAGES["uq"][0])
            for t in range(TT):
                for h0 in (0, hh):
                    qr = q_mla[:, t, h0 * DK:(h0 + hh) * DK].rearrange("p (h d) -> p h d", h=hh)
                    cos, sin = (rope_sb[:, t, o, :].unsqueeze(1).broadcast_to([P, hh, half]) for o in range(2))
                    rotate(qr[:, :, NOPE:NOPE + half], qr[:, :, NOPE + half:DK], cos, sin,
                           [rope_tmp[:, o, :].rearrange("p (h d) -> p h d", h=hh) for o in range(4)])

        @block.tensor
        def _(pe):
            def three(bank, lhs_hi, lhs_lo, rhs_hi, rhs_lo, start, stop):
                pe.matmul(bank, lhs_hi, rhs_hi, start=start, stop=False)
                pe.matmul(bank, lhs_hi, rhs_lo, start=False, stop=False)
                return pe.matmul(bank, lhs_lo, rhs_hi, start=False, stop=stop)

            def panel(U, j, T, k, bank, first, last, width=CW, tile_ready=None):
                signal_tile = last and U.stage in TILE_BASE
                pe.wait_ge(lo_done, U.done(j))
                s = U.slot(j)
                for t in range(TT):
                    if tile_ready is not None:
                        tile_ready(t)
                    for kk in range(2):
                        mm = three(ps[:, bank + t, 0:width], T[0][:, k + kk, t * P:(t + 1) * P],
                                   T[1][:, k + kk, t * P:(t + 1) * P],
                                   w_hi[:, s, kk * CW:kk * CW + width], w_lo[:, s, kk * CW:kk * CW + width],
                                   first and kk == 0, last and kk == 1)
                    if t == 0 and signal_tile:
                        mm.then_inc(tile_done, 1)
                mm.then_inc(mm_done, 1)

            def turn_ada(U, e):
                q = U.at(lambda u: ADA_OF[U.stage, u][e][0])
                a = ADA_OF[U.stage, U.first][e][1]
                pe.wait_ge(acc_step, ada_steps(U, e, START_STEPS if U.stage == "start" else KD))
                if not (U.stage == "start" and U.first == 0):
                    pe.wait_ge(mod_done, q)
                for b in range(4):
                    mm = pe.transpose(ps[:, ADA_BANK, b * P:(b + 1) * P], acc[:, a, b * P:(b + 1) * P], ident[:, :])
                mm.then_inc(acc_turned, 1)

            def start_ada(q, after):
                for p in (1, 3, 5, 7):
                    pe.wait_ge(ada_landed[p % RING], q * 32 + 16 * (p // RING + 1))
                    for kk in range(2):
                        k = 2 * p + kk
                        mm = pe.matmul(ps[0:1, ROW_BANK[q % 2], :], silu_c[:, k:k + 1],
                                       ada_raw[:, p % RING, kk * CW:(kk + 1) * CW], start=k == 2, stop=k == KD - 1)
                    mm.then_inc(ada_by_pe, 1)
                    if p in after:
                        after[p]()

            def turn_norm(n, r, src):
                nb = NBANKS[n]
                if r >= nb:
                    pe.wait_ge(nrm[n]["T_lo_done" if n == "o" else "tmp_done"], r - nb + 1)
                if n == "o" and r < HEADS // 2:
                    pe.wait_ge(A["o_done"], 2 * (NSA + 2 * r + 2))
                elif n == "o":
                    pe.wait_ge(A["cmp_o"], 2 * r + 2)
                for kk in range(2):
                    for t in range(TT):
                        dst = ps[:, T_BANK + r % nb, (kk * TT + t) * P:(kk * TT + t + 1) * P]
                        mm = pe.transpose(dst, src(2 * r + kk, t), ident[:, :])
                mm.then_inc(nrm[n]["turned"], 1)

            def x_tile(k, t):
                return x_sb[:, t, k * P:(k + 1) * P]

            def spread_rstd(n, bank):
                pe.wait_ge(nrm[n]["xn_done"], 1)
                for t in range(TT):
                    mm = pe.matmul(ps[:, bank, t * P:(t + 1) * P], ones[:, :], diag_r[:, t, :], start=True, stop=True)
                mm.then_inc(rstd_mm, 1)

            def rounds_ahead(n, r, src=x_tile):
                ahead = r + NBANKS[n] - 1
                if r >= 1 and ahead < KD // 2:
                    turn_norm(n, ahead, src)

            def turn_products(f, U):
                pe.wait_ge(gu[f]["prod_done"], U.at(lambda u: 2 * u + 2))
                for b in range(2):
                    for kk in range(2):
                        for t in range(TT):
                            mm = pe.transpose(ps[:, T_BANK + b, (kk * TT + t) * P:(kk * TT + t + 1) * P],
                                              act_sg[:, t, (2 * b + kk) * P:(2 * b + kk + 1) * P], ident[:, :])
                    mm.then_inc(gu[f]["prod_turned"], 1)

            def gate_up_unit(f, U, fresh):
                prev = None if U.first == 0 else before(U)
                for j in range(KD):
                    if fresh:
                        r = j // 2
                        if j % 2 == 0:
                            rounds_ahead(NORM_OF[U.stage], r)
                            pe.wait_ge(nrm[NORM_OF[U.stage]]["T_lo_done"], r + 1)
                    elif j == 0:
                        pe.wait_ge(gu[f]["silu_done"], U.at(lambda u: 2 * u))
                    elif j == 1:
                        pe.wait_ge(gu[f]["prod_done"], U.at(lambda u: 2 * u))
                    panel(U, j, (hT_hi, hT_lo), j // 2 * 2, 2 * (j % 2), j < 2, j >= KD - 2)
                    if j == 13 and (U.stage, U.first) in ADA_OF:
                        turn_ada(U, 0)
                    if not fresh and j == 1:
                        turn_products(f, prev)

            def gate_broadcast(f, c):
                pe.wait_ge(gat[f]["diag_done"], c + 1)
                if c > 0:
                    pe.wait_ge(gat[f]["gate_b_done"], c)
                pe.matmul(ps[:, MISC_BANK, :], ones[:, :], norm_tmp[:, c % 2, :], start=True, stop=True).then_inc(gat[f]["gate_mm"], 1)

            def down_unit(f, U):
                stage, L = U.stage, STAGES[U.stage][1]
                done = res[stage]["bank_read"]
                for j in range(L):
                    if j == L - 2 and U.first == 0:
                        pe.wait_ge(gu[f]["actT_lo_done"], 2 * (FF // CW))

                    def tile_ready(t):
                        if j == 0 and U.first > 0:
                            pe.wait_ge(done, U.at(lambda u: 2 * (u - 1) + t + 1))
                        elif j == 0:
                            pe.wait_ge(gu[f]["silu_done"], 2 * (FF // CW))
                    panel(U, j, (act_hi, act_lo), 2 * j, 0, j == 0, j == L - 1, tile_ready=tile_ready)
                    if j == 20 and f == 0:
                        turn_ada(U, 1)
                    if j == 1 and U.first == 0:
                        turn_products(f, Unit(f"gu{f}", FF // CW - 1))
                    if j == 14 and f == 0:
                        turn_ada(U, 0)
                    if U.first == 0 and j in (8, 10, 12, 14):
                        gate_broadcast(2 * f, (j - 8) // 2)

            pe.wait_ge(const_landed, 16 * 10)
            pe.transpose(ps[:, MISC_BANK, 0:NV], v_rows[:, :], ident[0:NV, 0:NV]).then_inc(v_turned, 1)
            pe.wait_ge(silu_c_done, 1)

            def turn_start(q):
                turn_ada(Unit("start", q), 0)

            def first_panel(j):
                if j % 2 == 0:
                    pe.wait_ge(nrm["ffn1"]["T_lo_done"], j // 2 + 1)
                panel(Unit("gu0", 0), j, (hT_hi, hT_lo), j // 2 * 2, 2 * (j % 2), j < 2, j >= KD - 2)

            start_ada(0, {})
            pe.wait_ge(rel_landed, 16)
            pe.wait_ge(ones_set, 1)
            pe.matmul(ps[0:HEADS + 1, T_BANK + 1, 0:384], rel_sb[:, :], bucket_sb[:, :], start=True, stop=True)\
                .then_inc(rev_mm, 1)
            pe.wait_ge(rev_done, 1)
            start_ada(1, {1: lambda: turn_start(0)})
            spread_rstd("ffn1", T_BANK)
            pe.wait_ge(rstd_b_done, 1)
            turn_norm("ffn1", 0, x_tile)
            for q in range(2, START_CHUNKS, 2):
                a = 2 * (q - 2)
                start_ada(q, {1: lambda: turn_start(q - 1), 3: lambda: turn_norm("ffn1", q - 1, x_tile),
                              5: lambda: first_panel(a)})
                start_ada(q + 1, {1: lambda: (turn_start(q), first_panel(a + 1)),
                                  3: lambda: turn_norm("ffn1", q, x_tile),
                                  5: lambda: first_panel(a + 2), 7: lambda: first_panel(a + 3)})
            turn_start(START_CHUNKS - 1)
            turn_norm("ffn1", KD // 2 - 1, x_tile)
            for j in range(KD - 4, KD):
                first_panel(j)

            def first_rounds(n, src, added=None):
                for r in range(NBANKS[n]):
                    if added is not None:
                        pe.wait_ge(added, 2 * (r // 2) + 2)
                    turn_norm(n, r, src)
                    if r == 0 and n in RSTD_USE:
                        spread_rstd(n, MISC_BANK)

            for U in units(pe, "gu0", 1, FF // CW):
                gate_up_unit(0, U, False)
            down_unit(0, Unit("dn0", 0))
            for U in units(pe, "dn0", 1, D // CW):
                down_unit(0, U)

            def project_in(U, width=CW):
                L = STAGES["win"][1]
                for j in range(L):
                    def tile_ready(t):
                        if j == 0 and U.first > 0:
                            pe.wait_ge(copied["win"], U.at(lambda u: 2 * (u - 1) + t + 1))
                        elif j == 0:
                            pe.wait_ge(res["dn0"]["bank_read"], 2 * (D // CW))
                    if U.first == 0:
                        rounds_ahead("mix", j)
                        pe.wait_ge(nrm["mix"]["T_lo_done"], j + 1)
                    panel(U, j, (hT_hi, hT_lo), 2 * j, 0, j == 0, j == L - 1, width, tile_ready)
                    if j == 0 and U.first > 0 and U.first % 2 == 0:
                        turn_ada(before(U), 0)

            pe.wait_ge(mod_done, ADA_OF["win", 1][0][0])
            first_rounds("mix", x_tile, res["dn0"]["x_added"])
            project_in(Unit("win", 0))
            for U in units(pe, "win", 1, STAGES["win"][0] - 1, 2):
                project_in(U)

            def turn_keys(r):
                for i in range(2):
                    for t in range(TT):
                        k0 = C_NK + (2 * r + i) * DK
                        cols = slice(i * SEQ + t * P, i * SEQ + (t + 1) * P)
                        pe.transpose(ps[:, KEY_BANK[r], cols], proj[:, t, k0:k0 + P], ident[:, :])
                        mm = pe.transpose(ps[0:ROPE, KEY_BANK[r] + 1, cols], proj[:, t, k0 + P:k0 + DK], ident[:, :])
                mm.then_inc(A["k_turned"], 1)

            id32 = ident[0:CMP_LEN, 0:CMP_LEN]
            pe.transpose(ps[:, MISC_BANK, 0:32], pe_sb[:, 0:P], id32)
            pe.transpose(ps[0:ROPE, MISC_BANK, 32:64], pe_sb[:, P:DK], id32)
            pe.transpose(ps[:, MISC_BANK, 64:96], pe_sb[:, DK:DK + VD], id32).then_inc(A["pe_turned"], 1)
            pe.wait_ge(copied["win"], 2 * ((C_NV - 1) // CW + 1))
            pe.wait_ge(nrm["mix"]["tmp_done"], KD // 2)
            turn_keys(0)
            turn_keys(1)
            project_in(Unit("win", STAGES["win"][0] - 1), LAST_W)
            pe.wait_ge(A["kT_copied"], 2)
            pe.wait_ge(A["kT64_copied"], 2)
            turn_keys(2)
            pe.wait_ge(copied["win"], 2 * ((C_NV + GROUPS * VD - 1) // CW + 1))
            for g in range(GROUPS):
                for t in range(TT):
                    mm = pe.transpose(ps[:, 2, g * SEQ + t * P:g * SEQ + (t + 1) * P],
                                      proj[:, t, C_NV + g * VD:C_NV + (g + 1) * VD], ident[:, :])
            mm.then_inc(A["v_turned_c"], 1)
            pe.wait_ge(mod_done, LATE)
            for m in range(CMP_PANELS):
                which, l0 = m // 8, m % 8 * 4
                if m % 8 == 0:
                    pe.wait_ge(A["kpe_done"], (4, 8, 12)[which])
                pe.wait_ge(ada_landed[m % RING], 16 * (2 * LATE + m // RING + 1))
                blocks, rows = ((kpe128, P), (kpe64, ROPE), (vpe, P))[which]
                for l in range(4):
                    mm = pe.matmul(ps[0:GROUPS * N_CMP, 6 + which // 2, 0:CMP_HID], blocks[:, l0 + l, :],
                                   ada_raw[0:rows, m % RING, l * CMP_HID:(l + 1) * CMP_HID],
                                   start=m in (0, 16) and l == 0, stop=m in (15, 23) and l == 3)
                mm.then_inc(A["cw_used"], 1)
                if m % 3 == 2 and m >= 8 and m < 23:
                    r = (m - 8) // 3
                    if r == 0:
                        pe.wait_ge(A["kT_copied"], 3)
                        pe.wait_ge(A["kT64_copied"], 3)
                        pe.wait_ge(nrm["mla"]["xn_done"], 4)
                    c0 = C_Q if r < 3 else C_KV - 6 * P
                    turn_norm("mla", r, lambda k, t: proj[:, t, c0 + k * P:c0 + (k + 1) * P])

            n = GROUPS * N_CMP

            def turn_hidden():
                pe.wait_ge(nrm["mla"]["tmp_done"], 5)
                pe.wait_ge(A["hid_done"], 2)
                for i in range(4):
                    mm = pe.transpose(ps[:, 4, i * 32:i * 32 + n], hid[:, i // 2, i % 2 * P:(i % 2 + 1) * P],
                                      ident[0:n, 0:n])
                mm.then_inc(A["hid_turned"], 1)

            def compressed_keys():
                pe.wait_ge(A["hidT_copied"], 1)
                pe.wait_ge(A["cmp_w_landed"], 32)
                for rows, c0 in ((P, 0), (ROPE, P)):
                    for i in range(2):
                        mm = pe.matmul(ps[0:rows, 5, c0 // 4:c0 // 4 + n], w2k[:, i, c0:c0 + rows], hidT[:, i, :],
                                       start=i == 0, stop=i == 1)
                mm.then_inc(A["kc_mm"], 1)

            def compressed_values():
                for g in range(GROUPS):
                    for h in range(HPG):
                        for i in range(2):
                            mm = pe.matmul(ps[32 * h:32 * h + N_CMP, 6 + g, h * VD:(h + 1) * VD],
                                           hidT[:, 2 + i, g * N_CMP:(g + 1) * N_CMP], w2v[:, i, :],
                                           start=i == 0, stop=i == 1)
                mm.then_inc(A["kc_mm"], 1)

            between_units = {("uq", 0): turn_hidden, ("uq", 1): compressed_keys, ("uq", 2): compressed_values}
            for stage, T, n0 in (("uq", cqT, 0), ("ukv", ckvT, 3)):
                for u in range(STAGES[stage][0]):
                    L = STAGES[stage][1]
                    b = 2 * ((u + (stage == "ukv")) % 2)

                    def tile_ready(t):
                        if u >= 2:
                            pe.wait_ge(copied[stage], 2 * (u - 2) + t + 1)
                        elif stage == "ukv":
                            pe.wait_ge(copied["uq"], 2 * (u + 1) + t + 1)
                        elif u == 1:
                            pe.wait_ge(A["kpe_done"], 12)
                    for j in range(L):
                        if u == 0:
                            pe.wait_ge(nrm["mla"]["T_lo_done"], n0 + j + 1)
                        panel(Unit(stage, u), j, T, 2 * j, b, j == 0, j == L - 1,
                              tile_ready=tile_ready if j == 0 else None)
                    if (stage, u) in between_units:
                        between_units[stage, u]()
            turn_ada(Unit("late", 0), 0)
            pe.wait_ge(copied["win"], 2 * STAGES["win"][0])
            pe.wait_ge(pool_step, 6 * TT)
            pe.wait_ge(A["hidT_copied"], 1)
            for t in range(TT):
                mm = pe.transpose(ps[0:ROPE, T_BANK, t * P:(t + 1) * P], proj[:, t, C_KR:C_KR + ROPE], ident[:, :])
            mm.then_inc(A["kr_turned"], 1)
            pe.wait_ge(A["kc_copied"], 2)
            pe.wait_ge(A["vc_copied"], 2 * HPG)

            def turn_q(u):
                nsa = u < NSA
                if nsa and u % 2:
                    return
                h = u // 2 if nsa else u - NSA
                e = h if nsa else HEADS + h
                if e == 0:
                    pe.wait_ge(A["kr_copied"], 1)
                else:
                    pe.wait_ge(A["qk_copied"], e)
                if e == HEADS:
                    pe.wait_ge(A["cmp_read"], TT)
                    pe.wait_ge(pool_step, 18 * TT)
                elif e > HEADS:
                    pe.wait_ge(A["qr_copied"], h)
                for t in range(TT):
                    cols = slice(t * P, (t + 1) * P)
                    cols2 = slice(SEQ + t * P, SEQ + (t + 1) * P)
                    if nsa:
                        q0 = C_NQ + h * DK
                        pe.transpose(ps[:, T_BANK, cols], proj[:, t, q0:q0 + NOPE], ident[:, :])
                        mm = pe.transpose(ps[0:ROPE, T_BANK, cols2], proj[:, t, q0 + NOPE:q0 + DK], ident[:, :])
                    else:
                        pe.transpose(ps[:, T_BANK, cols], q_mla[:, t, h * DK:h * DK + NOPE], ident[:, :])
                        pe.transpose(ps[:, T_BANK, cols2], kv_mla[:, t, h * 2 * P:h * 2 * P + P], ident[:, :])
                        mm = pe.transpose(ps[0:ROPE, T_BANK + 1, cols], q_mla[:, t, h * DK + NOPE:(h + 1) * DK],
                                          ident[:, :])
                mm.then_inc(A["q_turned"], 1)

            def score(u):
                nsa = u < NSA
                h = u // 2 if nsa else u - NSA
                e = h if nsa else HEADS + h
                b = e % 2
                pe.wait_ge(A["qk_copied"], e + 1)
                if not nsa:
                    pe.wait_ge(A["qr_copied"], h + 1)
                if u >= 2:
                    pe.wait_ge(A["maxed"], 2 * (u - 1))
                else:
                    pe.wait_ge(copied["ukv"], 2 * STAGES["ukv"][0])
                kx = (1 + u % 2) * GROUPS + h // HPG
                for t in range(TT):
                    w = (t + 1) * P
                    dst = ps[:, 2 + u % 2, t * P:t * P + w]
                    pe.matmul(dst, qkT[:, b, t * P:(t + 1) * P],
                              kT128[:, kx, 0:w] if nsa else qkT[:, b, SEQ:SEQ + w], start=True, stop=False)
                    mm = pe.matmul(dst, qrT[:, b, t * P:(t + 1) * P],
                                   kT64[:, kx, 0:w] if nsa else krT[:, 0:w], start=False, stop=True)
                mm.then_inc(A["scored"], 1)
                if nsa and u % 2 == 0:
                    g = h // HPG
                    for t in range(TT):
                        dst = ps[:, 5, t * SEQ + h * 32:t * SEQ + h * 32 + N_CMP]
                        pe.matmul(dst, qkT[:, b, t * P:(t + 1) * P], kc128[:, g * N_CMP:(g + 1) * N_CMP],
                                  start=True, stop=False)
                        mm = pe.matmul(dst, qrT[:, b, t * P:(t + 1) * P], kc64[:, g * N_CMP:(g + 1) * N_CMP],
                                       start=False, stop=True)
                    mm.then_inc(A["cmp_scored"], 1)

            def turn_p(u):
                pe.wait_ge(A["exped"], 2 * (u + 1))
                if u >= 2:
                    pe.wait_ge(A["pT_copied"], u - 1)
                elif u == 0:
                    pe.wait_ge(mod_done, LATE + 1)
                for b in range(3):
                    mm = pe.transpose(ps[:, 6 + u % 2, b * P:(b + 1) * P], probs[:, u % 2, b * P:(b + 1) * P],
                                      ident[:, :])
                mm.then_inc(A["p_turned"], 1)

            def times_v(u):
                pe.wait_ge(A["pT_copied"], u + 1)
                if u >= 2:
                    pe.wait_ge(A["o_done"], 2 * (u - 1))
                for t in range(TT):
                    for kt in range(t + 1):
                        if u >= NSA:
                            v = kv_mla[:, kt, (u - NSA) * 2 * P + P:(u - NSA + 1) * 2 * P]
                        else:
                            kx = (1 + u % 2) * GROUPS + u // 2 // HPG
                            v = proj[:, kt, C_NV + kx * VD:C_NV + (kx + 1) * VD]
                        mm = pe.matmul(ps[:, u % 2, t * P:(t + 1) * P], probsT[:, u % 2, (t + kt) * P:(t + kt + 1) * P],
                                       v, start=kt == 0, stop=kt == t)
                mm.then_inc(A["pv_done"], 1)

            def turn_cmp():
                pe.wait_ge(A["qk_copied"], 2 * HEADS)
                pe.wait_ge(A["qr_copied"], HEADS)
                for t in range(TT):
                    pe.wait_ge(A["cmp_exped"], t + 1)
                    for g in range(GROUPS):
                        mm = pe.transpose(ps[:, T_BANK + t, g * P:(g + 1) * P], cmp_p[:, t, g * P:(g + 1) * P],
                                          ident[:, :])
                    mm.then_inc(A["cmp_turned"], 1)

            def cmp_times_v(t):
                if t == 0:
                    pe.wait_ge(A["maxed"], 2 * (NSA + HEADS))
                    pe.wait_ge(A["cmp_copied"], TT)
                else:
                    pe.wait_ge(A["cmp_o"], HEADS)
                for g in range(GROUPS):
                    pe.matmul(ps[:, 2 + g, :], cmp_pT[:, t, g * P:(g + 1) * P], v_cmp[:, g, :],
                              start=True, stop=True).then_inc(A["cmp_pv"], 1)

            last = NSA + HEADS
            for s in range(last + 3):
                if s < last:
                    turn_q(s)
                if s == last:
                    turn_cmp()
                if 0 <= s - 1 < last:
                    score(s - 1)
                if 0 <= s - 2 < last:
                    turn_p(s - 2)
                if s == last + 1:
                    cmp_times_v(0)
                if 0 <= s - 3 < last:
                    times_v(s - 3)

            def o_tile(k, t):
                return (o_mla if k < HEADS else o_nsa)[:, t, k % HEADS * VD:(k % HEADS + 1) * VD]

            def project_out(U):
                L = STAGES["wout"][1]
                for j in range(L):
                    def tile_ready(t):
                        if j == 0 and U.first > 0:
                            pe.wait_ge(res["wout"]["bank_read"], U.at(lambda u: 2 * (u - 1) + t + 1))
                        elif j == 0:
                            pe.wait_ge(A["o_done"], 2 * last)
                    if U.first == 0:
                        rounds_ahead("o", j, o_tile)
                        pe.wait_ge(nrm["o"]["T_lo_done"], j + 1)
                        if 2 <= j <= 5:
                            gate_broadcast(1, j - 2)
                    panel(U, j, (hT_hi, hT_lo), 2 * j, 0, j == 0, j == L - 1, CW, tile_ready)
                    if U.first == 0 and j == 0:
                        cmp_times_v(1)
                    if U.first == 0 and j == 6:
                        turn_ada(Unit("late", 1), 0)

            pe.wait_ge(A["pT_copied"], last)
            first_rounds("o", o_tile)
            project_out(Unit("wout", 0))
            for U in units(pe, "wout", 1, STAGES["wout"][0]):
                project_out(U)

            first_rounds("ffn2", x_tile, res["wout"]["x_added"])
            pe.wait_ge(res["wout"]["bank_read"], 2 * (D // CW))
            gate_up_unit(1, Unit("gu1", 0), True)
            for a, b in ((1, 5), (5, FF // CW)):
                for U in units(pe, "gu1", a, b):
                    gate_up_unit(1, U, False)
            down_unit(1, Unit("dn1", 0))
            for U in units(pe, "dn1", 1, D // CW):
                down_unit(1, U)

        @block.scalar
        def _(act):
            def hi(U, j):
                s = U.slot(j)
                act.wait_ge(raw_landed[s], U.landed(j))
                free = U.slot_free(j)
                if free is not None:
                    act.wait_ge(mm_done, free)
                act.activation(part(U, w_hi, s), part(U, raw, s), ACT.Copy).then_inc(hi_done, 1)

            def silu(f, U):
                act.wait_ge(mm_done, U.done(KD - 2))
                for t in range(TT):
                    act.activation(act_sg[:, t, :], ps[:, t, :], ACT.Silu).then_inc(gu[f]["silu_done"], 1)

            def actT(f, U):
                for b in range(2):
                    act.wait_ge(gu[f]["prod_turned"], U.at(lambda u: 2 * u + b + 1))
                    at = U.at(lambda u: (4 * u + 2 * b) * SEQ)
                    act.activation(act_hi[:, :, :].rearrange("p k n -> p (k n)")[:, bass.ds(at, CW)],
                                   ps[:, T_BANK + b, :], ACT.Copy).then_inc(gu[f]["actT_hi_done"], 1)

            def load_root_table():
                act.activation(stat[:, 5, 3:4], ones[:, 0:1], ACT.Sqrt)

            def root(n, w):
                act.wait_ge(nrm[n]["mean"], 1)
                act.activation(stat[:, 2, 0:w], stat[:, 1, 0:w], ACT.Sqrt).then_inc(nrm[n]["root"], 1)

            def x_squares(n, added, U):
                c0 = U.at(lambda u: u * CW)
                for t in range(TT):
                    if added is not None:
                        act.wait_ge(added, U.at(lambda u: 2 * u + t + 1))
                    act.activation(norm_tmp[:, t, :], x_sb[:, t, bass.ds(c0, CW)], ACT.Square,
                                   accum_out=x_sq[:, t, bass.ds(U.at(lambda u: u), 1)]).then_inc(nrm[n]["squares"], 1)
                act.wait_ge(nrm[n]["squares"], U.at(lambda u: 2 * u + 2))

            def round_hi(n, r, T, k):
                if n == "o":
                    act.wait_ge(nrm[n]["turned"], r + 1)
                    src = ps[:, T_BANK + r % NBANKS[n], :]
                else:
                    act.wait_ge(nrm[n]["tmp_done"], r + 1)
                    src = norm_tmp[:, r % 2, :]
                if n == "ffn1":
                    for kk in range(2):
                        at = src[:, kk * SEQ:(kk + 1) * SEQ]
                        ins = act.activation(at, at, ACT.Identity, bias=shift_col(n, k + kk))
                    ins.then_inc(shifted, 1)
                    act.wait_ge(shifted, r + 1)
                if n in ("mix", "ffn2"):
                    for kk in range(2):
                        ins = act.activation(T[:, k + kk, :], src[:, kk * SEQ:(kk + 1) * SEQ], ACT.Identity,
                                             bias=shift_col(n, k + kk))
                else:
                    ins = act.activation(T[:, k:k + 2, :].rearrange("p k n -> p (k n)"), src, ACT.Copy)
                ins.then_inc(nrm[n]["T_hi_done"], 1)

            def copy_rstd(n, bank):
                act.wait_ge(rstd_mm, RSTD_USE[n])
                act.activation(rstd_b[:, :], ps[:, bank, 0:SEQ], ACT.Copy).then_inc(rstd_b_done, 1)

            def gate_copy(f, c, dst, factor):
                act.wait_ge(gat[f]["gate_mm"], c + 1)
                act.activation(dst[:, c * CW:(c + 1) * CW], ps[:, MISC_BANK, :], ACT.Copy, scale=factor)\
                   .then_inc(gat[f]["gate_b_done"], 1)

            def copy_out(stage, U, dst, bank, width=CW):
                at = U.at(lambda u: u * CW)
                for t in range(TT):
                    wait_products(act, U, t)
                    act.activation(dst[:, t, bass.ds(at, width)], ps[:, bank + t, 0:width], ACT.Copy)\
                       .then_inc(copied[stage], 1)

            dma = act.dma_start
            dma(ident[:, :], ident_c).then_inc(const_landed, 16)
            for name, v in (("ffn1", norm_ffn1), ("mix", norm_mix), ("ffn2", norm_ffn2), ("q", mla_q_norm),
                            ("kv", mla_kv_norm), ("c", c)):
                n = v.shape[1] // P
                dma(v_rows[VROWS[name]:VROWS[name] + n, :], v[0].rearrange("(k p) -> k p", p=P))\
                    .then_inc(const_landed, 16)
            dma(bucket_sb[:, :], bucket_c).then_inc(const_landed, 16)
            dma(pe_sb[:, 0:DK], pe_cmp_k[0]).then_inc(const_landed, 16)
            dma(pe_sb[:, DK:DK + VD], pe_cmp_v[0]).then_inc(const_landed, 16)
            act.wait_ge(rel_set, 2)
            dma(rel_sb[0:BUCKETS, 0:HEADS], rel_bias).then_inc(rel_landed, 16)
            dma(x_sb[:, :, :], x_t).then_inc(x_landed, 16)
            act.wait_ge(v_done, 1)
            act.activation(silu_c[:, :], v_cols[:, VROWS["c"]:NV], ACT.Silu).then_inc(silu_c_done, 1)

            def fresh_unit(n, U, per, added, last_chunk):
                hi(U, 0)
                hi(U, 1)
                load_root_table()
                x_squares(n, added, last_chunk)
                root(n, TT)
                copy_rstd(n, MISC_BANK)
                round_hi(n, 0, hT_hi, 0)
                round_hi(n, 1, hT_hi, 2)
                for j in range(2, STAGES[U.stage][1]):
                    hi(U, j)
                    if j % per == 0 and j // per >= 2:
                        round_hi(n, j // per, hT_hi, j // per * 2)

            def gate_up_unit(f, U):
                for j in range(KD):
                    hi(U, j)
                    if j == 1:
                        silu(f, before(U))
                    if j == 3:
                        actT(f, before(U))

            def down_unit(f, U):
                for j in range(STAGES[U.stage][1]):
                    hi(U, j)
                    if U.first == 0:
                        if j == 1:
                            silu(f, Unit(f"gu{f}", FF // CW - 1))
                        if j == 3:
                            actT(f, Unit(f"gu{f}", FF // CW - 1))
                        if j in (10, 12, 14, 16):
                            gate_copy(2 * f, (j - 10) // 2, gate_b, 0.5)
                    elif j == 3:
                        x_squares(("mix", "final")[f], res[U.stage]["x_added"], before(U))

            act.wait_ge(ones_set, 1)
            load_root_table()
            act.wait_ge(x_landed, 16)
            for u in range(D // CW):
                x_squares("ffn1", None, Unit("dn0", u))
            root("ffn1", TT)
            copy_rstd("ffn1", T_BANK)
            for j in range(0, KD, 4):
                hi(Unit("gu0", 0), j)
                hi(Unit("gu0", 0), j + 1)
                round_hi("ffn1", j // 2, hT_hi, j)
                round_hi("ffn1", j // 2 + 1, hT_hi, j + 2)
                if j == KD - 4:
                    act.wait_ge(rev_done, 1)
                    dma(bias_scratch.ap(), rev_sb[:, :].unsqueeze(1).broadcast_to([HEADS + 1, P, 384]))\
                        .then_inc(rev_stored, 16)
                hi(Unit("gu0", 0), j + 2)
                hi(Unit("gu0", 0), j + 3)
            act.wait_ge(rev_stored, 16)
            for U in units(act, "gu0", 1, FF // CW):
                gate_up_unit(0, U)
            down_unit(0, Unit("dn0", 0))
            for U in units(act, "dn0", 1, D // CW):
                down_unit(0, U)

            def project_in(U):
                for j in range(STAGES["win"][1]):
                    hi(U, j)
                    if j == 1:
                        copy_out("win", before(U), proj, 0)

            fresh_unit("mix", Unit("win", 0), 1, res["dn0"]["x_added"], Unit("dn0", D // CW - 1))
            for U in units(act, "win", 1, STAGES["win"][0] - 1, 2):
                project_in(U)
            last_in = Unit("win", STAGES["win"][0] - 1)
            project_in(last_in)

            def copy_keys(r):
                act.wait_ge(A["k_turned"], r + 1)
                act.activation(kT128[:, 2 * r:2 * r + 2, :].rearrange("p k n -> p (k n)"), ps[:, KEY_BANK[r], :],
                               ACT.Copy).then_inc(A["kT_copied"], 1)

            copy_keys(0)
            copy_keys(1)
            for i, (c0, w) in enumerate(((C_Q, Q_RANK), (C_KV, KV_RANK))):
                for t in range(TT):
                    act.activation(q_mla[:, t, c0:c0 + w], proj[:, t, c0:c0 + w], ACT.Square,
                                   accum_out=stat[:, 0, 2 * i + t:2 * i + t + 1]).then_inc(nrm["mla"]["squares"], 1)
            for j in range(STAGES["uq"][1]):
                hi(Unit("uq", 0), j)
            copy_out("win", last_in, proj, 0, LAST_W)
            copy_keys(2)
            act.wait_ge(copied["win"], 2 * STAGES["win"][0])
            act.activation(gates[:, :, :], proj[:, :, C_NG:D_IN], ACT.Exp, scale=-1.0).then_inc(A["gates_exp"], 1)
            load_root_table()
            root("mla", 4)
            for r in range(5):
                round_hi("mla", r, cqT[0] if r < 3 else ckvT[0], 2 * r if r < 3 else 2 * r - 6)
            for i in range(2):
                act.wait_ge(A["cw_used"], (16, 24)[i])
                act.activation(hid[:, i, :], ps[0:GROUPS * N_CMP, 6 + i, 0:CMP_HID], ACT.Silu)\
                   .then_inc(A["hid_done"], 1)
            small_units = [("uq", u) for u in range(STAGES["uq"][0])] + [("ukv", u) for u in range(STAGES["ukv"][0])]

            def copy_small(i):
                stage, u = small_units[i]
                copy_out(stage, Unit(stage, u), q_mla if stage == "uq" else kv_mla, 2 * (i % 2))

            for i, (stage, u) in enumerate(small_units):
                if i > 0:
                    for j in range(STAGES[stage][1]):
                        hi(Unit(stage, u), j)
                    copy_small(i - 1)
            copy_small(len(small_units) - 1)
            act.wait_ge(A["kr_turned"], 1)
            act.activation(krT[:, :], ps[0:ROPE, T_BANK, 0:SEQ], ACT.Copy).then_inc(A["kr_copied"], 1)

            def copy_q(u):
                nsa = u < NSA
                if nsa and u % 2:
                    return
                e = u // 2 if nsa else u - HEADS
                act.wait_ge(A["q_turned"], e + 1)
                if e >= 2:
                    act.wait_ge(A["scored"], 2 * e - 2 if e < HEADS + 2 else e + HEADS - 1)
                if nsa:
                    act.activation(qkT[:, e % 2, 0:SEQ], ps[:, T_BANK, 0:SEQ], ACT.Copy)
                    act.activation(qrT[:, e % 2, :], ps[0:ROPE, T_BANK, SEQ:2 * SEQ], ACT.Copy)\
                       .then_inc(A["qk_copied"], 1)
                else:
                    act.activation(qkT[:, e % 2, :], ps[:, T_BANK, :], ACT.Copy).then_inc(A["qk_copied"], 1)

            def exps(u):
                act.wait_ge(A["neg_done"], u + 1)
                for t in range(TT):
                    sl = slice(t * P, t * P + (t + 1) * P)
                    act.activation(probs[:, u % 2, sl], probs[:, u % 2, sl], ACT.Exp, bias=neg_max[:, u, t:t + 1],
                                   scale=SCALE, accum_out=row_sum[:, u, t:t + 1]).then_inc(A["exped"], 1)

            def copy_p(u):
                act.wait_ge(A["p_turned"], u + 1)
                if u >= 2:
                    act.wait_ge(A["pv_done"], u - 1)
                act.activation(probsT[:, u % 2, :], ps[:, 6 + u % 2, 0:3 * P], ACT.Copy).then_inc(A["pT_copied"], 1)

            last = NSA + HEADS
            for s in range(last + 3):
                if s < last:
                    copy_q(s)
                if 0 <= s - 1 < last:
                    exps(s - 1)
                if s == NSA + 3:
                    for t in range(TT):
                        act.wait_ge(A["cmp_ready"], t + 1)
                        pc = cmp_p[:, t, 0:SEQ].rearrange("p (h n) -> p h n", n=32)[:, :, 0:CMP_IN_REACH[t]]
                        act.activation(pc, pc, ACT.Exp, scale=SCALE).then_inc(A["cmp_exped"], 1)
                if s == last:
                    for t in range(TT):
                        act.wait_ge(A["cmp_turned"], t + 1)
                        act.activation(cmp_pT[:, t, :], ps[:, T_BANK + t, 0:SEQ], ACT.Copy).then_inc(A["cmp_copied"], 1)
                if 0 <= s - 2 < last:
                    copy_p(s - 2)
                if 10 <= s < 10 + RING:
                    hi(Unit("wout", 0), s - 10)

            for r in range(4):
                round_hi("o", r, hT_hi, 2 * r)
            U = Unit("wout", 0)
            for j in range(RING, STAGES["wout"][1]):
                round_hi("o", j, hT_hi, 2 * j)
                hi(U, j)
                gate_copy(1, j - RING, kv_mla[:, 0, :], 1.0)
            for U in units(act, "wout", 1, STAGES["wout"][0]):
                for j in range(STAGES["wout"][1]):
                    hi(U, j)
                    if j == 3:
                        x_squares("ffn2", res["wout"]["x_added"], before(U))

            fresh_unit("ffn2", Unit("gu1", 0), 2, res["wout"]["x_added"], Unit("wout", D // CW - 1))
            for U in units(act, "gu1", 1, FF // CW):
                gate_up_unit(1, U)
            down_unit(1, Unit("dn1", 0))
            for U in units(act, "dn1", 1, D // CW):
                down_unit(1, U)
            load_root_table()
            x_squares("final", res["dn1"]["x_added"], Unit("dn1", D // CW - 1))
            root("final", TT)

        @block.vector
        def _(dve):
            steps = 0

            def then_wait(ins):
                nonlocal steps
                steps += 1
                ins.then_inc(dve_step, 1)
                dve.wait_ge(dve_step, steps)

            def lo(U, j):
                s = U.slot(j)
                dve.wait_ge(hi_done, U.done(j))
                dve.tensor_tensor(part(U, w_lo, s), part(U, raw, s), part(U, w_hi, s).bitcast(F32), ALU.subtract)\
                   .then_inc(lo_done, 1)

            def add_ada(U, e, p):
                q = U.at(lambda u: ADA_OF[U.stage, u][e][0])
                q0, a = ADA_OF[U.stage, U.first][e]
                slot = p % RING
                dve.wait_ge(ada_landed[slot], U.at(lambda u: 16 * ada_use(ADA_OF[U.stage, u][e][0], p)))
                for kk in range(2):
                    k = 2 * p + kk
                    step = p + kk if U.stage == "start" else k
                    if k == 0:
                        dve.wait_ge(b_landed[a], U.at(lambda u: 16 * (ADA_BEFORE[ADA_OF[U.stage, u][e][0]][0] + 1)))
                        if ADA_BEFORE[q0][1] is not None:
                            dve.wait_ge(acc_turned, U.at(lambda u: ADA_BEFORE[ADA_OF[U.stage, u][e][0]][1] + 1))
                    else:
                        dve.wait_ge(acc_step, ada_steps(U, e, step))
                    dve.scalar_tensor_tensor(acc[:, a, :], ada_raw[:, slot, kk * CW:(kk + 1) * CW], silu_c[:, k:k + 1],
                                             b_row[:, a, :] if k == 0 else acc[:, a, :], ALU.mult, ALU.add)\
                       .then_inc(acc_step, 1)

            def start_chunk(q, after):
                U = Unit("start", q)
                for p in (0, 2, 4, 6):
                    add_ada(U, 0, p)
                    if p in after:
                        after[p]()
                dve.wait_ge(ada_by_pe, q * 4 + 4)
                dve.wait_ge(acc_step, ada_steps(U, 0, START_STEPS - 1))
                dve.tensor_tensor(acc[0:1, q % 2, :], acc[0:1, q % 2, :], ps[0:1, ROW_BANK[q % 2], :], ALU.add)\
                   .then_inc(acc_step, 1)

            def sum_ada(U, e):
                q = U.at(lambda u: ADA_OF[U.stage, u][e][0])
                dve.wait_ge(acc_turned, q + 1)
                col = U.at(lambda u: ada_column(ADA_OF[U.stage, u][e][0]))
                dve.tensor_reduce(mod_cols[:, bass.ds(col * 4, 4)],
                                  ps[:, ADA_BANK, :].rearrange("p (b n) -> p b n", b=4), AX.X, ALU.add)\
                   .then_inc(mod_done, 1)

            def rstd(n, parts):
                w = parts[-1][1]
                for i, (a, b, size) in enumerate(parts):
                    ins = dve.tensor_scalar(stat[:, 1, a:b], stat[:, 0, a:b], 1.0 / size, EPS, ALU.mult, ALU.add)
                ins.then_inc(nrm[n]["mean"], 1)
                dve.wait_ge(nrm[n]["root"], 1)
                v, root, r, e, out_ = (stat[:, i, 0:w] for i in (1, 2, 3, 4, 5))
                then_wait(dve.reciprocal(r, root))
                then_wait(dve.tensor_tensor(e, r, r, ALU.mult))
                then_wait(dve.tensor_tensor(e, e, v, ALU.mult))
                then_wait(dve.tensor_scalar(e, e, -0.5, 1.5, ALU.mult, ALU.add))
                then_wait(dve.tensor_tensor(out_, r, e, ALU.mult))

            def x_rstd(n):
                dve.wait_ge(nrm[n]["squares"], 2 * (D // CW))
                then_wait(dve.tensor_reduce(stat[:, 0, 0:TT], x_sq[:, :, :], AX.X, ALU.add))
                rstd(n, [(0, TT, D)])

            def norm_x(n):
                x_rstd(n)
                for t in range(TT):
                    ins = dve.tensor_scalar(diag_r[:, t, :], ident[:, :], stat[:, 5, t:t + 1], None, ALU.mult)
                ins.then_inc(nrm[n]["xn_done"], 1)

            def make_scale(n, seg, mods):
                dve.wait_ge(mod_done, mods)
                g0 = VROWS[n]
                then_wait(dve.scalar_tensor_tensor(scale_cols[:, :], mod_cols[:, seg * KD:(seg + 1) * KD], 1.0,
                                                   v_cols[:, g0:g0 + KD], ALU.add, ALU.mult))

            def round_tmp(n, r):
                dve.wait_ge(nrm[n]["turned"], r + 1)
                if r >= 2:
                    dve.wait_ge(nrm[n]["T_lo_done"], r - 1)
                if r == 0 and n in RSTD_USE:
                    dve.wait_ge(rstd_b_done, RSTD_USE[n])
                for kk in range(2):
                    k = 2 * r + kk
                    dst, src = (a[:, kk * SEQ:(kk + 1) * SEQ]
                                for a in (norm_tmp[:, r % 2, :], ps[:, T_BANK + r % NBANKS[n], :]))
                    if n == "mla":
                        ins = dve.tensor_scalar(dst, src, v_cols[:, VROWS["q"] + k:VROWS["q"] + k + 1], None, ALU.mult)
                    else:
                        ins = dve.scalar_tensor_tensor(dst, src, scale_cols[:, k:k + 1], rstd_b[:, :], ALU.mult, ALU.mult)
                ins.then_inc(nrm[n]["tmp_done"], 1)

            def round_lo(n, r):
                dve.wait_ge(nrm[n]["T_hi_done"], r + 1)
                for kk in range(2):
                    k = 2 * r + kk
                    ins = dve.scalar_tensor_tensor(hT_lo[:, k, :], norm_tmp[:, r % 2, kk * SEQ:(kk + 1) * SEQ],
                                                   shift_col(n, k), hT_hi[:, k, :].bitcast(F32), ALU.add, ALU.subtract)
                ins.then_inc(nrm[n]["T_lo_done"], 1)

            def o_lo(r):
                dve.wait_ge(nrm["o"]["T_hi_done"], r + 1)
                dve.tensor_tensor(hT_lo[:, 2 * r:2 * r + 2, :].rearrange("p k n -> p (k n)"),
                                  ps[:, T_BANK + r % NBANKS["o"], :],
                                  hT_hi[:, 2 * r:2 * r + 2, :].rearrange("p k n -> p (k n)").bitcast(F32), ALU.subtract)\
                   .then_inc(nrm["o"]["T_lo_done"], 1)

            def product(f, U):
                dve.wait_ge(mm_done, U.done(KD - 1))
                for t in range(TT):
                    dve.wait_ge(gu[f]["silu_done"], U.at(lambda u: 2 * u + t + 1))
                    dve.tensor_tensor(act_sg[:, t, :], act_sg[:, t, :], ps[:, 2 + t, :], ALU.mult)\
                       .then_inc(gu[f]["prod_done"], 1)

            def actT_low(f, U):
                flat = [a[:, :, :].rearrange("p k n -> p (k n)") for a in (act_hi, act_lo)]
                for b in range(2):
                    dve.wait_ge(gu[f]["actT_hi_done"], U.at(lambda u: 2 * u + b + 1))
                    at = U.at(lambda u: (4 * u + 2 * b) * SEQ)
                    dve.tensor_tensor(flat[1][:, bass.ds(at, CW)], ps[:, T_BANK + b, :],
                                      flat[0][:, bass.ds(at, CW)].bitcast(F32), ALU.subtract)\
                       .then_inc(gu[f]["actT_lo_done"], 1)

            def residual(U, gate):
                s = res[U.stage]
                at = U.at(lambda u: u * CW)
                for t in range(TT):
                    wait_products(dve, U, t)
                    dve.tensor_tensor(act_sg[:, t, :], ps[:, t, :], gate[:, bass.ds(at, CW)], ALU.mult)\
                       .then_inc(s["bank_read"], 1)
                    dve.wait_ge(s["bank_read"], U.at(lambda u: 2 * u + t + 1))
                    xs = x_sb[:, t, bass.ds(at, CW)]
                    dve.tensor_tensor(xs, xs, act_sg[:, t, :], ALU.add).then_inc(s["x_added"], 1)
                dve.wait_ge(s["x_added"], U.at(lambda u: 2 * u + 2))

            def gate_diag(f, c, seg):
                if c >= 2:
                    dve.wait_ge(gat[f]["gate_mm"], c - 1)
                for b in range(4):
                    col = seg * KD + 4 * c + b
                    ins = dve.tensor_scalar(norm_tmp[:, c % 2, b * P:(b + 1) * P], ident[:, :],
                                            mod_cols[:, col:col + 1], None, ALU.mult)
                ins.then_inc(gat[f]["diag_done"], 1)

            dve.memset(rel_sb[:, :], 0.0).then_inc(rel_set, 1)
            dve.wait_ge(rel_set, 1)
            dve.memset(rel_sb[BUCKETS:BUCKETS + 1, :], 1.0).then_inc(rel_set, 1)
            dve.wait_ge(v_turned, 1)
            dve.tensor_copy(v_cols[:, :], ps[:, MISC_BANK, 0:NV]).then_inc(v_done, 1)
            dve.wait_ge(silu_c_done, 1)

            def sum_start(q):
                sum_ada(Unit("start", q), 0)

            def first_features(i):
                cols = slice(4 * i, 4 * i + 4)
                g0 = VROWS["ffn1"]
                dve.wait_ge(mod_done, 2 * i + 2)
                then_wait(dve.scalar_tensor_tensor(scale_cols[:, cols], mod_cols[:, KD + 4 * i:KD + 4 * i + 4], 1.0,
                                                   v_cols[:, g0 + 4 * i:g0 + 4 * i + 4], ALU.add, ALU.mult))
                round_tmp("ffn1", 2 * i)

            def first_lo(*panels):
                for j in panels:
                    lo(Unit("gu0", 0), j)

            start_chunk(0, {})
            dve.wait_ge(rev_mm, 1)
            dve.tensor_scalar(rev_sb[:, :], ps[0:HEADS + 1, T_BANK + 1, 0:384], 1.0 / SCALE, None, ALU.mult)\
               .then_inc(rev_done, 1)
            start_chunk(1, {2: lambda: sum_start(0)})
            norm_x("ffn1")
            for q in range(2, START_CHUNKS, 2):
                a = 2 * (q - 2)
                start_chunk(q, {2: lambda: (sum_start(q - 1), first_features(q // 2 - 1)),
                                4: lambda: first_lo(a), 6: lambda: round_tmp("ffn1", q - 1)})
                start_chunk(q + 1, {0: lambda: first_lo(a + 1), 2: lambda: sum_start(q),
                                    4: lambda: first_lo(a + 2), 6: lambda: first_lo(a + 3)})
            sum_start(START_CHUNKS - 1)
            first_features(START_CHUNKS // 2 - 1)
            first_lo(KD - 4, KD - 3)
            round_tmp("ffn1", KD // 2 - 1)
            first_lo(KD - 2, KD - 1)

            def fresh_unit(U, n, scale, mods, per, prev):
                make_scale(n, scale, mods)
                prev()
                norm_x(n)
                lo(U, 0)
                for r in range(2):
                    round_tmp(n, r)
                round_lo(n, 0)
                lo(U, 1)
                round_lo(n, 1)
                for j in range(2, STAGES[U.stage][1]):
                    if j % per == 0 and j // per >= 2:
                        round_tmp(n, j // per)
                    lo(U, j)
                    if j % per == 0 and j // per >= 2:
                        round_lo(n, j // per)
                    if U.stage == "gu0":
                        ada_between(U, j)

            def ada_between(U, j):
                if (U.stage, U.first) not in ADA_OF:
                    return
                p = j - ada_after[U.stage]
                if 0 <= p < 8 * len(ADA_OF[U.stage, U.first]):
                    add_ada(U, p // 8, p % 8)
                if U.stage in ("gu0", "gu1") and j == KD - 1:
                    sum_ada(U, 0)
                if U.stage == "dn0" and j in (17, 21):
                    sum_ada(U, int(j == 21))

            def gate_up_unit(f, U):
                for j in range(KD):
                    lo(U, j)
                    if j == 1:
                        product(f, before(U))
                    if j == 3:
                        actT_low(f, before(U))
                    ada_between(U, j)

            def down_unit(f, U):
                L = STAGES[U.stage][1]
                for j in range(L):
                    lo(U, j)
                    if j == 1:
                        if U.first == 0:
                            product(f, Unit(f"gu{f}", FF // CW - 1))
                        else:
                            residual(before(U), gate_b)
                    if j == 3:
                        if U.first == 0:
                            actT_low(f, Unit(f"gu{f}", FF // CW - 1))
                    if U.first == 0 and j in (6, 8, 10, 12):
                        gate_diag(2 * f, (j - 6) // 2, 2 + 6 * f)
                    ada_between(U, j)

            for U in units(dve, "gu0", 1, FF // CW):
                gate_up_unit(0, U)
            down_unit(0, Unit("dn0", 0))
            for U in units(dve, "dn0", 1, D // CW):
                down_unit(0, U)

            fresh_unit(Unit("win", 0), "mix", 4, 20, 1,
                       lambda: residual(Unit("dn0", D // CW - 1), gate_b))
            for U in units(dve, "win", 1, STAGES["win"][0] - 1, 2):
                for j in range(8):
                    lo(U, j)
                    ada_between(U, j)
                    if j == 3 and U.first % 2 == 0:
                        sum_ada(before(U), 0)
            U = Unit("win", STAGES["win"][0] - 1)
            for j in range(8):
                lo(U, j)

            def copy_rope_keys(r):
                dve.wait_ge(A["k_turned"], r + 1)
                dve.tensor_copy(kT64[:, 2 * r:2 * r + 2, :].rearrange("p k n -> p (k n)"), ps[0:ROPE, KEY_BANK[r] + 1, :])\
                   .then_inc(A["kT64_copied"], 1)

            def add_position(i, rows, dst, src):
                for g in range(GROUPS):
                    for a in range(2):
                        ls = slice(16 * a, 16 * a + 16)
                        blocks = src(g)[:, 16 * a:16 * a + 16 * N_CMP].rearrange("p (n b) -> p b n", b=16)
                        dve.tensor_tensor(dst[:, ls, g * N_CMP:(g + 1) * N_CMP], blocks,
                                          peT[0:rows, i, ls].unsqueeze(2).broadcast_to([rows, 16, N_CMP]), ALU.add)\
                           .then_inc(A["kpe_done"], 1)

            copy_rope_keys(0)
            copy_rope_keys(1)
            dve.wait_ge(A["pe_turned"], 1)
            for i, rows in enumerate((P, ROPE, P)):
                ins = dve.tensor_copy(peT[0:rows, i, :], ps[0:rows, MISC_BANK, 32 * i:32 * i + 32])
            then_wait(ins)
            dve.wait_ge(A["kT_copied"], 1)
            add_position(0, P, kpe128, lambda g: kT128[:, g, :])
            dve.wait_ge(A["kT64_copied"], 1)
            add_position(1, ROPE, kpe64, lambda g: kT64[:, g, :])
            copy_rope_keys(2)
            dve.wait_ge(A["v_turned_c"], 1)
            add_position(2, P, vpe, lambda g: ps[:, 2, g * SEQ:(g + 1) * SEQ])

            dve.wait_ge(nrm["mla"]["squares"], 4)
            rstd("mla", [(0, TT, Q_RANK), (TT, 2 * TT, KV_RANK)])
            for i, (c0, w) in enumerate(((C_Q, Q_RANK), (C_KV, KV_RANK))):
                for t in range(TT):
                    at = proj[:, t, c0:c0 + w]
                    dve.tensor_scalar(at, at, stat[:, 5, 2 * i + t:2 * i + t + 1], None, ALU.mult)\
                       .then_inc(nrm["mla"]["xn_done"], 1)
            for j in range(STAGES["uq"][1]):
                lo(Unit("uq", 0), j)
            then_wait(dve.memset(v_cmp[:, :, :], 0.0))
            dve.wait_ge(A["gates_exp"], 1)
            then_wait(dve.tensor_scalar(gates[:, :, :], gates[:, :, :], 1.0, None, ALU.add))
            then_wait(dve.reciprocal(gates[:, :, :], gates[:, :, :]))
            for r in range(5):
                round_tmp("mla", r)

            n = GROUPS * N_CMP

            def copy_hidden():
                dve.wait_ge(A["hid_turned"], 1)
                dve.tensor_copy(hidT[:, :, :], ps[:, 4, 0:P].rearrange("p (i n) -> p i n", n=32)[:, :, 0:n])\
                   .then_inc(A["hidT_copied"], 1)

            def copy_keys():
                dve.wait_ge(A["kc_mm"], 1)
                dve.tensor_copy(kc128[:, :], ps[:, 5, 0:n]).then_inc(A["kc_copied"], 1)
                dve.tensor_copy(kc64[:, :], ps[0:ROPE, 5, 32:32 + n]).then_inc(A["kc_copied"], 1)

            def copy_values():
                dve.wait_ge(A["kc_mm"], 2)
                for g in range(GROUPS):
                    for h in range(HPG):
                        rows, cols = slice(32 * h, 32 * h + N_CMP), slice(h * VD, (h + 1) * VD)
                        dve.tensor_copy(v_cmp[rows, g, cols], ps[rows, 6 + g, cols]).then_inc(A["vc_copied"], 1)

            after_unit = {("uq", 1): copy_hidden, ("uq", 2): copy_keys, ("ukv", 0): copy_values}
            small = [(stage, u, j) for stage in ("uq", "ukv") for u in range(STAGES[stage][0])
                     for j in range(STAGES[stage][1])]
            for i, (stage, u, j) in enumerate(small[STAGES["uq"][1]:]):
                lo(Unit(stage, u), j)
                if j == STAGES[stage][1] - 1 and (stage, u) in after_unit:
                    after_unit[stage, u]()
                if 0 <= i - 2 < 8:
                    add_ada(Unit("late", 0), 0, i - 2)
            sum_ada(Unit("late", 0), 0)

            def copy_qr(u):
                if u >= NSA:
                    e = u - HEADS
                    dve.wait_ge(A["q_turned"], e + 1)
                    dve.wait_ge(A["scored"], 2 * e - 2 if e < HEADS + 2 else e + HEADS - 1)
                    dve.tensor_copy(qrT[:, e % 2, :], ps[0:ROPE, T_BANK + 1, 0:SEQ]).then_inc(A["qr_copied"], 1)

            def maxima(u):
                dve.wait_ge(A["scored"], u + 1)
                if u == 0:
                    dve.wait_ge(A["bias_landed"], 16)
                if u >= 2:
                    dve.wait_ge(A["p_turned"], u - 1)
                h = u // 2 if u < NSA else HEADS
                for t in range(TT):
                    sl = slice(t * P, t * P + (t + 1) * P)
                    dve.tensor_tensor_reduce(probs[:, u % 2, sl], ps[:, 2 + u % 2, sl], bias[:, h, (1 - t) * P:SEQ],
                                             1.0, -3e38, ALU.add, ALU.max, row_max[:, u, t:t + 1])\
                       .then_inc(A["maxed"], 1)
                dve.wait_ge(A["maxed"], 2 * u + 2)
                dve.tensor_scalar(neg_max[:, u, :], row_max[:, u, :], -SCALE, None, ALU.mult).then_inc(A["neg_done"], 1)

            def outputs(u):
                nsa = u < NSA
                h = u // 2 if nsa else u - NSA
                dve.wait_ge(A["exped"], 2 * u + 2)
                then_wait(dve.reciprocal(coef[:, u, :], row_sum[:, u, :]))
                if nsa:
                    then_wait(dve.tensor_tensor(coef[:, u, :], coef[:, u, :], gates[:, :, 3 * h + 1 + u % 2], ALU.mult))
                dve.wait_ge(A["pv_done"], u + 1)
                o = o_nsa if nsa else o_mla
                for t in range(TT):
                    dst, src = o[:, t, h * VD:(h + 1) * VD], ps[:, u % 2, t * P:(t + 1) * P]
                    if nsa and u % 2:
                        dve.wait_ge(A["o_done"], 2 * u)
                        ins = dve.scalar_tensor_tensor(dst, src, coef[:, u, t:t + 1], dst, ALU.mult, ALU.add)
                    else:
                        ins = dve.tensor_scalar(dst, src, coef[:, u, t:t + 1], None, ALU.mult)
                    ins.then_inc(A["o_done"], 1)

            def cmp_view(t, a):
                return a.rearrange("p (h n) -> p h n", n=32)[:, :, 0:CMP_IN_REACH[t]]

            def cmp_logits():
                then_wait(dve.memset(cmp_p[:, :, 0:SEQ], 0.0))
                dve.wait_ge(A["cmp_scored"], HEADS)
                for t in range(TT):
                    first = (1 - t) * P + CMP_LEN - 1
                    reach = CMP_STRIDE * (CMP_IN_REACH[t] - 1) + 1
                    dve.tensor_tensor(cmp_view(t, cmp_p[:, t, 0:SEQ]), cmp_view(t, ps[:, 5, t * SEQ:(t + 1) * SEQ]),
                                      bias[:, 0:HEADS, first:first + reach:CMP_STRIDE], ALU.add)\
                       .then_inc(A["cmp_read"], 1)

            def cmp_shift(t):
                pc, m = cmp_view(t, cmp_p[:, t, 0:SEQ]), cmp_stat[:, t, 0:HEADS]
                dve.wait_ge(A["cmp_read"], t + 1)
                then_wait(dve.tensor_reduce(m, pc, AX.X, ALU.max))
                then_wait(dve.tensor_scalar(m, m, 0.1 * MASKED, None, ALU.max))
                dve.tensor_tensor(pc, pc, m.unsqueeze(2).broadcast_to([P, HEADS, CMP_IN_REACH[t]]), ALU.subtract)\
                   .then_inc(A["cmp_ready"], 1)

            def cmp_coef(t):
                s = cmp_stat[:, 2 + t, 0:HEADS]
                dve.wait_ge(A["cmp_exped"], t + 1)
                then_wait(dve.tensor_reduce(s, cmp_view(t, cmp_p[:, t, 0:SEQ]), AX.X, ALU.add))
                then_wait(dve.tensor_scalar(s, s, 1e-30, None, ALU.max))
                then_wait(dve.reciprocal(s, s))
                then_wait(dve.tensor_tensor(s, s, gates[:, t, :].rearrange("p (h b) -> p h b", b=3)[:, :, 0], ALU.mult))

            def cmp_outputs(t):
                for h in range(HEADS):
                    if h % HPG == 0:
                        dve.wait_ge(A["cmp_pv"], 2 * t + h // HPG + 1)
                    dst = o_nsa[:, t, h * VD:(h + 1) * VD]
                    dve.scalar_tensor_tensor(dst, ps[:, 2 + h // HPG, h % HPG * VD:(h % HPG + 1) * VD],
                                             cmp_stat[:, 2 + t, h:h + 1], dst, ALU.mult, ALU.add)\
                       .then_inc(A["cmp_o"], 1)

            last = NSA + HEADS
            for s in range(last + 3):
                if s == NSA:
                    cmp_logits()
                if s in (NSA + 1, NSA + 2):
                    cmp_shift(s - NSA - 1)
                if s in (NSA + 4, NSA + 5):
                    cmp_coef(s - NSA - 4)
                if s < last:
                    copy_qr(s)
                if 0 <= s - 1 < last:
                    maxima(s - 1)
                if 0 <= s - 3 < last:
                    outputs(s - 3)
                if s == 2:
                    dve.wait_ge(pool_step, 18 * TT)
                if 2 <= s < 10:
                    add_ada(Unit("late", 1), 0, s - 2)
                if 10 <= s < 10 + RING:
                    lo(Unit("wout", 0), s - 10)
            o_lo(0)
            cmp_outputs(0)
            o_lo(1)
            cmp_outputs(1)

            for r in range(2, 4):
                o_lo(r)
            gate_diag(1, 0, 5)
            U = Unit("wout", 0)
            for j in range(RING, 8):
                o_lo(j)
                lo(U, j)
                if j < 7:
                    gate_diag(1, j - 3, 5)
            gate2 = kv_mla[:, 0, :]
            sum_ada(Unit("late", 1), 0)
            for U in units(dve, "wout", 1, D // CW):
                for j in range(8):
                    lo(U, j)
                    if j == 1:
                        residual(before(U), gate2)

            fresh_unit(Unit("gu1", 0), "ffn2", 7, LATE + 2, 2,
                       lambda: residual(Unit("wout", D // CW - 1), gate2))
            for a, b in ((1, 5), (5, FF // CW)):
                for U in units(dve, "gu1", a, b):
                    gate_up_unit(1, U)
            down_unit(1, Unit("dn1", 0))
            for U in units(dve, "dn1", 1, D // CW):
                down_unit(1, U)
            residual(Unit("dn1", D // CW - 1), gate_b)

            x_rstd("final")
            dve.wait_ge(final_b_landed, 16)
            for t, c in FINAL_PIECES:
                sl = slice(c * CW, (c + 1) * CW)
                dve.scalar_tensor_tensor(x_sb[:, t, sl], x_sb[:, t, sl], stat[:, 5, t:t + 1], final_b[:, sl],
                                         ALU.mult, ALU.mult).then_inc(final_done, 1)


_INS = ["x", "c", "w_ada", "b_ada", "norm_ffn1", "w1_gate", "w1_up", "w1_down", "norm_mix", "w_in",
        "mla_q_norm", "w_uq", "mla_kv_norm", "w_ukv", "pe_cmp_k", "w_cmp_k1", "w_cmp_k2", "pe_cmp_v",
        "w_cmp_v1", "w_cmp_v2", "rel_bias", "w_out", "norm_ffn2", "w2_gate", "w2_up", "w2_down",
        "norm_final"]
_OUTS = [((1, SEQ, D), "float32")]


def kernel(**inputs):
    import numpy as _np
    import concourse.bacc as _bacc
    from concourse import mybir as _mybir
    from concourse.bass_utils import run_bass_kernel_spmd as _run

    nc = _bacc.Bacc("TRN2", target_bir_lowering=False, num_devices=1, dynamic_dma_scratch_size=1024)
    arrays, args = {}, []
    for name in _INS:
        a = _np.ascontiguousarray(inputs[name])
        arrays[f"in_{name}_dram"] = a
        args.append(nc.dram_tensor(f"in_{name}_dram", a.shape, _mybir.dt.from_np(a.dtype), kind="ExternalInput").ap())
    for i, (shape, dtype) in enumerate(_OUTS):
        dt = _mybir.dt.from_np(_np.dtype(dtype))
        args.append(nc.dram_tensor(f"out_{i}_dram", shape, dt, kind="ExternalOutput").ap())
    decoder_layer(nc, *args)
    r = _run(nc, [arrays], core_ids=[0])
    got = tuple(r.results[0][f"out_{i}_dram"] for i in range(len(_OUTS)))
    return got[0]
```
